# Optimizing a Trainium2 kernel written in Bass

```python
import jax, jax.numpy as jnp
from jax import lax
import numpy as np

D_MODEL = 1024
BATCH = 1
SEQ = 512
DEPTH = 2

NORM_EPS = 1e-6
NEG_INF = -1e30
A_HEADS = 8
A_HEAD_DIM = 64
A_WIDTH = A_HEADS * A_HEAD_DIM
A_BRANCHES = ((128, 1), (512, 4), (2048, 16))
ATTN_BLOCK = 128
ROPE_THETA = 500000.0
ROPE_DIM = A_HEAD_DIM // 4
B_WIDTH = D_MODEL - A_WIDTH
CONV_WIDTH = 31
C_HEADS = 4
C_QK_DIM = 256
C_V_DIM = 512
C_QK_WIDTH = C_HEADS * C_QK_DIM
C_V_WIDTH = C_HEADS * C_V_DIM
RET_CHUNK = 128
RET_ROT_THETA = 10000.0
MOE_GROUPS = 4
MOE_EXPERTS_PER_GROUP = 8
MOE_EXPERTS = MOE_GROUPS * MOE_EXPERTS_PER_GROUP
MOE_TOP_K = 2
EXPERT_HIDDEN = 512
MOE_BLOCK = 128

EVEN_IN_WIDTH = 3 * A_WIDTH + 2 * B_WIDTH
ODD_IN_WIDTH = 2 * C_QK_WIDTH + 2 * C_V_WIDTH
N_EVEN = (DEPTH + 1) // 2
N_ODD = DEPTH // 2

kernel_name = 'hybrid_dilated_conv_retention_hmoe'

F32 = jnp.float32

def rms_norm(x, gain):
    xf = x.astype(F32)
    y = xf * lax.rsqrt(jnp.mean(xf * xf, axis=-1, keepdims=True) + NORM_EPS)
    return (y * gain.astype(F32)).astype(x.dtype)

def rotary_tables(seq, inv_freq):
    ang = jnp.arange(seq, dtype=F32)[:, None] * inv_freq[None, :]
    return jnp.cos(ang), jnp.sin(ang)

def rotate(x, cos, sin):
    x1, x2 = jnp.split(x, 2, axis=-1)
    return jnp.concatenate([x1 * cos - x2 * sin, x2 * cos + x1 * sin], axis=-1)

def partial_rope(x, cos, sin):
    xr = rotate(x[..., :ROPE_DIM].astype(F32), cos, sin).astype(x.dtype)
    return jnp.concatenate([xr, x[..., ROPE_DIM:]], axis=-1)

def banded_causal_attention(q, k, v, n_steps):
    bsz, grp, length, dh = q.shape
    nb = -(-length // ATTN_BLOCK)
    padw = ((0, 0), (0, 0), (0, nb * ATTN_BLOCK - length), (0, 0))
    qb, kb, vb = (jnp.pad(t, padw).reshape(bsz, grp, nb, ATTN_BLOCK, dh) for t in (q, k, v))

    def with_prev(t):
        prev = jnp.pad(t, ((0, 0), (0, 0), (1, 0), (0, 0), (0, 0)))[:, :, :-1]
        return jnp.concatenate([prev, t], axis=3)

    kk, vv = with_prev(kb), with_prev(vb)
    s = jnp.einsum('bgnqd,bgnkd->bgnqk', qb, kk, preferred_element_type=F32) * (dh ** -0.5)
    qi = jnp.arange(ATTN_BLOCK)[:, None]
    kj = jnp.arange(2 * ATTN_BLOCK)[None, :]
    dist = ATTN_BLOCK + qi - kj
    band = (dist >= 0) & (dist <= n_steps)
    blk = jnp.arange(nb)[:, None, None]
    valid = band[None] & ((blk > 0) | (kj >= ATTN_BLOCK)[None])
    s = jnp.where(valid, s, NEG_INF)
    m = jnp.max(s, axis=-1, keepdims=True)
    e = jnp.exp(s - m)
    den = jnp.sum(e, axis=-1, keepdims=True)
    out = jnp.einsum('bgnqk,bgnkd->bgnqd', (e / den).astype(v.dtype), vv, preferred_element_type=F32)
    lse = (m + jnp.log(den))[..., 0]
    out = out.reshape(bsz, grp, nb * ATTN_BLOCK, dh)[:, :, :length]
    lse = lse.reshape(bsz, grp, nb * ATTN_BLOCK)[:, :, :length]
    return out, lse

def to_residue_classes(t, dil):
    bsz, h, seq, d = t.shape
    return t.reshape(bsz, h, seq // dil, dil, d).transpose(0, 1, 3, 2, 4).reshape(bsz, h * dil, seq // dil, d)

def from_residue_classes(t, h, dil):
    bsz, _, length, d = t.shape
    return t.reshape(bsz, h, dil, length, d).transpose(0, 1, 3, 2, 4).reshape(bsz, h, dil * length, d)

def dilated_window_attention(q, k, v):
    h = q.shape[1]
    outs, lses = [], []
    for window, dil in A_BRANCHES:
        o, l = banded_causal_attention(to_residue_classes(q, dil), to_residue_classes(k, dil),
                                       to_residue_classes(v, dil), window // dil)
        outs.append(from_residue_classes(o, h, dil))
        lses.append(from_residue_classes(l[..., None], h, dil)[..., 0])
    w = jax.nn.softmax(jnp.stack(lses), axis=0)
    return jnp.einsum('rbhs,rbhsd->bhsd', w, jnp.stack(outs))

def conformer_conv(val, gate, conv_w, conv_b, ln_g, ln_b):
    a = val * jax.nn.sigmoid(gate)
    c = a.shape[-1]
    y = lax.conv_general_dilated(a, conv_w[:, None, :].astype(a.dtype), window_strides=(1,),
                                 padding=[(CONV_WIDTH - 1, 0)],
                                 dimension_numbers=('NWC', 'WIO', 'NWC'),
                                 feature_group_count=c) + conv_b.astype(a.dtype)
    yf = y.astype(F32)
    mu = jnp.mean(yf, axis=-1, keepdims=True)
    var = jnp.mean(jnp.square(yf - mu), axis=-1, keepdims=True)
    yn = (yf - mu) * lax.rsqrt(var + NORM_EPS) * ln_g.astype(F32) + ln_b.astype(F32)
    return jax.nn.silu(yn).astype(val.dtype)

def even_mixer(u, w_in, w_out, conv_w, conv_b, conv_g, conv_beta, cos, sin):
    bsz, seq, _ = u.shape
    proj = u @ w_in
    q, k, v, bval, bgate = jnp.split(
        proj, [A_WIDTH, 2 * A_WIDTH, 3 * A_WIDTH, 3 * A_WIDTH + B_WIDTH], axis=-1)

    def heads(t):
        return t.reshape(bsz, seq, A_HEADS, A_HEAD_DIM).transpose(0, 2, 1, 3)

    qh = partial_rope(heads(q), cos, sin)
    kh = partial_rope(heads(k), cos, sin)
    a_out = dilated_window_attention(qh, kh, heads(v))
    a_out = a_out.transpose(0, 2, 1, 3).reshape(bsz, seq, A_WIDTH).astype(u.dtype)
    b_out = conformer_conv(bval, bgate, conv_w, conv_b, conv_g, conv_beta)
    return jnp.concatenate([a_out, b_out], axis=-1) @ w_out

def retention(q, k, v, log_decay):
    bsz, h, seq, dk = q.shape
    dv = v.shape[-1]
    nc = seq // RET_CHUNK
    qc = q.reshape(bsz, h, nc, RET_CHUNK, dk)
    kc = k.reshape(bsz, h, nc, RET_CHUNK, dk)
    vc = v.reshape(bsz, h, nc, RET_CHUNK, dv)
    pos = jnp.arange(RET_CHUNK, dtype=F32)
    diff = pos[:, None] - pos[None, :]
    intra = jnp.where(diff >= 0, jnp.exp(log_decay[:, None, None] * jnp.maximum(diff, 0.0)), 0.0)
    scores = jnp.einsum('bhnid,bhnjd->bhnij', qc, kc) * intra[:, None]
    inner = jnp.einsum('bhnij,bhnje->bhnie', scores, vc)
    q_decay = jnp.exp(log_decay[:, None] * (pos + 1.0))[None, :, :, None]
    k_decay = jnp.exp(log_decay[:, None] * (RET_CHUNK - 1.0 - pos))[None, :, :, None]
    chunk_decay = jnp.exp(log_decay * RET_CHUNK)[None, :, None, None]

    def step(state, xs):
        qn, kn, vn = xs
        cross = jnp.einsum('bhid,bhde->bhie', qn, state) * q_decay
        state = state * chunk_decay + jnp.einsum('bhjd,bhje->bhde', kn * k_decay, vn)
        return state, cross

    init = jnp.zeros((bsz, h, dk, dv), F32)
    xs = (qc.transpose(2, 0, 1, 3, 4), kc.transpose(2, 0, 1, 3, 4), vc.transpose(2, 0, 1, 3, 4))
    _, cross = lax.scan(step, init, xs)
    out = inner + cross.transpose(1, 2, 0, 3, 4)
    return out.reshape(bsz, h, seq, dv)

def odd_mixer(u, w_in, w_out, cos, sin):
    bsz, seq, _ = u.shape
    proj = u @ w_in
    q, k, v, g = jnp.split(proj, [C_QK_WIDTH, 2 * C_QK_WIDTH, 2 * C_QK_WIDTH + C_V_WIDTH], axis=-1)

    def heads(t, d):
        return t.reshape(bsz, seq, C_HEADS, d).transpose(0, 2, 1, 3).astype(F32)

    qh = rotate(heads(q, C_QK_DIM), cos, sin)
    kh = rotate(heads(k, C_QK_DIM), cos, sin) * (C_QK_DIM ** -0.5)
    log_decay = jnp.log(1.0 - jnp.exp2(-5.0 - jnp.arange(C_HEADS, dtype=F32)))
    o = retention(qh, kh, heads(v, C_V_DIM), log_decay)
    mu = jnp.mean(o, axis=-1, keepdims=True)
    var = jnp.mean(jnp.square(o - mu), axis=-1, keepdims=True)
    o = (o - mu) * lax.rsqrt(var + NORM_EPS)
    o = o.transpose(0, 2, 1, 3).reshape(bsz, seq, C_V_WIDTH)
    y = jax.nn.silu(g.astype(F32)) * o
    return y.astype(u.dtype) @ w_out

def grouped_experts(x2, experts, gates, w_gate, w_up, w_down):
    n_tok, d = x2.shape
    n_assign = n_tok * MOE_TOP_K
    flat_e = experts.reshape(-1)
    flat_tok = jnp.repeat(jnp.arange(n_tok, dtype=jnp.int32), MOE_TOP_K)
    flat_g = gates.reshape(-1)
    order = jnp.argsort(flat_e)
    sorted_e = flat_e[order]
    counts = jnp.bincount(flat_e, length=MOE_EXPERTS)
    starts = jnp.cumsum(counts) - counts
    padded = (counts + MOE_BLOCK - 1) // MOE_BLOCK * MOE_BLOCK
    pad_end = jnp.cumsum(padded)
    pad_start = pad_end - padded
    dest = pad_start[sorted_e] + jnp.arange(n_assign, dtype=jnp.int32) - starts[sorted_e]
    n_rows = n_assign + MOE_EXPERTS * MOE_BLOCK
    n_blocks = n_rows // MOE_BLOCK
    row_tok = jnp.zeros((n_rows,), jnp.int32).at[dest].set(flat_tok[order])
    row_gate = jnp.zeros((n_rows,), F32).at[dest].set(flat_g[order])
    block_expert = jnp.minimum(
        jnp.searchsorted(pad_end, jnp.arange(n_blocks, dtype=jnp.int32) * MOE_BLOCK, side='right'),
        MOE_EXPERTS - 1)
    xb = x2[row_tok].reshape(n_blocks, MOE_BLOCK, d)

    def expert_block(args):
        xblk, e = args
        hid = jax.nn.silu(xblk @ w_gate[e]) * (xblk @ w_up[e])
        return hid @ w_down[e]

    yb = lax.map(expert_block, (xb, block_expert))
    yr = yb.reshape(n_rows, d).astype(F32) * row_gate[:, None]
    return jax.ops.segment_sum(yr, row_tok, num_segments=n_tok).astype(x2.dtype)

def hierarchical_moe(h, w_r1, b_r1, w_r2, b_r2, w_gate, w_up, w_down):
    bsz, seq, d = h.shape
    x2 = h.reshape(-1, d)
    n_tok = x2.shape[0]
    group_prob = jax.nn.softmax((x2 @ w_r1).astype(F32) + b_r1.astype(F32), axis=-1)
    gp, gi = lax.top_k(group_prob, 1)
    fine = ((x2 @ w_r2).astype(F32) + b_r2.astype(F32)).reshape(n_tok, MOE_GROUPS, MOE_EXPERTS_PER_GROUP)
    sel = jnp.einsum('tg,tge->te', jax.nn.one_hot(gi[:, 0], MOE_GROUPS, dtype=F32), fine)
    ev, ei = lax.top_k(sel, MOE_TOP_K)
    gates = gp * jax.nn.softmax(ev, axis=-1)
    experts = gi * MOE_EXPERTS_PER_GROUP + ei
    y = grouped_experts(x2, experts, gates, w_gate, w_up, w_down)
    return y.reshape(bsz, seq, d)

def setup_inputs(seed: int = 0) -> dict:
    key = jax.random.key(seed)
    ks = jax.random.split(key, 20)

    def nrm(k, shape, scale):
        return jax.random.normal(k, shape, F32) * scale

    return {
        'x': nrm(ks[0], (BATCH, SEQ, D_MODEL), 1.0),
        'mix_norm': 1.0 + nrm(ks[1], (DEPTH, D_MODEL), 0.02),
        'ffn_norm': 1.0 + nrm(ks[2], (DEPTH, D_MODEL), 0.02),
        'final_norm': 1.0 + nrm(ks[3], (D_MODEL,), 0.02),
        'even_w_in': nrm(ks[4], (N_EVEN, D_MODEL, EVEN_IN_WIDTH), D_MODEL ** -0.5),
        'even_w_out': nrm(ks[5], (N_EVEN, A_WIDTH + B_WIDTH, D_MODEL), (A_WIDTH + B_WIDTH) ** -0.5),
        'conv_w': nrm(ks[6], (N_EVEN, CONV_WIDTH, B_WIDTH), CONV_WIDTH ** -0.5),
        'conv_b': nrm(ks[7], (N_EVEN, B_WIDTH), 0.02),
        'conv_norm_g': 1.0 + nrm(ks[8], (N_EVEN, B_WIDTH), 0.02),
        'conv_norm_b': nrm(ks[9], (N_EVEN, B_WIDTH), 0.02),
        'odd_w_in': nrm(ks[10], (N_ODD, D_MODEL, ODD_IN_WIDTH), D_MODEL ** -0.5),
        'odd_w_out': nrm(ks[11], (N_ODD, C_V_WIDTH, D_MODEL), C_V_WIDTH ** -0.5),
        'router_w1': nrm(ks[12], (DEPTH, D_MODEL, MOE_GROUPS), D_MODEL ** -0.5),
        'router_b1': nrm(ks[13], (DEPTH, MOE_GROUPS), 0.01),
        'router_w2': nrm(ks[14], (DEPTH, D_MODEL, MOE_EXPERTS), D_MODEL ** -0.5),
        'router_b2': nrm(ks[15], (DEPTH, MOE_EXPERTS), 0.01),
        'expert_w_gate': nrm(ks[16], (DEPTH, MOE_EXPERTS, D_MODEL, EXPERT_HIDDEN), D_MODEL ** -0.5),
        'expert_w_up': nrm(ks[17], (DEPTH, MOE_EXPERTS, D_MODEL, EXPERT_HIDDEN), D_MODEL ** -0.5),
        'expert_w_down': nrm(ks[18], (DEPTH, MOE_EXPERTS, EXPERT_HIDDEN, D_MODEL), EXPERT_HIDDEN ** -0.5),
    }

def reference(x, mix_norm, ffn_norm, final_norm, even_w_in, even_w_out, conv_w, conv_b,
              conv_norm_g, conv_norm_b, odd_w_in, odd_w_out, router_w1, router_b1, router_w2,
              router_b2, expert_w_gate, expert_w_up, expert_w_down):
    seq = x.shape[1]
    cos_a, sin_a = rotary_tables(seq, ROPE_THETA ** (-jnp.arange(0, ROPE_DIM, 2, dtype=F32) / ROPE_DIM))
    cos_r, sin_r = rotary_tables(seq, RET_ROT_THETA ** (-jnp.linspace(0.0, 1.0, C_QK_DIM // 2, dtype=F32)))
    h = x
    for layer in range(DEPTH):
        u = rms_norm(h, mix_norm[layer])
        i = layer // 2
        if layer % 2 == 0:
            h = h + even_mixer(u, even_w_in[i], even_w_out[i], conv_w[i], conv_b[i],
                               conv_norm_g[i], conv_norm_b[i], cos_a, sin_a)
        else:
            h = h + odd_mixer(u, odd_w_in[i], odd_w_out[i], cos_r, sin_r)
        h = h + hierarchical_moe(rms_norm(h, ffn_norm[layer]), router_w1[layer], router_b1[layer],
                                 router_w2[layer], router_b2[layer], expert_w_gate[layer],
                                 expert_w_up[layer], expert_w_down[layer])
    return rms_norm(h, final_norm)


_drawn_inputs = setup_inputs


def setup_inputs(seed=0):
    import zlib

    import numpy as np

    out = dict(_drawn_inputs(seed))
    spreads = {}
    factors = {'final_norm': 9.008, 'router_b1': 4.78, 'router_b2': 2.847}
    for name, (base, spread) in spreads.items():
        noise = np.random.default_rng([zlib.crc32(name.encode()), seed]).standard_normal(out[name].shape)
        drawn = base * np.exp(spread * noise) if base else spread * noise
        out[name] = __import__('jax').numpy.asarray(drawn.astype(out[name].dtype))
    for name, factor in factors.items():
        out[name] = (out[name] * factor).astype(out[name].dtype)
    return out
```

```python
from contextlib import ExitStack

import numpy as np

import concourse.bass as bass
from concourse import mybir

F32 = mybir.dt.float32
U32 = mybir.dt.uint32
ALU = mybir.AluOpType
ACT = mybir.ActivationFunctionType
AX = mybir.AxisListType

P = 128
SEQ, DM, DEPTH = 512, 1024, 2
TILES = SEQ // P
KC = DM // P
EPS = 1e-6
NEG = -1e30
A_HEADS, A_DIM = 8, 64
A_WIDTH = A_HEADS * A_DIM
BRANCHES = ((128, 1), (512, 4), (2048, 16))
ROPE_THETA, ROPE_DIM = 500000.0, 16
B_WIDTH = DM - A_WIDTH
BC = B_WIDTH // P
TAPS = 31
PAD = TAPS - 1
R_HEADS, R_QK, R_V = 4, 256, 512
R_QKW, R_VW = R_HEADS * R_QK, R_HEADS * R_V
RET_THETA = 10000.0
GROUPS, PER_GROUP = 4, 8
EXPERTS = GROUPS * PER_GROUP
HID = 512
HC = HID // P
TOPK = 2
NROUT = GROUPS + EXPERTS
N_CONST = 9
ST_AT = [0, 4 * P, 7 * P, 9 * P]
SLOTS = 6
BLOCK = 4096
SLOT_TILES = SEQ // P
EMPTY = 4096.0


def shape_constants():
    p = np.arange(P)
    ident = np.eye(P, dtype=np.float32)
    ones = np.ones((P, P), np.float32)
    before = (p[:, None] < p[None, :]).astype(np.float32)
    mean = np.full((P, P), 1.0 / B_WIDTH, np.float32)
    half = ROPE_DIM // 2
    swap = np.zeros((P, P), np.float32)
    for h in range(P // A_DIM):
        for i in range(half):
            swap[h * A_DIM + half + i, h * A_DIM + i] = -1.0
            swap[h * A_DIM + i, h * A_DIM + half + i] = 1.0
    square = np.stack([ident, ones, before, mean, swap], 1)

    inv = (np.float32(ROPE_THETA) ** (-np.arange(0, ROPE_DIM, 2, dtype=np.float32) / ROPE_DIM)).astype(np.float32)
    ang = (np.arange(SEQ, dtype=np.float32)[:, None] * inv[None]).astype(np.float32)
    cos_a, sin_a = np.ones((P, SEQ), np.float32), np.zeros((P, SEQ), np.float32)
    for h in range(P // A_DIM):
        for i in range(ROPE_DIM):
            cos_a[h * A_DIM + i] = np.cos(ang[:, i % half])
            sin_a[h * A_DIM + i] = np.sin(ang[:, i % half])
    bias = np.empty((P, SEQ), np.float32)
    for b in range(TILES):
        dist = P * (TILES - 1 - b) + p[:, None] - p[None, :]
        count = sum(((dist >= 0) & (dist % dil == 0) & (dist <= win)).astype(np.int64) for win, dil in BRANCHES)
        bias[:, b * P:(b + 1) * P] = np.where(count > 0, np.log(np.maximum(count, 1)), NEG)
    tab_a = np.stack([cos_a, sin_a, bias], 1)

    inv = (np.float32(RET_THETA) ** (-np.linspace(0.0, 1.0, R_QK // 2, dtype=np.float32))).astype(np.float32)
    ang = (inv[:, None] * np.arange(SEQ, dtype=np.float32)[None]).astype(np.float32)
    decay = np.empty((P, R_HEADS, SEQ), np.float32)
    for h in range(R_HEADS):
        log_decay = np.log(1.0 - 2.0 ** (-5.0 - h))
        for d in range(TILES):
            diff = P * d + p[None, :] - p[:, None]
            decay[:, h, d * P:(d + 1) * P] = np.where(diff >= 0, np.exp(log_decay * np.maximum(diff, 0)), 0.0) * R_QK ** -0.5
    tab_r = np.concatenate([np.cos(ang)[:, None], np.sin(ang)[:, None], decay], 1).astype(np.float32)

    slot = np.broadcast_to(np.arange(SEQ, dtype=np.float32), (P, SEQ)).copy()
    small = np.zeros((P, 32), np.float32)
    small[:, 0:4] = np.arange(GROUPS, 0, -1)
    small[:, 4:12] = np.arange(PER_GROUP, 0, -1)
    for k in range(TOPK):
        for q in range(TILES):
            small[:, 12 + k * TILES + q] = k * SEQ + q * P + p + 1
    return {"c_square": square, "c_tab_a": tab_a, "c_tab_r": tab_r, "c_slot": slot, "c_small": small}


class Banks:

    def __init__(self):
        self.uses = [0] * 8
        self.fulls = [0] * 8
        self.jobs = {}
        self.turn = 0

    def plan(self, name, bank=None):
        if bank is None:
            bank, self.turn = self.turn, (self.turn + 1) % 8
        self.fulls[bank] += name[0] != "O"
        self.jobs[name] = (bank, self.uses[bank], self.fulls[bank])
        self.uses[bank] += 1

    def at(self, *name):
        return self.jobs[name]


def plan_banks():
    b = Banks()

    def norm(n):
        for j in range(KC):
            b.plan(("norm", n, j))

    norm(0)
    for c in range(BC):
        b.plan(("gate", c))
    for c in range(BC):
        b.plan(("val", c))
    for kind, which, c in rope_order():
        b.plan((kind, which, c))
    for q in range(TILES):
        b.plan(("v", q))
    units = attention_units()
    for n in range(len(units) + 2):
        if n < len(units):
            b.plan(("S", units[n]), n % 3)
        if n == 4:
            b.plan(("cmean",), 7)
        if n == 8:
            b.plan(("cvar",), 7)
        if 1 <= n <= len(units):
            b.plan(("PT", units[n - 1]), 3 + (n - 1) % 2)
        if n >= 2:
            q, h = units[n - 2]
            if h == 0:
                b.plan(("O", q), 5 + q % 2)
        if n >= 4:
            q, h = units[min(n - 2, len(units) - 1)]
            if h == 2 and q > 0:
                b.plan(("aT", q - 1), 7)
    b.plan(("aT", TILES - 1), 7)
    b.turn = 0
    for half in range(2):
        for q in range(TILES):
            b.plan(("out0", half, q))
    norm(1)
    b.plan(("logits", 0))
    b.plan(("pos", 0))
    b.plan(("table", 0))
    b.before_experts = [list(b.uses)]
    norm(2)
    for kind, h, i in retention_order():
        b.plan((kind, h, i))
    norm(3)
    b.plan(("logits", 1))
    b.plan(("pos", 1))
    b.plan(("table", 1))
    b.before_experts.append(list(b.uses))
    return b


def rope_order():
    steps = [(w, c) for w in "qk" for c in range(A_WIDTH // P)]
    order = []
    for n, s in enumerate(steps):
        order.append(("proj",) + s)
        if n >= 1:
            order.append(("rot",) + steps[n - 1])
    return order + [("rot",) + steps[-1]]


def attention_units():
    return [(q, h) for q in range(TILES) for h in range(A_HEADS)]


def retention_order():
    order = []

    def tail(h):
        for q in range(TILES):
            order.append(("yT", h, q))
        for i in range(2 * TILES):
            order.append(("out1", h, i))

    for h in range(R_HEADS):
        order += [("qk", h, i) for i in range(4)]
        if h:
            tail(h - 1)
        order += [("rv", h, q) for q in range(TILES)]
        order += [("ST", h, j) for j in range(TILES)]
        order += [("rg", h, q) for q in range(TILES)]
        order += [("inner", h, q) for q in range(TILES)]
    tail(R_HEADS - 1)
    return order


def plan_blocks():
    even = [("w_in", c) for c in (4, 3, 0, 1, 2)] + [("w_out", c) for c in range(2)]
    odd = []
    for h in range(R_HEADS):
        odd.append(("qk", h))
        if h:
            odd.append(("wo", h - 1))
        odd += [("v", h), ("g", h)]
    odd.append(("wo", R_HEADS - 1))
    return even, odd


def trunk_kernel(nc, x, even_w_in, even_w_out, odd_w_in, odd_w_out, expert_w_gate, expert_w_up, expert_w_down,
                 gains, final_gain, conv_w, conv_p, router_w, router_b, c_square, c_tab_a, c_tab_r, c_slot, c_small, out):
    gains_dram = gains
    banks = plan_banks()
    even_blocks, odd_blocks = plan_blocks()
    n_moe = 3 * EXPERTS
    block_no = {("even",) + b: n for n, b in enumerate(even_blocks)}
    moe_start = [len(even_blocks)]
    first_odd = moe_start[0] + n_moe
    block_no.update({("odd",) + b: first_odd + n for n, b in enumerate(odd_blocks)})
    moe_start.append(first_odd + len(odd_blocks))
    landed_at = {}
    fills = [0] * SLOTS
    for n in range(moe_start[1] + n_moe):
        two = first_odd <= n < moe_start[1] and odd_blocks[n - first_odd][0] == "qk"
        fills[n % SLOTS] += 32 if two else 16
        landed_at[n] = fills[n % SLOTS]

    xs_dram = nc.dram_tensor("xs_dram", (SEQ, DM), F32, kind="Internal").ap()
    y_dram = nc.dram_tensor("y_dram", (TOPK * SEQ, DM), F32, kind="Internal").ap()

    with ExitStack() as ctx:
        def sb(name, shape, dt=F32):
            return ctx.enter_context(nc.sbuf_tensor(name, shape, dt))

        def sem(name):
            return ctx.enter_context(nc.semaphore(name))

        psum = ctx.enter_context(nc.psum_tensor("psum", [P, 8, 512], F32))

        ring = sb("ring", [P, SLOTS, BLOCK])
        h = sb("h", [P, TILES, DM])
        xs = sb("xs", [P, TILES * DM])
        uT = sb("uT", [P, KC, SEQ])
        tab_a = sb("tab_a", [P, 3, SEQ])
        square = sb("square", [P, 5, P])
        slot_no = sb("slot_no", [P, SEQ])
        small = sb("small", [P, 32])
        gains = sb("gains", [P, 4, KC])
        convw = sb("convw", [P, BC, TAPS])
        convp = sb("convp", [P, 3, BC])
        wr = sb("wr", [P, DEPTH, KC, NROUT])
        br = sb("br", [P, DEPTH, NROUT])
        stat = sb("stat", [P, 96])
        index = sb("index", [P, SLOT_TILES, EXPERTS, 2], U32)
        load = sb("load", [P, DEPTH], U32)
        gather_at = sb("gather_at", [P, 2], U32)
        scatter_at = sb("scatter_at", [P, 2], U32)
        scratch = sb("scratch", [P, 11500])

        used = [0]

        def take(n):
            used[0] += n
            assert used[0] <= 11500
            return scratch[:, used[0] - n:used[0]]

        qT = take(2048).rearrange("p (c t) -> p c t", c=4)
        kT = take(2048).rearrange("p (c t) -> p c t", c=4)
        v0 = take(2048).rearrange("p (q n) -> p q n", q=TILES)
        conv_in = take(BC * (SEQ + PAD)).rearrange("p (c t) -> p c t", c=BC)
        sm = take(1024).rearrange("p (b n) -> p b n", b=2)
        prob = take(1024).rearrange("p (b n) -> p b n", b=2)
        probT = take(1024).rearrange("p (b n) -> p b n", b=2)
        sigT = qT
        catT = xs[:, :].rearrange("p (c t) -> p c t", c=KC)
        raw = catT
        a_out = uT[:, :, :].rearrange("p c t -> p (c t)")[:, 0:2048].rearrange("p (q n) -> p q n", q=TILES)
        csq = conv_in[:, :, 0:SEQ]
        crs = uT[:, 6, :]
        crt = uT[:, 7, :]
        used[0] = 0
        qkT = take(2048).rearrange("p (c t) -> p c t", c=4)
        v1 = take(2048).rearrange("p (q n) -> p q n", q=TILES)
        sg = take(2048).rearrange("p (q n) -> p q n", q=TILES)
        yT = take(2048).rearrange("p (c t) -> p c t", c=4)
        smT = take(1280)
        rot_tmp = take(1024).rearrange("p (b n) -> p b n", b=2)
        gn = take(512)
        tab_r = xs[:, 0:6 * SEQ].rearrange("p (c t) -> p c t", c=6)
        used[0] = 0
        x_e = take(2048).rearrange("p (b n) -> p b n", b=2)
        xeT = take(2048).rearrange("p (b c t) -> p b c t", b=2, c=KC)
        silu_g = take(512)
        hid = take(512)
        hidT = take(512).rearrange("p (c t) -> p c t", c=HC)
        y_e = take(2048).rearrange("p (b n) -> p b n", b=2)
        junk = scratch[:, 2048:3072]
        fin_gain = take(1024)
        logit = take(TILES * NROUT).rearrange("p (q n) -> p q n", q=TILES)
        diff1 = take(16)
        exps1 = take(16)
        diff2 = take(TILES)
        exps2 = take(TILES)
        gp = take(TILES)
        best = take(TILES)
        best2 = take(TILES)
        pick = take(TILES)
        gate = take(TOPK * TILES).rearrange("p (k q) -> p k q", k=TOPK)
        of_group = take(16).rearrange("p (q g) -> p q g", q=TILES)
        cand = take(32)
        sel = take(32).rearrange("p (q n) -> p q n", q=TILES)
        sel2 = take(32).rearrange("p (q n) -> p q n", q=TILES)
        fine = [take(32).rearrange("p (q n) -> p q n", q=TILES) for _ in range(TOPK)]
        prod = take(TILES * EXPERTS)
        chosen_k = [take(TILES * EXPERTS).rearrange("p (q n) -> p q n", q=TILES) for _ in range(TOPK)]
        both = take(TILES * EXPERTS).rearrange("p (q n) -> p q n", q=TILES)
        pos = take(TILES * EXPERTS).rearrange("p (q n) -> p q n", q=TILES)
        place = take(TOPK * TILES)
        most_f = take(1)
        rows = take(TOPK * TILES * EXPERTS).rearrange("p (k n) -> p k n", k=TOPK * TILES)
        oh = uT
        y_back = [xs[:, :].rearrange("p (q n) -> p q n", q=TILES), uT[:, :, :].rearrange("p (q c) t -> p q (c t)", q=TILES)]

        ident, ones, before = square[:, 0], square[:, 1], square[:, 2]
        mean_w, swap = square[:, 3], square[:, 4]
        cos_a, sin_a, bias_a = tab_a[:, 0], tab_a[:, 1], tab_a[:, 2]

        bank_full = [sem(f"bank_full{b}") for b in range(8)]
        bank_free = [sem(f"bank_free{b}") for b in range(8)]
        landed = [sem(f"landed{s}") for s in range(SLOTS)]
        x_in = [sem(f"x_in{q}") for q in range(TILES)]
        const_in = sem("const_in")
        tab_r_in = sem("tab_r_in")
        fin_in = sem("fin_in")
        h_ready = sem("h_ready")
        squares = sem("squares")
        mean_sq = sem("mean_sq")
        root = sem("root")
        rstd_ok = sem("rstd_ok")
        xs_ready = sem("xs_ready")
        rot_cos = sem("rot_cos")
        rot_done = sem("rot_done")
        tap = sem("tap")
        csq_ok = sem("csq_ok")
        crs_ok = sem("crs_ok")
        cnorm = sem("cnorm")
        b_ok = sem("b_ok")
        mx_ok = sem("mx_ok")
        p_ok = sem("p_ok")
        pv_done = sem("pv_done")
        den_r = sem("den_r")
        radd = sem("radd")
        gstat = sem("gstat")
        gaggr = sem("gaggr")
        groot = sem("groot")
        grec = sem("grec")
        y_ok = sem("y_ok")
        out_sent = sem("out_sent")
        fin_ok = sem("fin_ok")

        class MoePass:

            def __init__(self, tag):
                self.indexed = [sem(f"{tag}_gather_at{b}") for b in range(2)]
                self.gathered = [sem(f"{tag}_gathered{b}") for b in range(2)]
                self.xT_psum = sem(f"{tag}_xT_psum")
                self.xT_ok = sem(f"{tag}_xT_ok")
                self.gate_psum = sem(f"{tag}_gate_psum")
                self.up_psum = sem(f"{tag}_up_psum")
                self.silu_ok = sem(f"{tag}_silu_ok")
                self.hid_ok = sem(f"{tag}_hid_ok")
                self.hidT_psum = sem(f"{tag}_hidT_psum")
                self.hidT_ok = sem(f"{tag}_hidT_ok")
                self.down_psum = sem(f"{tag}_down_psum")
                self.y_act = sem(f"{tag}_y_act")
                self.y_dve = sem(f"{tag}_y_dve")
                self.sc_indexed = sem(f"{tag}_sc_indexed")
                self.scattered = [sem(f"{tag}_scattered{b}") for b in range(2)]
                self.y_free = sem(f"{tag}_y_free")
                self.go = sem(f"{tag}_go")

        main = [MoePass(f"m{l}") for l in range(DEPTH)]
        over = [MoePass(f"o{l}") for l in range(DEPTH)]
        over_landed = [[sem(f"over_landed{l}_{i}") for i in range(3)] for l in range(DEPTH)]
        xs_stored = sem("xs_stored")
        step = sem("step")
        exp_done = sem("exp_done")
        index_ok = sem("index_ok")
        lists_read = sem("lists_read")
        reduced = sem("reduced")
        second = sem("second")
        chosen = sem("chosen")
        placed = sem("placed")
        eps_ok = sem("eps_ok")
        y_in = [sem(f"y_in{q}") for q in range(TILES)]
        moe_done = sem("moe_done")
        y_sum = sem("y_sum")

        w_in = even_w_in[0].rearrange("(p j) n -> p j n", j=KC)
        w_out = even_w_out[0].rearrange("(j p) n -> p j n", p=P)
        o_in = odd_w_in[0].rearrange("(p j) n -> p j n", j=KC)
        o_out = odd_w_out[0].rearrange("(h j p) n -> p h j n", h=R_HEADS, p=P)
        wg_dram = expert_w_gate.rearrange("l e (p j) n -> l e p (j n)", j=KC)
        wu_dram = expert_w_up.rearrange("l e (p j) n -> l e p (j n)", j=KC)
        wd_dram = expert_w_down.rearrange("l e (p j) n -> l e p (j n)", j=HC)
        x_dram = x[0].rearrange("(q p) d -> p q d", p=P)
        out_dram = out[0].rearrange("(q p) d -> p q d", p=P)
        xs_rows = xs_dram.rearrange("(q p) d -> p q d", p=P)
        y_rows = y_dram.rearrange("(k q p) d -> p k q d", k=TOPK, p=P)

        def slot8(n):
            return ring[:, n % SLOTS, :].rearrange("p (j n) -> p j n", j=KC)

        def slot4(n):
            return ring[:, n % SLOTS, :].rearrange("p (j n) -> p j n", j=HC)

        def down_no(e):
            return gate_no(e + 1) + 2 if e < EXPERTS - 1 else n_moe - 1

        def gate_no(e):
            return 2 + 3 * (e - 1) if e else 0

        def up_no(e):
            return gate_no(e) + 1

        PAIRS = (EXPERTS - 2) // 2

        def one(src, layer, e):
            return src[layer, e] if type(e) is int else src[layer, bass.ds(e, 1)].rearrange("a p n -> p (a n)")

        def expert_steps(eng, body):
            body(0, 0, 0)
            with eng.Fori(0, PAIRS) as i:
                body(2 * i + 1, 1, i)
                body(2 * i + 2, 2, i)
            body(EXPERTS - 1, 1, PAIRS)

        def copied(eng, *name):
            b, u, _ = banks.at(*name)
            eng.wait_ge(bank_free[b], u + 1)

        def normed(eng, n):
            for j in range(KC):
                copied(eng, "norm", n, j)

        def block_used(n):
            for layer in range(DEPTH):
                k = n - moe_start[layer]
                if 0 <= k < n_moe:
                    m = main[layer]
                    if k < 2:
                        return (m.gate_psum, m.up_psum)[k], 1
                    if k == n_moe - 1:
                        return m.down_psum, EXPERTS
                    e, kind = (k - 2) // 3 + 1, (k - 2) % 3
                    return ((m.gate_psum, e + 1), (m.up_psum, e + 1), (m.down_psum, e))[kind]
            if n < moe_start[0]:
                kind, c = even_blocks[n]
                name = ("out0", c, 3) if kind == "w_out" else \
                    {4: ("gate", 3), 3: ("val", 3), 0: ("proj", "q", 3), 1: ("proj", "k", 3), 2: ("v", 3)}[c]
            else:
                kind, hd = odd_blocks[n - first_odd]
                name = {"qk": ("qk", hd, 3), "wo": ("out1", hd, 7), "v": ("rv", hd, 3), "g": ("rg", hd, 3)}[kind]
            bank, _, full = banks.at(*name)
            return bank_full[bank], full

        block = ctx.enter_context(nc.Block())

        @block.sync
        def _(sp):
            def fill(n, parts):
                if n >= SLOTS:
                    done, value = block_used(n - SLOTS)
                    sp.wait_ge(done, value)
                for dst, src in parts:
                    sp.dma_start(dst, src).then_inc(landed[n % SLOTS], 16)

            for q in range(TILES):
                sp.dma_start(h[:, q], x_dram[:, q]).then_inc(x_in[q], 16)
            for b in even_blocks:
                src, c = (w_in, b[1]) if b[0] == "w_in" else (w_out, b[1])
                fill(block_no[("even",) + b], [(slot8(block_no[("even",) + b]), src[:, :, c * 512:(c + 1) * 512])])

            def experts(layer):
                m, first = main[layer], moe_start[layer]
                for e in range(3):
                    fill(first + gate_no(e), [(ring[:, (first + gate_no(e)) % SLOTS], wg_dram[layer, e])])
                    fill(first + up_no(e), [(ring[:, (first + up_no(e)) % SLOTS], wu_dram[layer, e])])
                    if e:
                        fill(first + down_no(e - 1), [(ring[:, (first + down_no(e - 1)) % SLOTS], wd_dram[layer, e - 1])])

                def load_step(e, s):
                    sp.wait_ge(m.gate_psum, e - 1)
                    g = (first + gate_no(s)) % SLOTS
                    sp.dma_start(ring[:, g], one(wg_dram, layer, e)).then_inc(landed[g], 16)
                    sp.wait_ge(m.up_psum, e - 1)
                    u = (first + up_no(s)) % SLOTS
                    sp.dma_start(ring[:, u], one(wu_dram, layer, e)).then_inc(landed[u], 16)
                    sp.wait_ge(m.down_psum, e - 2)
                    d = (first + gate_no(s) + 2) % SLOTS
                    sp.dma_start(ring[:, d], one(wd_dram, layer, e - 1)).then_inc(landed[d], 16)

                with sp.Fori(0, (EXPERTS - 4) // 2) as i:
                    load_step(2 * i + 3, 1)
                    load_step(2 * i + 4, 2)
                load_step(EXPERTS - 1, 1)
                fill(first + n_moe - 1, [(ring[:, (first + n_moe - 1) % SLOTS], wd_dram[layer, EXPERTS - 1])])

                sp.wait_ge(index_ok, layer + 1)
                most = sp.value_load(load[0:1, layer:layer + 1], min_val=0, max_val=SEQ)
                with sp.If(most > P):
                    m = over[layer]
                    for c in range(1, SLOT_TILES):
                        with sp.Fori(0, EXPERTS) as e:
                            sp.wait_ge(m.go, e + (EXPERTS * (c - 1) + 1))
                            for k, src in enumerate((wg_dram, wu_dram, wd_dram)):
                                sp.dma_start(ring[:, k], one(src, layer, e)).then_inc(over_landed[layer][k], 16)
                    sp.wait_ge(moe_done, layer + 1)

            experts(0)
            for b in odd_blocks:
                n = block_no[("odd",) + b]
                kind, hd = b
                if kind == "qk":
                    fill(n, [(slot8(n)[:, :, 0:R_QK], o_in[:, :, hd * R_QK:(hd + 1) * R_QK]),
                             (slot8(n)[:, :, R_QK:], o_in[:, :, R_QKW + hd * R_QK:R_QKW + (hd + 1) * R_QK])])
                elif kind == "wo":
                    fill(n, [(slot4(n), o_out[:, hd])])
                else:
                    c = 2 * R_QKW + (R_VW if kind == "g" else 0) + hd * R_V
                    fill(n, [(slot8(n), o_in[:, :, c:c + R_V])])
            experts(1)
            for q in range(TILES):
                sp.wait_ge(fin_ok, q + 1)
                sp.dma_start(out_dram[:, q], xs[:, q * DM:(q + 1) * DM]).then_inc(out_sent, 16)
            sp.wait_ge(out_sent, 16 * TILES)

        @block.tensor
        def _(pe):
            def open_bank(*name):
                b, u, _ = banks.at(*name)
                if u:
                    pe.wait_ge(bank_free[b], u)
                return psum[:, b], bank_full[b]

            def norm(n):
                pe.wait_ge(xs_ready, TILES * (n + 1))
                for j in range(KC):
                    dst, full = open_bank("norm", n, j)
                    for q in range(TILES):
                        mm = nc.tensor.transpose(dst[:, q * P:(q + 1) * P], xs[:, q * DM + j:(q + 1) * DM:KC], ident)
                    mm.then_inc(full, 1)

            def use_block(n):
                pe.wait_ge(landed[n % SLOTS], landed_at[n])

            def transpose_tokens(m, b):
                for j in range(KC):
                    mm = nc.tensor.transpose(psum[:, j // 4, (j % 4) * P:(j % 4 + 1) * P], x_e[:, b, j:DM:KC], ident)
                mm.then_inc(m.xT_psum, 1)

            def up_product(w, bank, b, done):
                for j in range(KC):
                    mm = nc.tensor.matmul(psum[:, bank], xeT[:, b, j], w[:, j], start=(j == 0), stop=(j == KC - 1))
                mm.then_inc(done, 1)

            def transpose_hidden(m):
                for j in range(HC):
                    mm = nc.tensor.transpose(psum[:, 4, j * P:(j + 1) * P], hid[:, j:HID:HC], ident)
                mm.then_inc(m.hidT_psum, 1)

            def down_product(m, w):
                for half in range(2):
                    for j in range(HC):
                        mm = nc.tensor.matmul(psum[:, 5 + half], hidT[:, j], w[:, j, half * 512:(half + 1) * 512],
                                              start=(j == 0), stop=(j == HC - 1))
                mm.then_inc(m.down_psum, 1)

            def moe(layer):
                m, first = main[layer], moe_start[layer]
                norm(2 * layer + 1)
                normed(pe, 2 * layer + 1)
                dst, full = open_bank("logits", layer)
                for q in range(TILES):
                    for j in range(KC):
                        mm = nc.tensor.matmul(dst[:, q * NROUT:(q + 1) * NROUT], uT[:, j, q * P:(q + 1) * P], wr[:, layer, j],
                                              start=(j == 0), stop=(j == KC - 1))
                mm.then_inc(full, 1)
                dst, full = open_bank("pos", layer)
                pe.wait_ge(chosen, layer + 1)
                for q in range(TILES):
                    for t in range(q + 1):
                        nc.tensor.matmul(dst[:, q * EXPERTS:(q + 1) * EXPERTS], before if t == q else ones, both[:, t],
                                         start=(t == 0), stop=(t == q))
                for t in range(TILES):
                    mm = nc.tensor.matmul(dst[:, TILES * EXPERTS:(TILES + 1) * EXPERTS], ones, both[:, t],
                                          start=(t == 0), stop=(t == TILES - 1))
                mm.then_inc(full, 1)
                dst, full = open_bank("table", layer)
                pe.wait_ge(placed, layer + 1)
                for c in range(SLOT_TILES):
                    for k in range(TOPK * TILES):
                        mm = nc.tensor.matmul(dst[:, c * EXPERTS:(c + 1) * EXPERTS], oh[:, k, c * P:(c + 1) * P], rows[:, k],
                                              start=(k == 0), stop=(k == TOPK * TILES - 1))
                mm.then_inc(full, 1)

                for b in range(8):
                    pe.wait_ge(bank_free[b], banks.before_experts[layer][b])
                pe.wait_ge(m.gathered[0], 16)
                transpose_tokens(m, 0)

                def wait_block(number, turn):
                    n = first + number
                    pe.wait_ge(landed[n % SLOTS], landed_at[n] + 16 * turn)

                def body(e, s, turn):
                    pe.wait_ge(m.xT_ok, e + 1)
                    if s:
                        pe.wait_ge(m.silu_ok, e)
                    wait_block(gate_no(s), turn)
                    up_product(slot8(first + gate_no(s)), 2, s % 2, m.gate_psum)
                    if s:
                        pe.wait_ge(m.hid_ok, e)
                        transpose_hidden(m)
                    wait_block(up_no(s), turn)
                    up_product(slot8(first + up_no(s)), 3, s % 2, m.up_psum)
                    if type(e) is not int or e < EXPERTS - 1:
                        pe.wait_ge(m.gathered[(s + 1) % 2], 16 * (turn + (s + 1) // 2 + 1))
                        transpose_tokens(m, (s + 1) % 2)
                    if s:
                        down(e - 1, gate_no(s) + 2, turn)

                def down(e, number, turn):
                    pe.wait_ge(m.hidT_ok, e + 1)
                    pe.wait_ge(m.y_act, e + 1)
                    pe.wait_ge(m.y_dve, e + 1)
                    wait_block(number, turn)
                    down_product(m, slot4(first + number))

                expert_steps(pe, body)
                pe.wait_ge(m.hid_ok, EXPERTS)
                transpose_hidden(m)
                down(EXPERTS - 1, n_moe - 1, 0)

                pe.wait_ge(index_ok, layer + 1)
                most = pe.value_load(load[0:1, layer:layer + 1], min_val=0, max_val=SEQ)
                with pe.If(most > P):
                    m, there = over[layer], over_landed[layer]
                    for c in range(1, SLOT_TILES):
                        with pe.Fori(0, EXPERTS) as e:
                            n = e + (EXPERTS * (c - 1) + 1)
                            pe.wait_ge(m.gathered[0], 16 * n)
                            transpose_tokens(m, 0)
                            pe.wait_ge(m.xT_ok, n)
                            pe.wait_ge(there[0], 16 * n)
                            up_product(slot8(0), 2, 0, m.gate_psum)
                            pe.wait_ge(there[1], 16 * n)
                            up_product(slot8(1), 3, 0, m.up_psum)
                            pe.wait_ge(m.hid_ok, n)
                            transpose_hidden(m)
                            pe.wait_ge(m.hidT_ok, n)
                            pe.wait_ge(there[2], 16 * n)
                            down_product(m, slot4(2))

            def a_transpose(q):
                dst, full = open_bank("aT", q)
                copied(pe, "O", q)
                for c in range(4):
                    mm = nc.tensor.transpose(dst[:, c * P:(c + 1) * P], a_out[:, q, c * P:(c + 1) * P], ident)
                mm.then_inc(full, 1)

            pe.wait_ge(const_in, 16 * N_CONST)
            norm(0)
            normed(pe, 0)
            n = block_no[("even", "w_in", 4)]
            use_block(n)
            for c in range(BC):
                dst, full = open_bank("gate", c)
                for j in range(KC):
                    mm = nc.tensor.matmul(dst, slot8(n)[:, j, c * P:(c + 1) * P], uT[:, j], start=(j == 0), stop=(j == KC - 1))
                mm.then_inc(full, 1)
            n = block_no[("even", "w_in", 3)]
            use_block(n)
            for c in range(BC):
                dst, full = open_bank("val", c)
                for j in range(KC):
                    mm = nc.tensor.matmul(dst, slot8(n)[:, j, c * P:(c + 1) * P], uT[:, j], start=(j == 0), stop=(j == KC - 1))
                mm.then_inc(full, 1)
            for kind, which, c in rope_order():
                dst, full = open_bank(kind, which, c)
                if kind == "proj":
                    n = block_no[("even", "w_in", "qk".index(which))]
                    if c == 0:
                        use_block(n)
                    for j in range(KC):
                        mm = nc.tensor.matmul(dst, slot8(n)[:, j, c * P:(c + 1) * P], uT[:, j], start=(j == 0), stop=(j == KC - 1))
                    mm.then_inc(full, 1)
                else:
                    copied(pe, "proj", which, c)
                    nc.tensor.matmul(dst, swap, raw[:, c], start=True, stop=True).then_inc(full, 1)
            n = block_no[("even", "w_in", 2)]
            use_block(n)
            for q in range(TILES):
                dst, full = open_bank("v", q)
                for j in range(KC):
                    mm = nc.tensor.matmul(dst, uT[:, j, q * P:(q + 1) * P], slot8(n)[:, j], start=(j == 0), stop=(j == KC - 1))
                mm.then_inc(full, 1)

            units = attention_units()
            pe.wait_ge(rot_done, 8)
            for n in range(len(units) + 2):
                if n < len(units):
                    q, hd = units[n]
                    dst, full = open_bank("S", (q, hd))
                    r = slice((hd % 2) * A_DIM, (hd % 2 + 1) * A_DIM)
                    w = (q + 1) * P
                    nc.tensor.matmul(dst[:, 0:w], qT[r, hd // 2, q * P:(q + 1) * P], kT[r, hd // 2, 0:w],
                                     start=True, stop=True).then_inc(full, 1)
                if n == 4:
                    dst, full = open_bank("cmean")
                    pe.wait_ge(tap, BC * TAPS)
                    for c in range(BC):
                        mm = nc.tensor.matmul(dst, mean_w, catT[:, 4 + c], start=(c == 0), stop=(c == BC - 1))
                    mm.then_inc(full, 1)
                if n == 8:
                    dst, full = open_bank("cvar")
                    pe.wait_ge(csq_ok, BC)
                    for c in range(BC):
                        mm = nc.tensor.matmul(dst, mean_w, csq[:, c], start=(c == 0), stop=(c == BC - 1))
                    mm.then_inc(full, 1)
                if 1 <= n <= len(units):
                    q, hd = units[n - 1]
                    dst, full = open_bank("PT", (q, hd))
                    pe.wait_ge(p_ok, n)
                    for j in range(q + 1):
                        mm = nc.tensor.transpose(dst[:, j * P:(j + 1) * P], prob[:, (n - 1) % 2, j * P:(j + 1) * P], ident)
                    mm.then_inc(full, 1)
                if n >= 2:
                    q, hd = units[n - 2]
                    if hd == 0:
                        o_dst, _ = open_bank("O", q)
                        copied(pe, "v", TILES - 1)
                    copied(pe, "PT", (q, hd))
                    for j in range(q + 1):
                        mm = nc.tensor.matmul(o_dst[:, hd * A_DIM:(hd + 1) * A_DIM], probT[:, n % 2, j * P:(j + 1) * P],
                                              v0[:, j, hd * A_DIM:(hd + 1) * A_DIM], start=(j == 0), stop=(j == q))
                    mm.then_inc(pv_done, 1)
                    if hd == 2 and q > 0:
                        a_transpose(q - 1)
            a_transpose(TILES - 1)
            copied(pe, "aT", TILES - 1)
            pe.wait_ge(b_ok, BC)
            for half in range(2):
                n = block_no[("even", "w_out", half)]
                use_block(n)
                for q in range(TILES):
                    dst, full = open_bank("out0", half, q)
                    for j in range(KC):
                        mm = nc.tensor.matmul(dst, catT[:, j, q * P:(q + 1) * P], slot8(n)[:, j], start=(j == 0), stop=(j == KC - 1))
                    mm.then_inc(full, 1)
            moe(0)

            norm(2)
            normed(pe, 2)

            def tail(hd):
                for q in range(TILES):
                    dst, full = open_bank("yT", hd, q)
                    pe.wait_ge(y_ok, hd * TILES + q + 1)
                    for c in range(4):
                        mm = nc.tensor.transpose(dst[:, c * P:(c + 1) * P], sg[:, q, c * P:(c + 1) * P], ident)
                    mm.then_inc(full, 1)
                n = block_no[("odd", "wo", hd)]
                use_block(n)
                for i in range(2 * TILES):
                    q, half = i // 2, i % 2
                    dst, full = open_bank("out1", hd, i)
                    copied(pe, "yT", hd, q)
                    for j in range(4):
                        mm = nc.tensor.matmul(dst, yT[:, j, q * P:(q + 1) * P], slot4(n)[:, j, half * 512:(half + 1) * 512],
                                              start=(j == 0), stop=(j == 3))
                    mm.then_inc(full, 1)

            for hd in range(R_HEADS):
                n = block_no[("odd", "qk", hd)]
                use_block(n)
                for c in range(4):
                    dst, full = open_bank("qk", hd, c)
                    for j in range(KC):
                        mm = nc.tensor.matmul(dst, slot8(n)[:, j, c * P:(c + 1) * P], uT[:, j], start=(j == 0), stop=(j == KC - 1))
                    mm.then_inc(full, 1)
                if hd:
                    tail(hd - 1)
                n = block_no[("odd", "v", hd)]
                use_block(n)
                for q in range(TILES):
                    dst, full = open_bank("rv", hd, q)
                    for j in range(KC):
                        mm = nc.tensor.matmul(dst, uT[:, j, q * P:(q + 1) * P], slot8(n)[:, j], start=(j == 0), stop=(j == KC - 1))
                    mm.then_inc(full, 1)
                pe.wait_ge(radd, 4 * (hd + 1))
                for j in range(TILES):
                    dst, full = open_bank("ST", hd, j)
                    w = (TILES - j) * P
                    for c in range(2):
                        mm = nc.tensor.matmul(dst[:, 0:w], qkT[:, 2 + c, j * P:(j + 1) * P], qkT[:, c, j * P:SEQ],
                                              start=(c == 0), stop=(c == 1))
                    mm.then_inc(full, 1)
                n = block_no[("odd", "g", hd)]
                use_block(n)
                for q in range(TILES):
                    dst, full = open_bank("rg", hd, q)
                    for j in range(KC):
                        mm = nc.tensor.matmul(dst, uT[:, j, q * P:(q + 1) * P], slot8(n)[:, j], start=(j == 0), stop=(j == KC - 1))
                    mm.then_inc(full, 1)
                copied(pe, "rv", hd, TILES - 1)
                copied(pe, "ST", hd, TILES - 1)
                for q in range(TILES):
                    dst, full = open_bank("inner", hd, q)
                    for j in range(q + 1):
                        mm = nc.tensor.matmul(dst, smT[:, ST_AT[j] + (q - j) * P:ST_AT[j] + (q - j + 1) * P], v1[:, j],
                                              start=(j == 0), stop=(j == q))
                    mm.then_inc(full, 1)
            tail(R_HEADS - 1)
            moe(1)

        @block.scalar
        def _(act):
            def bank(*name):
                b, _, full = banks.at(*name)
                act.wait_ge(bank_full[b], full)
                return psum[:, b], bank_free[b]

            def norm(n):
                for q in range(TILES):
                    if n == 0:
                        act.wait_ge(x_in[q], 16)
                    elif n == 1:
                        copied(act, "out0", 1, q)
                    elif n == 3:
                        copied(act, "out1", R_HEADS - 1, 2 * q + 1)
                    else:
                        act.wait_ge(h_ready, TILES * (n // 2 - 1) + q + 1)
                    if n or q:
                        act.wait_ge(squares, TILES * n + q)
                    nc.scalar.activation(junk, h[:, q], ACT.Square, accum_out=stat[:, q:q + 1]).then_inc(squares, 1)
                act.wait_ge(mean_sq, n + 1)
                nc.scalar.activation(stat[:, 8:12], stat[:, 4:8], ACT.Sqrt).then_inc(root, 1)

            def norm_copies(n):
                for j in range(1, KC, 2):
                    src, free = bank("norm", n, j)
                    nc.scalar.activation(uT[:, j], src, ACT.Copy, scale=gains[:, n, j:j + 1]).then_inc(free, 1)

            for dst, src in ((square[:], c_square), (gains[:], gains_dram), (tab_a[:], c_tab_a), (small[:], c_small),
                             (slot_no[:], c_slot), (convw[:], conv_w), (convp[:], conv_p), (wr[:], router_w), (br[:], router_b)):
                act.dma_start(dst, src).then_inc(const_in, 16)

            norm(0)
            act.wait_ge(const_in, 16 * N_CONST)
            norm_copies(0)
            for c in range(BC):
                src, free = bank("gate", c)
                nc.scalar.activation(sigT[:, c], src, ACT.Sigmoid).then_inc(free, 1)
            for kind, which, c in rope_order():
                if kind == "proj":
                    src, free = bank(kind, which, c)
                    if which == "k":
                        act.wait_ge(rot_cos, c + 1)
                        b, _, full = banks.at("rot", "q", c)
                        act.wait_ge(bank_full[b], full)
                    nc.scalar.activation(raw[:, c], src, ACT.Copy).then_inc(free, 1)
            for q in range(TILES):
                src, free = bank("v", q)
                nc.scalar.activation(v0[:, q], src, ACT.Copy).then_inc(free, 1)

            units = attention_units()
            for n in range(len(units) + 2):
                if n < len(units):
                    q, hd = units[n]
                    w = (q + 1) * P
                    act.wait_ge(mx_ok, n + 1)
                    if n >= 2:
                        b, _, full = banks.at("PT", units[n - 2])
                        act.wait_ge(bank_full[b], full)
                    if hd == 0 and q:
                        act.wait_ge(den_r, q)
                    nc.scalar.activation(prob[:, n % 2, 0:w], sm[:, n % 2, 0:w], ACT.Exp, bias=stat[:, 16 + n % 2:17 + n % 2],
                                         accum_out=stat[:, 24 + hd:25 + hd]).then_inc(p_ok, 1)
                if n >= 1 and n <= len(units):
                    q, hd = units[n - 1]
                    w = (q + 1) * P
                    src, free = bank("PT", (q, hd))
                    if n >= 3:
                        act.wait_ge(pv_done, n - 2)
                    nc.scalar.activation(probT[:, (n - 1) % 2, 0:w], src[:, 0:w], ACT.Copy).then_inc(free, 1)
                if n == 6:
                    copied(act, "cmean")
                    for c in range(BC):
                        nc.scalar.activation(csq[:, c], catT[:, 4 + c], ACT.Square).then_inc(csq_ok, 1)
                if n == 10:
                    src, free = bank("cvar")
                    act.wait_ge(eps_ok, 1)
                    nc.scalar.activation(crt, src, ACT.Sqrt, bias=stat[:, 40:41]).then_inc(free, 1)
                if n == 14:
                    for c in range(BC):
                        act.wait_ge(cnorm, c + 1)
                        nc.scalar.activation(catT[:, 4 + c], catT[:, 4 + c], ACT.Silu, bias=convp[:, 2, c:c + 1],
                                             scale=convp[:, 1, c:c + 1]).then_inc(b_ok, 1)
                if n >= 4:
                    q, hd = units[min(n - 2, len(units) - 1)]
                    if hd == 2 and q > 0:
                        src, free = bank("aT", q - 1)
                        nc.scalar.activation(catT[:, 0:4, (q - 1) * P:q * P], src.rearrange("p (c t) -> p c t", c=4),
                                             ACT.Copy).then_inc(free, 1)
            q = TILES - 1
            src, free = bank("aT", q)
            nc.scalar.activation(catT[:, 0:4, q * P:(q + 1) * P], src.rearrange("p (c t) -> p c t", c=4),
                                 ACT.Copy).then_inc(free, 1)

            def store_rows(layer):
                act.wait_ge(xs_ready, TILES * (2 * layer + 2))
                act.dma_start(xs_rows, xs[:, :].rearrange("p (q d) -> p q d", q=TILES)).then_inc(xs_stored, 16)

            def silu(m, n):
                act.wait_ge(m.gate_psum, n)
                nc.scalar.activation(silu_g, psum[:, 2], ACT.Silu).then_inc(m.silu_ok, 1)

            def copy_hidden(m, n):
                act.wait_ge(m.hidT_psum, n)
                nc.scalar.activation(hidT.rearrange("p c t -> p (c t)"), psum[:, 4], ACT.Copy).then_inc(m.hidT_ok, 1)

            def copy_y(m, n, b):
                act.wait_ge(m.down_psum, n)
                act.wait_ge(m.y_free, n)
                nc.scalar.activation(y_e[:, b, 0:512], psum[:, 5], ACT.Copy).then_inc(m.y_act, 1)

            def moe(layer):
                m = main[layer]
                act.wait_ge(reduced, layer + 1)
                nc.scalar.activation(exps1, diff1, ACT.Exp).then_inc(exp_done, 1)
                act.wait_ge(second, layer + 1)
                nc.scalar.activation(exps2, diff2, ACT.Exp).then_inc(exp_done, 1)
                act.sem_inc(m.y_act, 1)

                def body(e, s, turn):
                    if s:
                        act.wait_ge(m.hid_ok, e)
                    silu(m, e + 1)
                    if s:
                        copy_hidden(m, e)
                        copy_y(m, e, (s - 1) % 2)

                expert_steps(act, body)
                copy_hidden(m, EXPERTS)
                copy_y(m, EXPERTS, (EXPERTS - 1) % 2)
                act.wait_ge(index_ok, layer + 1)
                most = act.value_load(load[0:1, layer:layer + 1], min_val=0, max_val=SEQ)
                with act.If(most > P):
                    m = over[layer]
                    for c in range(1, SLOT_TILES):
                        with act.Fori(0, EXPERTS) as e:
                            n = e + (EXPERTS * (c - 1) + 1)
                            silu(m, n)
                            copy_hidden(m, n)
                            copy_y(m, n, 0)
                act.wait_ge(moe_done, layer + 1)
                for q in range(TILES):
                    for k in range(TOPK):
                        act.dma_start(y_back[k][:, q], y_rows[:, k, q]).then_inc(y_in[q], 16)

            norm(1)
            store_rows(0)
            norm_copies(1)
            moe(0)

            norm(2)
            b, _, full = banks.at("norm", 2, KC - 1)
            act.wait_ge(bank_full[b], full)
            act.dma_start(tab_r, c_tab_r).then_inc(tab_r_in, 16)
            norm_copies(2)

            def tail(hd):
                for q in range(TILES):
                    src, free = bank("yT", hd, q)
                    if hd:
                        b, _, full = banks.at("out1", hd - 1, 2 * TILES - 1)
                        act.wait_ge(bank_full[b], full)
                    nc.scalar.activation(yT[:, :, q * P:(q + 1) * P], src.rearrange("p (c t) -> p c t", c=4),
                                         ACT.Copy).then_inc(free, 1)

            for hd in range(R_HEADS):
                if hd:
                    tail(hd - 1)
                for q in range(TILES):
                    src, free = bank("rv", hd, q)
                    nc.scalar.activation(v1[:, q], src, ACT.Copy).then_inc(free, 1)
                for q in range(TILES):
                    src, free = bank("rg", hd, q)
                    nc.scalar.activation(sg[:, q], src, ACT.Silu).then_inc(free, 1)
                act.wait_ge(gaggr, TILES * (hd + 1))
                nc.scalar.activation(stat[:, 44:48], stat[:, 49:56:2], ACT.Sqrt, bias=stat[:, 40:41]).then_inc(groot, 1)
            tail(R_HEADS - 1)
            norm(3)
            store_rows(1)
            norm_copies(3)
            moe(1)
            act.dma_start(fin_gain, final_gain).then_inc(fin_in, 16)
            norm(4)

        @block.vector
        def _(dve):
            V = nc.vector
            steps = [0]

            def link(ins):
                steps[0] += 1
                ins.then_inc(step, 1)
                dve.wait_ge(step, steps[0])

            def bank(*name):
                b, _, full = banks.at(*name)
                dve.wait_ge(bank_full[b], full)
                return psum[:, b], bank_free[b]

            def root_mean(n):
                dve.wait_ge(squares, TILES * (n + 1))
                V.tensor_scalar(stat[:, 4:8], stat[:, 0:4], 1.0 / DM, EPS, ALU.mult, ALU.add).then_inc(mean_sq, 1)
                dve.wait_ge(root, n + 1)
                V.reciprocal(stat[:, 12:16], stat[:, 8:12]).then_inc(rstd_ok, 1)
                dve.wait_ge(rstd_ok, n + 1)

            def norm(n):
                root_mean(n)
                for q in range(TILES):
                    V.tensor_scalar(xs[:, q * DM:(q + 1) * DM], h[:, q], stat[:, 12 + q:13 + q], None, ALU.mult) \
                        .then_inc(xs_ready, 1)
                if n == 0:
                    dve.wait_ge(const_in, 16 * N_CONST)
                for j in range(0, KC, 2):
                    src, free = bank("norm", n, j)
                    V.tensor_scalar(uT[:, j], src, gains[:, n, j:j + 1], None, ALU.mult).then_inc(free, 1)

            V.memset(stat[:, 40:41], EPS).then_inc(eps_ok, 1)
            norm(0)
            V.memset(conv_in[:, :, 0:PAD], 0.0).then_inc(eps_ok, 1)
            dve.wait_ge(eps_ok, 2)
            for c in range(BC):
                copied(dve, "gate", c)
                src, free = bank("val", c)
                V.tensor_tensor(conv_in[:, c, PAD:], src, sigT[:, c], ALU.mult).then_inc(free, 1)
            copied(dve, "val", BC - 1)

            def taps(first, last):
                for i in range(first, last):
                    k, c = i // BC, i % BC
                    if i >= BC:
                        dve.wait_ge(tap, i - BC + 1)
                        V.scalar_tensor_tensor(out=catT[:, 4 + c], in0=conv_in[:, c, k:k + SEQ], scalar=convw[:, c, k:k + 1],
                                               in1=catT[:, 4 + c], op0=ALU.mult, op1=ALU.add).then_inc(tap, 1)
                    else:
                        V.tensor_scalar(catT[:, 4 + c], conv_in[:, c, k:k + SEQ], convw[:, c, k:k + 1], convp[:, 0, c:c + 1],
                                        ALU.mult, ALU.add).then_inc(tap, 1)

            rots = [(which, c) for kind, which, c in rope_order() if kind == "rot"]
            done = 0
            for n, (which, c) in enumerate(rots):
                taps(done, done + 14)
                done += 14
                src, free = bank("rot", which, c)
                if n >= 2:
                    dve.wait_ge(rot_done, n - 1)
                V.tensor_tensor(sm[:, n % 2], src, sin_a, ALU.mult).then_inc(free, 1)
                copied(dve, "rot", which, c)
                dve.wait_ge(rot_cos, n + 1)
                t = (qT if which == "q" else kT)[:, c]
                V.tensor_tensor(t, t, sm[:, n % 2], ALU.add).then_inc(rot_done, 1)
            taps(done, BC * TAPS)
            dve.wait_ge(rot_done, 8)

            units = attention_units()
            for n in range(len(units) + 3):
                if n < len(units):
                    q, hd = units[n]
                    w = (q + 1) * P
                    src, free = bank("S", (q, hd))
                    if n >= 2:
                        dve.wait_ge(p_ok, n - 1)
                    V.scalar_tensor_tensor(out=sm[:, n % 2, 0:w], in0=src[:, 0:w], scalar=A_DIM ** -0.5,
                                           in1=bias_a[:, SEQ - w:SEQ], op0=ALU.mult, op1=ALU.add).then_inc(free, 1)
                    copied(dve, "S", (q, hd))
                    V.tensor_reduce(stat[:, 16 + n % 2:17 + n % 2], sm[:, n % 2, 0:w], AX.X, ALU.max, negate=True) \
                        .then_inc(mx_ok, 1)
                if n % A_HEADS == 0 and n:
                    dve.wait_ge(p_ok, n)
                    if n > A_HEADS:
                        copied(dve, "O", n // A_HEADS - 2)
                    V.reciprocal(stat[:, 32:40], stat[:, 24:32]).then_inc(den_r, 1)
                    dve.wait_ge(den_r, n // A_HEADS)
                if n >= 3 and (n - 3) % A_HEADS == A_HEADS - 1:
                    q = (n - 3) // A_HEADS
                    b, _, _ = banks.at("O", q)
                    dve.wait_ge(pv_done, n - 2)
                    V.tensor_tensor(a_out[:, q].rearrange("p (h d) -> p h d", h=A_HEADS),
                                    psum[:, b].rearrange("p (h d) -> p h d", h=A_HEADS),
                                    stat[:, 32:40].unsqueeze(2).broadcast_to([P, A_HEADS, A_DIM]), ALU.mult) \
                        .then_inc(bank_free[b], 1)
                if n == 5:
                    src, free = bank("cmean")
                    for c in range(BC):
                        ins = V.tensor_tensor(catT[:, 4 + c], catT[:, 4 + c], src, ALU.subtract)
                    ins.then_inc(free, 1)
                if n == 12:
                    copied(dve, "cvar")
                    V.reciprocal(crs, crt).then_inc(crs_ok, 1)
                    dve.wait_ge(crs_ok, 1)
                    for c in range(BC):
                        V.tensor_tensor(catT[:, 4 + c], catT[:, 4 + c], crs, ALU.mult).then_inc(cnorm, 1)
            for half in range(2):
                for q in range(TILES):
                    src, free = bank("out0", half, q)
                    dst = h[:, q, half * 512:(half + 1) * 512]
                    V.tensor_tensor(dst, dst, src, ALU.add).then_inc(free, 1)

            def first_best(values, width, top, rank, out):
                c = cand[:, 0:TILES * width].rearrange("p (q n) -> p q n", q=TILES)
                wide = [P, TILES, width]
                link(V.tensor_reduce(top, values, AX.X, ALU.max))
                link(V.tensor_tensor(c, values, top.unsqueeze(2).broadcast_to(wide), ALU.is_equal))
                link(V.tensor_tensor(c, c, rank.unsqueeze(1).broadcast_to(wide), ALU.mult))
                link(V.tensor_reduce(pick, c, AX.X, ALU.max))
                link(V.tensor_tensor(out, c, pick.unsqueeze(2).broadcast_to(wide), ALU.is_equal))

            def route(layer):
                src, free = bank("logits", layer)
                V.tensor_tensor(logit, src[:, 0:TILES * NROUT].rearrange("p (q n) -> p q n", q=TILES),
                                br[:, layer].unsqueeze(1).broadcast_to([P, TILES, NROUT]), ALU.add).then_inc(free, 1)
                copied(dve, "logits", layer)
                group = logit[:, :, 0:GROUPS]
                first_best(group, GROUPS, best, small[:, 0:4], of_group)
                V.tensor_tensor(diff1.rearrange("p (q g) -> p q g", q=TILES), group,
                                best.unsqueeze(2).broadcast_to([P, TILES, GROUPS]), ALU.subtract).then_inc(reduced, 1)
                for q in range(TILES):
                    link(V.tensor_tensor(prod[:, 0:EXPERTS].rearrange("p (g e) -> p g e", g=GROUPS),
                                         logit[:, q, GROUPS:].rearrange("p (g e) -> p g e", g=GROUPS),
                                         of_group[:, q].unsqueeze(2).broadcast_to([P, GROUPS, PER_GROUP]), ALU.mult))
                    link(V.tensor_reduce(sel[:, q], prod[:, 0:EXPERTS].rearrange("p (g e) -> p e g", g=GROUPS), AX.X, ALU.add))
                first_best(sel, PER_GROUP, best, small[:, 4:12], fine[0])
                link(V.scalar_tensor_tensor(out=sel2, in0=fine[0], scalar=NEG, in1=sel, op0=ALU.mult, op1=ALU.add))
                first_best(sel2, PER_GROUP, best2, small[:, 4:12], fine[1])
                V.tensor_tensor(diff2, best2, best, ALU.subtract).then_inc(second, 1)
                for k in range(TOPK):
                    for q in range(TILES):
                        ins = V.tensor_tensor(chosen_k[k][:, q].rearrange("p (g e) -> p g e", g=GROUPS),
                                              of_group[:, q].unsqueeze(2).broadcast_to([P, GROUPS, PER_GROUP]),
                                              fine[k][:, q].unsqueeze(1).broadcast_to([P, GROUPS, PER_GROUP]), ALU.mult)
                link(ins)
                V.tensor_tensor(both, chosen_k[0], chosen_k[1], ALU.add).then_inc(chosen, 1)
                dve.wait_ge(exp_done, 2 * layer + 2)
                link(V.tensor_reduce(gp, exps1.rearrange("p (q g) -> p q g", q=TILES), AX.X, ALU.add))
                link(V.tensor_scalar(pick, exps2, 1.0, None, ALU.add))
                link(V.tensor_tensor(pick, pick, gp, ALU.mult))
                link(V.reciprocal(gate[:, 0], pick))
                link(V.tensor_tensor(gate[:, 1], gate[:, 0], exps2, ALU.mult))
                for k in range(TOPK):
                    ins = V.tensor_tensor(rows[:, k * TILES:(k + 1) * TILES], chosen_k[k],
                                          small[:, 12 + k * TILES:12 + (k + 1) * TILES].unsqueeze(2)
                                          .broadcast_to([P, TILES, EXPERTS]), ALU.mult)
                src, free = bank("pos", layer)
                V.tensor_reduce(most_f, src[:, TILES * EXPERTS:(TILES + 1) * EXPERTS], AX.X, ALU.max)
                V.tensor_copy(pos, src[:, 0:TILES * EXPERTS].rearrange("p (q n) -> p q n", q=TILES)).then_inc(free, 1)
                copied(dve, "pos", layer)
                V.tensor_copy(load[:, layer:layer + 1], most_f)
                for k in range(TOPK):
                    link(V.tensor_tensor(prod.rearrange("p (q n) -> p q n", q=TILES), pos, chosen_k[k], ALU.mult))
                    link(V.tensor_reduce(place[:, k * TILES:(k + 1) * TILES], prod.rearrange("p (q n) -> p q n", q=TILES),
                                         AX.X, ALU.add))
                for k in range(TOPK * TILES):
                    ins = V.tensor_scalar(oh[:, k], slot_no[:], place[:, k:k + 1], None, ALU.is_equal)
                ins.then_inc(placed, 1)
                src, free = bank("table", layer)
                V.tensor_copy(pos.rearrange("p q n -> p (q n)"), src[:, 0:SLOT_TILES * EXPERTS]).then_inc(free, 1)
                copied(dve, "table", layer)
                table = pos.rearrange("p q n -> p (q n)")
                link(V.tensor_scalar(prod, table, 0.0, EMPTY, ALU.is_equal, ALU.mult))
                link(V.scalar_tensor_tensor(out=table, in0=table, scalar=-1.0, in1=prod, op0=ALU.add, op1=ALU.add))
                link(V.tensor_scalar(prod, table, float(SEQ), -float(SEQ), ALU.is_ge, ALU.mult))
                both_at = index[:, :, :, :].rearrange("p c e k -> p (c e) k")
                link(V.tensor_copy(both_at[:, :, 1], table))
                V.tensor_tensor(both_at[:, :, 0], table, prod, ALU.add).then_inc(index_ok, 1)

            def copy_tokens(m, n, b, layer):
                dve.wait_ge(m.xT_psum, n)
                for half in range(2):
                    ins = V.tensor_tensor(xeT[:, b, 4 * half:4 * half + 4], psum[:, half].rearrange("p (c t) -> p c t", c=4),
                                          gains[:, 2 * layer + 1, 4 * half:4 * half + 4].unsqueeze(2).broadcast_to([P, 4, P]),
                                          ALU.mult)
                ins.then_inc(m.xT_ok, 1)

            def hidden(m, n):
                dve.wait_ge(m.up_psum, n)
                dve.wait_ge(m.silu_ok, n)
                V.tensor_tensor(hid, silu_g, psum[:, 3], ALU.mult).then_inc(m.hid_ok, 1)

            def copy_y(m, n, b):
                dve.wait_ge(m.down_psum, n)
                dve.wait_ge(m.y_free, n)
                V.tensor_copy(y_e[:, b, 512:1024], psum[:, 6]).then_inc(m.y_dve, 1)

            def moe(layer):
                norm(2 * layer + 1)
                route(layer)
                m = main[layer]
                dve.sem_inc(m.y_dve, 1)
                copy_tokens(m, 1, 0, layer)

                def body(e, s, turn):
                    if s:
                        dve.wait_ge(m.hidT_psum, e)
                    hidden(m, e + 1)
                    if type(e) is not int or e < EXPERTS - 1:
                        copy_tokens(m, e + 2, (s + 1) % 2, layer)
                    if s:
                        copy_y(m, e, (s - 1) % 2)

                expert_steps(dve, body)
                copy_y(m, EXPERTS, (EXPERTS - 1) % 2)
                most = dve.value_load(load[0:1, layer:layer + 1], min_val=0, max_val=SEQ)
                with dve.If(most > P):
                    m = over[layer]
                    for c in range(1, SLOT_TILES):
                        with dve.Fori(0, EXPERTS) as e:
                            n = e + (EXPERTS * (c - 1) + 1)
                            copy_tokens(m, n, 0, layer)
                            hidden(m, n)
                            copy_y(m, n, 0)
                for q in range(TILES):
                    dve.wait_ge(y_in[q], 32 * (layer + 1))
                    link(V.scalar_tensor_tensor(out=h[:, q], in0=y_back[0][:, q], scalar=gate[:, 0, q:q + 1],
                                                in1=h[:, q], op0=ALU.mult, op1=ALU.add))
                    V.scalar_tensor_tensor(out=h[:, q], in0=y_back[1][:, q], scalar=gate[:, 1, q:q + 1],
                                           in1=h[:, q], op0=ALU.mult, op1=ALU.add).then_inc(h_ready, 1)

            moe(0)

            norm(2)
            dve.wait_ge(tab_r_in, 16)
            cos_r, sin_r = tab_r[:, 0], tab_r[:, 1]

            def tail(hd):
                for i in range(2 * TILES):
                    q, half = i // 2, i % 2
                    src, free = bank("out1", hd, i)
                    dst = h[:, q, half * 512:(half + 1) * 512]
                    V.tensor_tensor(dst, dst, src, ALU.add).then_inc(free, 1)

            for hd in range(R_HEADS):
                for a in (0, 2):
                    x1, free1 = bank("qk", hd, a)
                    x2, free2 = bank("qk", hd, a + 1)
                    if hd and not a:
                        dve.wait_ge(y_ok, TILES * hd)
                    if hd or a:
                        dve.wait_ge(radd, 4 * hd + a)
                    V.tensor_tensor(rot_tmp[:, 0], x1, cos_r, ALU.mult)
                    V.tensor_tensor(rot_tmp[:, 1], x2, sin_r, ALU.mult)
                    V.tensor_tensor(qkT[:, a + 1], x2, cos_r, ALU.mult).then_inc(free2, 1)
                    V.tensor_tensor(gn, x1, sin_r, ALU.mult).then_inc(free1, 1)
                    copied(dve, "qk", hd, a)
                    copied(dve, "qk", hd, a + 1)
                    V.tensor_tensor(qkT[:, a], rot_tmp[:, 0], rot_tmp[:, 1], ALU.subtract).then_inc(radd, 1)
                    V.tensor_tensor(qkT[:, a + 1], qkT[:, a + 1], gn, ALU.add).then_inc(radd, 1)
                if hd:
                    tail(hd - 1)
                for j in range(TILES):
                    src, free = bank("ST", hd, j)
                    w = (TILES - j) * P
                    V.tensor_tensor(smT[:, ST_AT[j]:ST_AT[j] + w], src[:, 0:w], tab_r[:, 2 + hd, 0:w], ALU.mult).then_inc(free, 1)
                dve.wait_ge(radd, 4 * (hd + 1))
                if hd:
                    dve.wait_ge(y_ok, TILES * hd)
                for q in range(TILES):
                    src, _ = bank("inner", hd, q)
                    V.bn_stats(stat[:, 64 + 6 * q:70 + 6 * q], src).then_inc(gstat, 1)
                    dve.wait_ge(gstat, hd * TILES + q + 1)
                    V.bn_aggr(stat[:, 48 + 2 * q:50 + 2 * q], stat[:, 64 + 6 * q:70 + 6 * q]).then_inc(gaggr, 1)
                dve.wait_ge(groot, hd + 1)
                V.reciprocal(stat[:, 56:60], stat[:, 44:48]).then_inc(grec, 1)
                dve.wait_ge(grec, hd + 1)
                for q in range(TILES):
                    src, free = bank("inner", hd, q)
                    if q >= 2:
                        dve.wait_ge(y_ok, hd * TILES + q - 1)
                    V.tensor_scalar(rot_tmp[:, q % 2], src, stat[:, 48 + 2 * q:49 + 2 * q], stat[:, 56 + q:57 + q],
                                    ALU.subtract, ALU.mult).then_inc(free, 1)
                    copied(dve, "inner", hd, q)
                    copied(dve, "rg", hd, q)
                    V.tensor_tensor(sg[:, q], sg[:, q], rot_tmp[:, q % 2], ALU.mult).then_inc(y_ok, 1)
            tail(R_HEADS - 1)
            moe(1)
            root_mean(4)
            dve.wait_ge(fin_in, 16)
            for q in range(TILES):
                V.scalar_tensor_tensor(out=xs[:, q * DM:(q + 1) * DM], in0=h[:, q], scalar=stat[:, 12 + q:13 + q],
                                       in1=fin_gain, op0=ALU.mult, op1=ALU.mult).then_inc(fin_ok, 1)

        @block.gpsimd
        def _(pool):
            G = nc.gpsimd
            pool.wait_ge(const_in, 16 * N_CONST)
            for kind, which, c in rope_order():
                if kind == "rot":
                    copied(pool, "proj", which, c)
                    if which == "q":
                        copied(pool, "val", c)
                    G.tensor_tensor((qT if which == "q" else kT)[:, c], raw[:, c], cos_a, ALU.mult).then_inc(rot_cos, 1)

            def gather(m, c, e, b, n):
                src = index[:, c, e, 0:1] if type(e) is int else index[:, c, bass.ds(e, 1), 0]
                G.tensor_copy(gather_at[:, b:b + 1], src).then_inc(m.indexed[b], 1)
                pool.wait_ge(m.indexed[b], n)
                pool.sem_inc(lists_read, 1)
                G.indirect_dma_start(x_e[:, b], None, xs_dram, bass.IndirectOffsetOnAxis(ap=gather_at[:, b:b + 1], axis=0),
                                     bounds_check=SEQ - 1, oob_is_err=False).then_inc(m.gathered[b], 16)

            def scatter(m, c, e, b, n, count):
                src = index[:, c, e, 1:2] if type(e) is int else index[:, c, bass.ds(e, 1), 1]
                G.tensor_copy(scatter_at[:, 0:1], src).then_inc(m.sc_indexed, 1)
                pool.wait_ge(m.sc_indexed, n)
                pool.sem_inc(lists_read, 1)
                G.indirect_dma_start(y_dram, bass.IndirectOffsetOnAxis(ap=scatter_at[:, 0:1], axis=0), y_e[:, b], None,
                                     bounds_check=TOPK * SEQ - 1, oob_is_err=False).then_inc(m.scattered[b], 16)
                pool.wait_ge(m.scattered[b], 16 * count)
                pool.sem_inc(m.y_free, 1)

            def number(v):
                return v if type(v) is int else pool.snap(v)

            for layer in range(DEPTH):
                m = main[layer]
                pool.sem_inc(m.y_free, 2)
                pool.wait_ge(index_ok, layer + 1)
                pool.wait_ge(xs_stored, 16 * (layer + 1))
                gather(m, 0, 0, 0, 1)
                gather(m, 0, 1, 1, 1)

                def body(e, s, turn):
                    if type(e) is not int or e < EXPERTS - 2:
                        ahead, count = number(e + 2), number(turn + s // 2 + 2)
                        pool.wait_ge(m.xT_psum, e + 1)
                        gather(m, 0, ahead, s % 2, count)
                    if s:
                        store(e - 1, s - 1, turn)

                def store(e, s, turn):
                    e, count = number(e), number(turn + s // 2 + 1)
                    pool.wait_ge(m.y_act, e + 2)
                    pool.wait_ge(m.y_dve, e + 2)
                    scatter(m, 0, e, s % 2, e + 1, count)

                body(0, 0, 0)
                with pool.Fori(0, PAIRS - 1) as i:
                    body(2 * i + 1, 1, i)
                    body(2 * i + 2, 2, i)
                body(EXPERTS - 3, 1, PAIRS - 1)
                body(EXPERTS - 2, 2, PAIRS - 1)
                body(EXPERTS - 1, 1, PAIRS)
                store(EXPERTS - 1, 1, PAIRS)

                most = pool.value_load(load[0:1, layer:layer + 1], min_val=0, max_val=SEQ)
                with pool.If(most > P):
                    m = over[layer]
                    pool.sem_inc(m.y_free, 1)
                    for c in range(1, SLOT_TILES):
                        with pool.Fori(0, EXPERTS) as e:
                            n = e + (EXPERTS * (c - 1) + 1)
                            pool.sem_inc(m.go, 1)
                            gather(m, c, e, 0, n)
                            pool.wait_ge(m.y_act, n)
                            pool.wait_ge(m.y_dve, n)
                            scatter(m, c, e, 0, n, n)
                pool.sem_inc(moe_done, 1)


def kernel(**inputs):
    import concourse.bacc as bacc
    from concourse.bass_utils import run_bass_kernel_spmd

    a = {k: np.asarray(v) for k, v in inputs.items()}
    arrays = {k: np.ascontiguousarray(a[k]) for k in
              ("x", "even_w_in", "even_w_out", "odd_w_in", "odd_w_out", "expert_w_gate", "expert_w_up", "expert_w_down")}
    gains = np.stack([a["mix_norm"][0], a["ffn_norm"][0], a["mix_norm"][1], a["ffn_norm"][1]])
    arrays["gains"] = np.ascontiguousarray(gains.reshape(4, P, KC).transpose(1, 0, 2))
    arrays["final_gain"] = np.ascontiguousarray(np.broadcast_to(a["final_norm"], (P, DM)))
    arrays["conv_w"] = np.ascontiguousarray(a["conv_w"][0].reshape(TAPS, BC, P).transpose(2, 1, 0))
    arrays["conv_p"] = np.ascontiguousarray(
        np.stack([a[k][0].reshape(BC, P) for k in ("conv_b", "conv_norm_g", "conv_norm_b")]).transpose(2, 0, 1))
    router = np.concatenate([a["router_w1"], a["router_w2"]], 2)
    arrays["router_w"] = np.ascontiguousarray(router.reshape(DEPTH, P, KC, NROUT).transpose(1, 0, 2, 3))
    arrays["router_b"] = np.ascontiguousarray(
        np.broadcast_to(np.concatenate([a["router_b1"], a["router_b2"]], 1), (P, DEPTH, NROUT)))
    arrays.update(shape_constants())
    arrays = {f"in_{k}": v for k, v in arrays.items()}

    nc = bacc.Bacc("TRN2", target_bir_lowering=False, num_devices=1)
    aps = {k[3:]: nc.dram_tensor(k, v.shape, mybir.dt.from_np(v.dtype), kind="ExternalInput").ap() for k, v in arrays.items()}
    out = nc.dram_tensor("out", (1, SEQ, DM), F32, kind="ExternalOutput").ap()
    trunk_kernel(nc, out=out, **aps)
    r = run_bass_kernel_spmd(nc, [arrays], core_ids=[0])
    return r.results[0]["out"]
```

```python
from contextlib import ExitStack

import numpy as np

import concourse.bass as bass
from concourse import mybir

F32 = mybir.dt.float32
F32R = mybir.dt.float32r
U32 = mybir.dt.uint32
ALU = mybir.AluOpType
ACT = mybir.ActivationFunctionType
AX = mybir.AxisListType

P = 128
SEQ, DM, DEPTH = 512, 1024, 2
TILES = SEQ // P
KC = DM // P
EPS = 1e-6
NEG = -1e30
A_HEADS, A_DIM = 8, 64
A_WIDTH = A_HEADS * A_DIM
BRANCHES = ((128, 1), (512, 4), (2048, 16))
ROPE_THETA, ROPE_DIM = 500000.0, 16
B_WIDTH = DM - A_WIDTH
BC = B_WIDTH // P
TAPS = 31
PAD = TAPS - 1
R_HEADS, R_QK, R_V = 4, 256, 512
R_QKW, R_VW = R_HEADS * R_QK, R_HEADS * R_V
RET_THETA = 10000.0
GROUPS, PER_GROUP = 4, 8
EXPERTS = GROUPS * PER_GROUP
HID = 512
HC = HID // P
TOPK = 2
NROUT = GROUPS + EXPERTS
N_CONST = 8
CONV_AT = 13
ST_AT = [0, 4 * P, 7 * P, 9 * P]
SLOTS = 3
BLOCK = 4096
HALF = BLOCK // 2
SLOT_TILES = SEQ // P
ARENA = 55040
EMPTY = 4096.0


def shape_constants():
    p = np.arange(P)
    ident = np.eye(P, dtype=np.float32)
    ones = np.ones((P, P), np.float32)
    before = (p[:, None] < p[None, :]).astype(np.float32)
    mean = np.full((P, P), 1.0 / B_WIDTH, np.float32)
    half = ROPE_DIM // 2
    swap = np.zeros((P, P), np.float32)
    for h in range(P // A_DIM):
        for i in range(half):
            swap[h * A_DIM + half + i, h * A_DIM + i] = -1.0
            swap[h * A_DIM + i, h * A_DIM + half + i] = 1.0
    square = np.stack([ident, ones, before, mean, swap], 1)

    inv = (np.float32(ROPE_THETA) ** (-np.arange(0, ROPE_DIM, 2, dtype=np.float32) / ROPE_DIM)).astype(np.float32)
    ang = (np.arange(SEQ, dtype=np.float32)[:, None] * inv[None]).astype(np.float32)
    cos_a, sin_a = np.ones((P, SEQ), np.float32), np.zeros((P, SEQ), np.float32)
    for h in range(P // A_DIM):
        for i in range(ROPE_DIM):
            cos_a[h * A_DIM + i] = np.cos(ang[:, i % half])
            sin_a[h * A_DIM + i] = np.sin(ang[:, i % half])
    bias = np.empty((P, SEQ), np.float32)
    for b in range(TILES):
        dist = P * (TILES - 1 - b) + p[:, None] - p[None, :]
        count = sum(((dist >= 0) & (dist % dil == 0) & (dist <= win)).astype(np.int64) for win, dil in BRANCHES)
        bias[:, b * P:(b + 1) * P] = np.where(count > 0, np.log(np.maximum(count, 1)), NEG)
    tab_a = np.stack([cos_a, sin_a, bias], 1)

    inv = (np.float32(RET_THETA) ** (-np.linspace(0.0, 1.0, R_QK // 2, dtype=np.float32))).astype(np.float32)
    ang = (inv[:, None] * np.arange(SEQ, dtype=np.float32)[None]).astype(np.float32)
    decay = np.empty((P, R_HEADS, SEQ), np.float32)
    for h in range(R_HEADS):
        log_decay = np.log(1.0 - 2.0 ** (-5.0 - h))
        for d in range(TILES):
            diff = P * d + p[None, :] - p[:, None]
            decay[:, h, d * P:(d + 1) * P] = np.where(diff >= 0, np.exp(log_decay * np.maximum(diff, 0)), 0.0) * R_QK ** -0.5
    tab_r = np.concatenate([np.cos(ang)[:, None], np.sin(ang)[:, None], decay], 1).astype(np.float32)

    slot = np.broadcast_to(np.arange(SEQ, dtype=np.float32), (P, SEQ)).copy()
    small = np.zeros((P, 32), np.float32)
    small[:, 0:4] = np.arange(GROUPS, 0, -1)
    small[:, 4:12] = np.arange(PER_GROUP, 0, -1)
    for k in range(TOPK):
        for q in range(TILES):
            small[:, 12 + k * TILES + q] = k * SEQ + q * P + p + 1
    return {"c_square": square, "c_tab_a": tab_a, "c_tab_r": tab_r, "c_slot": slot, "c_small": small}


class Banks:

    def __init__(self):
        self.uses = [0] * 8
        self.fulls = [0] * 8
        self.jobs = {}
        self.turn = 0

    def plan(self, name, bank=None):
        if bank is None:
            bank, self.turn = self.turn, (self.turn + 1) % 8
        self.fulls[bank] += name[0] != "O"
        self.jobs[name] = (bank, self.uses[bank], self.fulls[bank])
        self.uses[bank] += 1

    def at(self, *name):
        return self.jobs[name]


def plan_banks():
    b = Banks()

    def norm(n):
        for j in range(KC):
            b.plan(("norm", n, j))

    norm(0)
    for c in range(BC):
        b.plan(("gate", c))
    for c in range(BC):
        b.plan(("val", c))
    for which, c in ROPE_CHUNKS[:4]:
        b.plan(("proj", which, c))
    for which, c in ROPE_CHUNKS[4:]:
        b.plan(("proj", which, c))
    for which, c in ROPE_CHUNKS[:4]:
        b.plan(("rot", which, c))
    for q in range(TILES):
        b.plan(("v", q))
    for which, c in ROPE_CHUNKS[4:]:
        b.plan(("rot", which, c))
    units = attention_units()
    for n in range(len(units) + 2):
        if n < len(units):
            b.plan(("S", units[n]), n % 3)
        if n == CONV_AT:
            b.plan(("cmean",), 7)
        if n == CONV_AT + 3:
            b.plan(("cvar",), 7)
        if 1 <= n <= len(units):
            b.plan(("PT", units[n - 1]), 3 + (n - 1) % 2)
        if n >= 2:
            q, h = units[n - 2]
            if h == 0:
                b.plan(("O", q), 5 + q % 2)
        if n >= 4:
            q, h = units[min(n - 2, len(units) - 1)]
            if h == 2 and q > 0:
                b.plan(("aT", q - 1), 7)
    b.plan(("aT", TILES - 1), 7)
    b.turn = 0
    for half in range(2):
        for q in range(TILES):
            b.plan(("out0", half, q))
    norm(1)
    b.plan(("logits", 0))
    b.plan(("pos", 0))
    b.plan(("table", 0))
    b.before_experts = [list(b.uses)]
    norm(2)
    for kind, h, i in retention_order():
        b.plan((kind, h) + (i if type(i) is tuple else (i,)))
    norm(3)
    b.plan(("logits", 1))
    b.plan(("pos", 1))
    b.plan(("table", 1))
    b.before_experts.append(list(b.uses))
    return b


ROPE_CHUNKS = [(which, c) for which in "qk" for c in range(A_WIDTH // P)]


def attention_units():
    return [(q, h) for q in range(TILES) for h in range(A_HEADS)]


def retention_order():
    order = []

    def tail(h):
        for q in range(TILES):
            order.append(("yT", h, q))
        for half in range(2):
            for q in range(TILES):
                order.append(("out1", h, (half, q)))

    for h in range(R_HEADS):
        order += [("qk", h, i) for i in range(4)]
        if h:
            tail(h - 1)
        order += [("rv", h, q) for q in range(TILES)]
        order += [("ST", h, j) for j in range(TILES)]
        order += [("rg", h, q) for q in range(TILES)]
        order += [("inner", h, q) for q in range(TILES)]
    tail(R_HEADS - 1)
    return order


def plan_blocks():
    even = [("w_in", c) for c in (4, 3, 0, 1, 2)] + [("w_out", c) for c in range(2)]
    odd = []
    for h in range(R_HEADS):
        odd.append(("qk", h))
        if h:
            odd.append(("wo", h - 1))
        odd += [("v", h), ("g", h)]
    odd.append(("wo", R_HEADS - 1))
    return even, odd


def trunk_kernel(nc, x, even_w_in, even_w_out, odd_w_in, odd_w_out, expert_w_gate, expert_w_up, expert_w_down,
                 gains, conv_w, conv_p, router_w, router_b, c_square, c_tab_a, c_tab_r, c_slot, c_small, out):
    gains_dram = gains
    banks = plan_banks()
    even_blocks, odd_blocks = plan_blocks()
    n_moe = 3 * EXPERTS
    block_no = {("even",) + b: n for n, b in enumerate(even_blocks)}
    moe_start = [len(even_blocks)]
    first_odd = moe_start[0] + n_moe
    block_no.update({("odd",) + b: first_odd + n for n, b in enumerate(odd_blocks)})
    moe_start.append(first_odd + len(odd_blocks))
    landed_at = {}
    fills = [0] * SLOTS
    for n in range(moe_start[1] + n_moe):
        two = first_odd <= n < moe_start[1] and odd_blocks[n - first_odd][0] == "qk"
        fills[n % SLOTS] += 32 if two else 16
        landed_at[n] = fills[n % SLOTS]
    dense = {}
    for n in list(range(moe_start[0])) + list(range(first_odd, moe_start[1])):
        dense[n] = len(dense)

    xs_dram = nc.dram_tensor("xs_dram", (SEQ, DM), F32, kind="Internal").ap()
    y_dram = nc.dram_tensor("y_dram", (TOPK * SEQ, DM), F32, kind="Internal").ap()

    with ExitStack() as ctx:
        def sb(name, shape, dt=F32):
            return ctx.enter_context(nc.sbuf_tensor(name, shape, dt))

        def sem(name):
            return ctx.enter_context(nc.semaphore(name))

        psum = ctx.enter_context(nc.psum_tensor("psum", [P, 8, 512], F32))

        base = (nc.sbuf_base + 31) // 32 * 32
        ctx.enter_context(nc.sbuf_tensor("arena", [P, ARENA + 8], F32))
        top = [0]

        def place(name, shape, dt=F32, at=None):
            size = int(np.prod(shape[1:]))
            if at is None:
                at, top[0] = top[0], top[0] + (size + 7) // 8 * 8
            assert at + size <= ARENA, name
            return nc.alloc_sbuf_tensor_at(name, shape, dt, offset=base + 4 * at)[tuple([slice(None)] * len(shape))]

        raw = place("raw", [P, SLOTS, BLOCK])
        w_hi = [place(f"w_hi{b}", [P, HALF], F32R) for b in range(2)]
        w_lo = [place(f"w_lo{b}", [P, HALF], F32R) for b in range(2)]
        h = place("h", [P, TILES, DM])
        xs = place("xs", [P, TILES * DM])
        uT_hi = place("uT_hi", [P, KC, SEQ], F32R)
        uT_lo = place("uT_lo", [P, KC, SEQ], F32R)
        square = place("square", [P, 5, P])
        slot_no = place("slot_no", [P, SEQ])
        small = place("small", [P, 32])
        gain_row = place("gain_row", [P, DM])
        convw = place("convw", [P, BC, TAPS])
        convp = place("convp", [P, 3, BC])
        wr = place("wr", [P, DEPTH, KC, NROUT])
        br = place("br", [P, DEPTH, NROUT])
        stat = place("stat", [P, 96])
        index = place("index", [P, SLOT_TILES, EXPERTS, 2], U32)
        load = place("load", [P, DEPTH], U32)
        gather_at = place("gather_at", [P, 2], U32)
        scatter_at = place("scatter_at", [P, 2], U32)
        shared = top[0]

        qT = place("qT", [P, 4, SEQ])
        kT = place("kT", [P, 4, SEQ])
        v0 = place("v0", [P, TILES, 512])
        conv_in = place("conv_in", [P, BC, SEQ + PAD])
        sm = place("sm", [P, 2, 512])
        prob = place("prob", [P, 2, 512])
        probT = place("probT", [P, 2, 512])
        tab_a = place("tab_a", [P, 3, SEQ])
        tap_in = place("tap_in", [P, 2, SEQ])
        sigT = qT
        mixT = xs[:, :].rearrange("p (c t) -> p c t", c=KC)
        rawT = mixT
        conv = mixT
        a_out = xs[:, 0:2048].rearrange("p (q n) -> p q n", q=TILES)
        cat_hi, cat_lo = uT_hi, uT_lo
        csq = conv_in[:, :, 0:SEQ]
        crt, crs = gain_row[:, 0:SEQ], gain_row[:, SEQ:]

        top[0] = shared
        qkT = place("qkT", [P, 4, SEQ])
        v1 = place("v1", [P, TILES, 512])
        sg = place("sg", [P, TILES, 512])
        smT = place("smT", [P, 10 * P])
        rot_tmp = place("rot_tmp", [P, 2, SEQ])
        gn = place("gn", [P, SEQ])
        yT_hi = place("yT_hi", [P, 4, SEQ], F32R)
        yT_lo = place("yT_lo", [P, 4, SEQ], F32R)
        tab_r = xs[:, 0:6 * SEQ].rearrange("p (c t) -> p c t", c=6)

        top[0] = shared
        uT = place("uT", [P, KC, SEQ])
        x_e = place("x_e", [P, 2, DM], at=shared)
        y_e = place("y_e", [P, 2, DM], at=shared + 2 * DM)
        oh = uT
        silu_g = place("silu_g", [P, HID])
        hid = place("hid", [P, HID])
        rt = place("rt", [P, 1408])
        w_hi += [place(f"w_hi{b}", [P, HALF], F32R) for b in (2, 3)]
        w_lo += [place(f"w_lo{b}", [P, HALF], F32R) for b in (2, 3)]
        xeT_hi, xeT_lo = [u[:, 4 * 0:4].rearrange("p a (b t) -> p (a b) t", t=P) for u in (uT_hi, uT_lo)]
        hidT_hi, hidT_lo = [u[:, 4].rearrange("p (c t) -> p c t", c=HC) for u in (uT_hi, uT_lo)]
        junk = place("junk", [P, DM], at=shared + 4096)
        y_back = [xs[:, :].rearrange("p (q n) -> p q n", q=TILES), uT[:, :, :].rearrange("p (q c) t -> p q (c t)", q=TILES)]

        used = [0]

        def take(n):
            used[0] += n
            assert used[0] <= 1408
            return rt[:, used[0] - n:used[0]]

        logit = take(TILES * NROUT).rearrange("p (q n) -> p q n", q=TILES)
        diff1 = take(16)
        exps1 = take(16)
        diff2 = take(TILES)
        exps2 = take(TILES)
        gp = take(TILES)
        best = take(TILES)
        best2 = take(TILES)
        pick = take(TILES)
        gate = take(TOPK * TILES).rearrange("p (k q) -> p k q", k=TOPK)
        of_group = take(16).rearrange("p (q g) -> p q g", q=TILES)
        cand = take(32)
        sel = take(32).rearrange("p (q n) -> p q n", q=TILES)
        sel2 = take(32).rearrange("p (q n) -> p q n", q=TILES)
        fine = [take(32).rearrange("p (q n) -> p q n", q=TILES) for _ in range(TOPK)]
        prod = take(TILES * EXPERTS)
        chosen_k = [take(TILES * EXPERTS).rearrange("p (q n) -> p q n", q=TILES) for _ in range(TOPK)]
        both = take(TILES * EXPERTS).rearrange("p (q n) -> p q n", q=TILES)
        pos = take(TILES * EXPERTS).rearrange("p (q n) -> p q n", q=TILES)
        rank = take(TOPK * TILES)
        most_f = take(1)
        rows = take(TOPK * TILES * EXPERTS).rearrange("p (k n) -> p k n", k=TOPK * TILES)
        ident, ones, before = square[:, 0], square[:, 1], square[:, 2]
        mean_w, swap = square[:, 3], square[:, 4]
        cos_a, sin_a, bias_a = tab_a[:, 0], tab_a[:, 1], tab_a[:, 2]

        bank_full = [sem(f"bank_full{b}") for b in range(8)]
        bank_free = [sem(f"bank_free{b}") for b in range(8)]
        landed = [sem(f"landed{s}") for s in range(SLOTS)]
        x_in = [sem(f"x_in{q}") for q in range(TILES)]
        const_in = sem("const_in")
        tab_r_in = sem("tab_r_in")
        h_ready = sem("h_ready")
        squares = sem("squares")
        mean_sq = sem("mean_sq")
        root = sem("root")
        rstd_ok = sem("rstd_ok")
        gain_in = sem("gain_in")
        norm_hi = sem("norm_hi")
        aT_hi = sem("aT_hi")
        b_silu = sem("b_silu")
        b_hi = sem("b_hi")
        yT_hi_ok = sem("yT_hi_ok")
        hi_ok = [sem(f"hi_ok{b}") for b in range(2)]
        lo_ok = [sem(f"lo_ok{b}") for b in range(2)]
        first_half = sem("first_half")
        xs_ready = sem("xs_ready")
        rot_cos = sem("rot_cos")
        rot_done = sem("rot_done")
        tap = sem("tap")
        tap_pool = sem("tap_pool")
        tap_mul = sem("tap_mul")
        csq_ok = sem("csq_ok")
        crs_ok = sem("crs_ok")
        cnorm = sem("cnorm")
        b_ok = sem("b_ok")
        mx_ok = sem("mx_ok")
        p_ok = sem("p_ok")
        pv_done = sem("pv_done")
        den_r = sem("den_r")
        radd = sem("radd")
        gstat = sem("gstat")
        gaggr = sem("gaggr")
        groot = sem("groot")
        grec = sem("grec")
        y_ok = sem("y_ok")
        out_sent = sem("out_sent")

        class MoePass:

            def __init__(self, tag, over_pass=False):
                buffers = 1 if over_pass else 2
                self.indexed = [sem(f"{tag}_gather_at{b}") for b in range(buffers)]
                self.gathered = [sem(f"{tag}_gathered{b}") for b in range(buffers)]
                self.xT_psum = sem(f"{tag}_xT_psum")
                self.xT_ok = sem(f"{tag}_xT_ok")
                self.xT_hi = sem(f"{tag}_xT_hi")
                self.hidT_hi = sem(f"{tag}_hidT_hi")
                if over_pass:
                    self.hi, self.lo = sem(f"{tag}_hi"), sem(f"{tag}_lo")
                else:
                    self.hi = [sem(f"{tag}_hi{b}") for b in range(4)]
                    self.lo = [sem(f"{tag}_lo{b}") for b in range(4)]
                if not over_pass:
                    self.gate_half = sem(f"{tag}_gate_half")
                    self.up_half = sem(f"{tag}_up_half")
                    self.down_half = sem(f"{tag}_down_half")
                self.gate_psum = sem(f"{tag}_gate_psum")
                self.up_psum = sem(f"{tag}_up_psum")
                self.silu_ok = sem(f"{tag}_silu_ok")
                self.hid_ok = sem(f"{tag}_hid_ok")
                self.hidT_psum = sem(f"{tag}_hidT_psum")
                self.hidT_ok = sem(f"{tag}_hidT_ok")
                self.down_psum = sem(f"{tag}_down_psum")
                self.y_act = sem(f"{tag}_y_act")
                self.y_dve = sem(f"{tag}_y_dve")
                self.sc_indexed = sem(f"{tag}_sc_indexed")
                self.scattered = [sem(f"{tag}_scattered{b}") for b in range(buffers)]
                self.y_free = sem(f"{tag}_y_free")
                if over_pass:
                    self.go = sem(f"{tag}_go")

        main = MoePass("m")
        over = [MoePass(f"o{l}", True) for l in range(DEPTH)]
        over_landed = [sem(f"over_landed{l}") for l in range(DEPTH)]
        xs_stored = sem("xs_stored")
        step = sem("step")
        exp_done = sem("exp_done")
        index_ok = sem("index_ok")
        lists_read = sem("lists_read")
        reduced = sem("reduced")
        second = sem("second")
        chosen = sem("chosen")
        placed = sem("placed")
        eps_ok = sem("eps_ok")
        y_in = [sem(f"y_in{q}") for q in range(TILES)]
        moe_done = sem("moe_done")
        y_sum = sem("y_sum")

        w_in = even_w_in[0].rearrange("(p j) n -> p j n", j=KC)
        w_out = even_w_out[0].rearrange("(j p) n -> p j n", p=P)
        o_in = odd_w_in[0].rearrange("(p j) n -> p j n", j=KC)
        o_out = odd_w_out[0].rearrange("(h j p) n -> p h j n", h=R_HEADS, p=P)
        wg_dram = expert_w_gate.rearrange("l e (p j) n -> l e p (j n)", j=KC)
        wu_dram = expert_w_up.rearrange("l e (p j) n -> l e p (j n)", j=KC)
        wd_dram = expert_w_down.rearrange("l e (p j) n -> l e p (j n)", j=HC)
        x_dram = x[0].rearrange("(q p) d -> p q d", p=P)
        out_dram = out[0].rearrange("(q p) d -> p q d", p=P)
        xs_rows = xs_dram.rearrange("(q p) d -> p q d", p=P)
        y_rows = y_dram.rearrange("(k q p) d -> p k q d", k=TOPK, p=P)

        def half_of(n, half, by_columns):
            if by_columns:
                return raw[:, n % SLOTS].rearrange("p (j c n) -> p c j n", j=HC, c=2)[:, half]
            return raw[:, n % SLOTS].rearrange("p (c j n) -> p c j n", c=2, j=4)[:, half]

        def part(w):
            return w[:, :].rearrange("p (j n) -> p j n", j=4)

        def down_no(e):
            return gate_no(e + 1) + 2 if e < EXPERTS - 1 else n_moe - 1

        def gate_no(e):
            return 2 + 3 * (e - 1) if e else 0

        def up_no(e):
            return gate_no(e) + 1

        FILLS = n_moe // 2
        TURNS = (EXPERTS - 4) // 2

        def one(src, layer, e):
            return src[layer, e] if type(e) is int else src[layer, bass.ds(e, 1)].rearrange("a p n -> p (a n)")

        def expert_steps(eng, body):
            body(0, 0, 0)
            body(1, 1, 0)
            with eng.Fori(0, TURNS) as i:
                body(2 * i + 2, 2, i)
                body(2 * i + 3, 3, i)
            body(EXPERTS - 2, 2, TURNS)
            body(EXPERTS - 1, 3, TURNS)

        def copied(eng, *name):
            b, u, _ = banks.at(*name)
            eng.wait_ge(bank_free[b], u + 1)

        def normed(eng, n):
            for j in range(KC):
                copied(eng, "norm", n, j)

        def last_product(n):
            if n < moe_start[0]:
                kind, c = even_blocks[n]
                name = ("out0", c, 3) if kind == "w_out" else \
                    {4: ("gate", 3), 3: ("val", 3), 0: ("proj", "q", 3), 1: ("proj", "k", 3), 2: ("v", 3)}[c]
            else:
                kind, hd = odd_blocks[n - first_odd]
                name = {"qk": ("qk", hd, 3), "wo": ("out1", hd, 1, 3), "v": ("rv", hd, 3), "g": ("rg", hd, 3)}[kind]
            bank, _, full = banks.at(*name)
            return bank_full[bank], full

        half_count, count = {}, 0
        for n in dense:
            if not (n >= first_odd and odd_blocks[n - first_odd][0] == "wo"):
                count += 1
                half_count[n] = count

        def half_used(n, half):
            if half:
                return last_product(n)
            if n in half_count:
                return first_half, half_count[n]
            bank, _, full = banks.at("out1", odd_blocks[n - first_odd][1], 0, 3)
            return bank_full[bank], full

        def moe_half_used(layer, k, half):
            m = main
            if k < 2:
                e, kind = 0, k
            elif k == n_moe - 1:
                e, kind = EXPERTS - 1, 2
            else:
                kind = (k - 2) % 3
                e = (k - 2) // 3 + (kind < 2)
            return ((m.gate_half, m.gate_psum), (m.up_half, m.up_psum), (m.down_half, m.down_psum))[kind][half], \
                EXPERTS * layer + e + 1

        def split_hi(act, n):
            by_columns = n >= first_odd and odd_blocks[n - first_odd][0] == "wo"
            act.wait_ge(landed[n % SLOTS], landed_at[n])
            for half in range(2):
                if n - 1 in dense:
                    act.wait_ge(*half_used(n - 1, half))
                elif n:
                    act.wait_ge(main.down_psum, EXPERTS)
                nc.scalar.activation(part(w_hi[half]), half_of(n, half, by_columns), ACT.Copy).then_inc(hi_ok[half], 1)

        def split_lo(dve, n, half):
            by_columns = n >= first_odd and odd_blocks[n - first_odd][0] == "wo"
            dve.wait_ge(hi_ok[half], dense[n] + 1)
            nc.vector.tensor_tensor(part(w_lo[half]), half_of(n, half, by_columns), part(w_hi[half]).bitcast(F32),
                                    ALU.subtract).then_inc(lo_ok[half], 1)

        def moe_split(eng, layer, kind, s, turn, lo):
            m = main
            k = {"gate": gate_no, "up": up_no, "down": down_no}[kind](s)
            n = moe_start[layer] + k
            for half in range(2):
                b = 2 * (k % 2) + half
                src = half_of(n, half, kind == "down")
                if lo:
                    eng.wait_ge(m.hi[b], layer * FILLS + k // 2 + 1 + 3 * turn)
                    nc.vector.tensor_tensor(part(w_lo[b]), src, part(w_hi[b]).bitcast(F32), ALU.subtract).then_inc(m.lo[b], 1)
                    continue
                eng.wait_ge(landed[n % SLOTS], landed_at[n] + 32 * turn)
                if k >= 2:
                    done, value = moe_half_used(layer, k - 2, half)
                    eng.wait_ge(done, value + 2 * turn)
                elif k == 0:
                    eng.wait_ge(*half_used(n - 1, half))
                nc.scalar.activation(part(w_hi[b]), src, ACT.Copy).then_inc(m.hi[b], 1)

        block = ctx.enter_context(nc.Block())

        @block.sync
        def _(sp):
            def split(n):
                if n in dense:
                    return lo_ok[1], dense[n] + 1
                layer = int(n >= moe_start[1])
                k = n - moe_start[layer]
                return main.lo[2 * (k % 2) + 1], layer * FILLS + k // 2 + 1

            def fill(n, parts):
                if n >= SLOTS:
                    sp.wait_ge(*split(n - SLOTS))
                for dst, src in parts:
                    sp.dma_start(dst, src).then_inc(landed[n % SLOTS], 16)

            def blocked(n):
                return raw[:, n % SLOTS].rearrange("p (j n) -> p j n", j=KC)

            for q in range(TILES):
                sp.dma_start(h[:, q], x_dram[:, q]).then_inc(x_in[q], 16)
            sp.wait_ge(const_in, 16)
            sp.wait_ge(gain_in, 16)
            for b in even_blocks:
                n = block_no[("even",) + b]
                if n == 1:
                    sp.wait_ge(const_in, 16 * N_CONST)
                src, c = (w_in, b[1]) if b[0] == "w_in" else (w_out, b[1])
                fill(n, [(blocked(n), src[:, :, c * 512:(c + 1) * 512])])

            def experts(layer):
                first = moe_start[layer]

                def load_step(e, s, turn):
                    for kind, src, x in (("gate", wg_dram, e), ("up", wu_dram, e), ("down", wd_dram, e - 1)):
                        if s == 0 and kind == "down":
                            continue
                        n = first + (down_no(s - 1) if kind == "down" else gate_no(s) + (kind == "up"))
                        done, value = split(n - SLOTS)
                        if n - SLOTS in dense:
                            sp.wait_ge(done, value)
                        else:
                            sp.wait_ge(done, value + 3 * turn)
                        sp.dma_start(raw[:, n % SLOTS], one(src, layer, x)).then_inc(landed[n % SLOTS], 16)

                expert_steps(sp, load_step)
                fill(first + n_moe - 1, [(raw[:, (first + n_moe - 1) % SLOTS], wd_dram[layer, EXPERTS - 1])])

                sp.wait_ge(index_ok, layer + 1)
                most = sp.value_load(load[0:1, layer:layer + 1], min_val=0, max_val=SEQ)
                with sp.If(most > P):
                    m = over[layer]
                    for c in range(1, SLOT_TILES):
                        with sp.Fori(0, EXPERTS) as e:
                            sp.wait_ge(m.go, e + (EXPERTS * (c - 1) + 1))
                            for k, src in enumerate((wg_dram, wu_dram, wd_dram)):
                                sp.dma_start(raw[:, k], one(src, layer, e)).then_inc(over_landed[layer], 16)
                    sp.wait_ge(moe_done, layer + 1)

            experts(0)
            for b in odd_blocks:
                n = block_no[("odd",) + b]
                kind, hd = b
                if n == first_odd + 1:
                    for q in range(TILES):
                        sp.wait_ge(y_in[q], 32)
                if kind == "qk":
                    fill(n, [(blocked(n)[:, :, 0:R_QK], o_in[:, :, hd * R_QK:(hd + 1) * R_QK]),
                             (blocked(n)[:, :, R_QK:], o_in[:, :, R_QKW + hd * R_QK:R_QKW + (hd + 1) * R_QK])])
                elif kind == "wo":
                    fill(n, [(raw[:, n % SLOTS].rearrange("p (j n) -> p j n", j=HC), o_out[:, hd])])
                else:
                    c = 2 * R_QKW + (R_VW if kind == "g" else 0) + hd * R_V
                    fill(n, [(blocked(n), o_in[:, :, c:c + R_V])])
            experts(1)
            for q in range(TILES):
                sp.wait_ge(xs_ready, 4 * TILES + q + 1)
                sp.dma_start(out_dram[:, q], xs[:, q * DM:(q + 1) * DM]).then_inc(out_sent, 16)
            sp.wait_ge(out_sent, 16 * TILES)

        @block.tensor
        def _(pe):
            def open_bank(*name):
                b, u, _ = banks.at(*name)
                if u:
                    pe.wait_ge(bank_free[b], u)
                return psum[:, b], bank_full[b]

            def product(dst, still, moving, start, stop):
                nc.tensor.matmul(dst, still[0], moving[0], start=start, stop=False)
                nc.tensor.matmul(dst, still[1], moving[0], start=False, stop=False)
                return nc.tensor.matmul(dst, still[0], moving[1], start=False, stop=stop)

            def norm(n):
                pe.wait_ge(xs_ready, TILES * (n + 1))
                for j in range(KC):
                    dst, full = open_bank("norm", n, j)
                    for q in range(TILES):
                        mm = nc.tensor.transpose(dst[:, q * P:(q + 1) * P], xs[:, q * DM + j:(q + 1) * DM:KC], ident)
                    mm.then_inc(full, 1)

            def parts(half):
                return part(w_hi[half]), part(w_lo[half])

            def dense_half(n, half, names, x_hi, x_lo, channels_out, between=None):
                pe.wait_ge(lo_ok[half], dense[n] + 1)
                hi, lo = parts(half)
                for i, name in enumerate(names):
                    if half == 0:
                        dst, full = open_bank(*name)
                    else:
                        b, _, _ = banks.at(*name)
                        dst, full = psum[:, b], bank_full[b]
                    c = slice(i * P, (i + 1) * P)
                    for j in range(4):
                        w = (hi[:, j], lo[:, j])
                        x = (x_hi[:, 4 * half + j], x_lo[:, 4 * half + j])
                        if channels_out:
                            mm = product(dst, [a[:, c] for a in w], x, half + j == 0, half * j == 3)
                        else:
                            mm = product(dst, [a[:, c] for a in x], w, half + j == 0, half * j == 3)
                    if half:
                        mm.then_inc(full, 1)
                if not half:
                    mm.then_inc(first_half, 1)

            def transpose_tokens(m, b):
                for j in range(KC):
                    mm = nc.tensor.transpose(psum[:, j // 4, (j % 4) * P:(j % 4 + 1) * P], x_e[:, b, j:DM:KC], ident)
                mm.then_inc(m.xT_psum, 1)

            def up_product(pairs, bank, b, half_done, done, ready):
                for half, pair in enumerate(pairs):
                    hi, lo = part(w_hi[pair]), part(w_lo[pair])
                    ready(pair, False)
                    for j in range(4):
                        c = 8 * b + 4 * half + j
                        nc.tensor.matmul(psum[:, bank], xeT_hi[:, c], hi[:, j], start=(half + j == 0), stop=False)
                        nc.tensor.matmul(psum[:, bank], xeT_lo[:, c], hi[:, j], start=False, stop=False)
                    ready(pair, True)
                    for j in range(4):
                        c = 8 * b + 4 * half + j
                        mm = nc.tensor.matmul(psum[:, bank], xeT_hi[:, c], lo[:, j], start=False, stop=(half * j == 3))
                    if half:
                        mm.then_inc(done, 1)
                    elif half_done:
                        mm.then_inc(half_done, 1)

            def transpose_hidden(m):
                for j in range(HC):
                    mm = nc.tensor.transpose(psum[:, 4, j * P:(j + 1) * P], hid[:, j:HID:HC], ident)
                mm.then_inc(m.hidT_psum, 1)

            def down_product(m, pairs, half_done, ready):
                for half, pair in enumerate(pairs):
                    hi, lo = part(w_hi[pair]), part(w_lo[pair])
                    ready(pair, False)
                    for j in range(HC):
                        nc.tensor.matmul(psum[:, 5 + half], hidT_hi[:, j], hi[:, j], start=(j == 0), stop=False)
                        nc.tensor.matmul(psum[:, 5 + half], hidT_lo[:, j], hi[:, j], start=False, stop=False)
                    ready(pair, True)
                    for j in range(HC):
                        mm = nc.tensor.matmul(psum[:, 5 + half], hidT_hi[:, j], lo[:, j], start=False, stop=(j == HC - 1))
                    if half:
                        mm.then_inc(m.down_psum, 1)
                    elif half_done:
                        mm.then_inc(half_done, 1)

            def moe(layer):
                m, past = main, EXPERTS * layer
                norm(2 * layer + 1)
                normed(pe, 2 * layer + 1)
                dst, full = open_bank("logits", layer)
                for q in range(TILES):
                    for j in range(KC):
                        mm = nc.tensor.matmul(dst[:, q * NROUT:(q + 1) * NROUT], uT[:, j, q * P:(q + 1) * P], wr[:, layer, j],
                                              start=(j == 0), stop=(j == KC - 1))
                mm.then_inc(full, 1)
                dst, full = open_bank("pos", layer)
                pe.wait_ge(chosen, layer + 1)
                for q in range(TILES):
                    for t in range(q + 1):
                        nc.tensor.matmul(dst[:, q * EXPERTS:(q + 1) * EXPERTS], before if t == q else ones, both[:, t],
                                         start=(t == 0), stop=(t == q))
                for t in range(TILES):
                    mm = nc.tensor.matmul(dst[:, TILES * EXPERTS:(TILES + 1) * EXPERTS], ones, both[:, t],
                                          start=(t == 0), stop=(t == TILES - 1))
                mm.then_inc(full, 1)
                dst, full = open_bank("table", layer)
                pe.wait_ge(placed, layer + 1)
                for c in range(SLOT_TILES):
                    for k in range(TOPK * TILES):
                        mm = nc.tensor.matmul(dst[:, c * EXPERTS:(c + 1) * EXPERTS], oh[:, k, c * P:(c + 1) * P], rows[:, k],
                                              start=(k == 0), stop=(k == TOPK * TILES - 1))
                mm.then_inc(full, 1)

                for b in range(8):
                    pe.wait_ge(bank_free[b], banks.before_experts[layer][b])
                pe.wait_ge(m.gathered[0], 16 * (past // 2 + 1))
                transpose_tokens(m, 0)

                def split_of(k, turn):
                    def ready(pair, lo):
                        pe.wait_ge((m.lo if lo else m.hi)[pair], layer * FILLS + k // 2 + 1 + 3 * turn)
                    return (2 * (k % 2), 2 * (k % 2) + 1), ready

                def body(e, s, turn):
                    pe.wait_ge(m.xT_ok, e + (past + 1))
                    if past or s:
                        pe.wait_ge(m.silu_ok, e + past)
                    pairs, ready = split_of(gate_no(s), turn)
                    up_product(pairs, 2, s % 2, m.gate_half, m.gate_psum, ready)
                    if past or s:
                        pe.wait_ge(m.hid_ok, e + past)
                    if s:
                        transpose_hidden(m)
                    pairs, ready = split_of(up_no(s), turn)
                    up_product(pairs, 3, s % 2, m.up_half, m.up_psum, ready)
                    if type(e) is not int or e < EXPERTS - 1:
                        pe.wait_ge(m.gathered[(s + 1) % 2], 16 * (turn + (past // 2 + (s + 1) // 2 + 1)))
                        transpose_tokens(m, (s + 1) % 2)
                    if s:
                        down(e - 1, down_no(s - 1), turn)

                def down(e, k, turn):
                    pe.wait_ge(m.hidT_ok, e + (past + 1))
                    pe.wait_ge(m.y_act, e + (past + 1))
                    pe.wait_ge(m.y_dve, e + (past + 1))
                    pairs, ready = split_of(k, turn)
                    down_product(m, pairs, m.down_half, ready)

                expert_steps(pe, body)
                pe.wait_ge(m.hid_ok, past + EXPERTS)
                transpose_hidden(m)
                down(EXPERTS - 1, n_moe - 1, 0)

                pe.wait_ge(index_ok, layer + 1)
                most = pe.value_load(load[0:1, layer:layer + 1], min_val=0, max_val=SEQ)
                with pe.If(most > P):
                    m = over[layer]
                    for c in range(1, SLOT_TILES):
                        with pe.Fori(0, EXPERTS) as e:
                            n = e + (EXPERTS * (c - 1) + 1)

                            def ready_at(first):
                                def ready(pair, lo):
                                    pe.wait_ge(m.lo if lo else m.hi, 6 * n - 5 + first + pair % 2)
                                return ready

                            pe.wait_ge(m.gathered[0], 16 * n)
                            transpose_tokens(m, 0)
                            pe.wait_ge(m.xT_ok, n)
                            up_product((0, 1), 2, 0, None, m.gate_psum, ready_at(0))
                            up_product((2, 3), 3, 0, None, m.up_psum, ready_at(2))
                            pe.wait_ge(m.hid_ok, n)
                            transpose_hidden(m)
                            pe.wait_ge(m.hidT_ok, n)
                            down_product(m, (0, 1), None, ready_at(4))

            def a_transpose(q):
                dst, full = open_bank("aT", q)
                copied(pe, "O", q)
                for c in range(4):
                    mm = nc.tensor.transpose(dst[:, c * P:(c + 1) * P], a_out[:, q, c * P:(c + 1) * P], ident)
                mm.then_inc(full, 1)

            pe.wait_ge(const_in, 16)
            norm(0)
            pe.wait_ge(const_in, 16 * N_CONST)
            normed(pe, 0)

            def even(c, half):
                n = block_no[("even", "w_in", c)]
                names = {4: [("gate", i) for i in range(4)], 3: [("val", i) for i in range(4)],
                         0: [("proj", "q", i) for i in range(4)], 1: [("proj", "k", i) for i in range(4)],
                         2: [("v", i) for i in range(4)]}[c]
                dense_half(n, half, names, uT_hi, uT_lo, c != 2)

            def rotate(which):
                for c in range(4):
                    dst, full = open_bank("rot", which, c)
                    copied(pe, "proj", which, c)
                    nc.tensor.matmul(dst, swap, rawT[:, c], start=True, stop=True).then_inc(full, 1)

            for c, half in ((4, 0), (4, 1), (3, 0), (3, 1), (0, 0), (0, 1), (1, 0)):
                even(c, half)
            even(1, 1)
            rotate("q")
            even(2, 0)
            rotate("k")
            even(2, 1)

            units = attention_units()
            pe.wait_ge(rot_done, 8)
            for n in range(len(units) + 2):
                if n < len(units):
                    q, hd = units[n]
                    dst, full = open_bank("S", (q, hd))
                    r = slice((hd % 2) * A_DIM, (hd % 2 + 1) * A_DIM)
                    w = (q + 1) * P
                    nc.tensor.matmul(dst[:, 0:w], qT[r, hd // 2, q * P:(q + 1) * P], kT[r, hd // 2, 0:w],
                                     start=True, stop=True).then_inc(full, 1)
                if n == CONV_AT:
                    dst, full = open_bank("cmean")
                    pe.wait_ge(tap, 3 * TAPS)
                    pe.wait_ge(tap_pool, TAPS)
                    for c in range(BC):
                        mm = nc.tensor.matmul(dst, mean_w, conv[:, 4 + c], start=(c == 0), stop=(c == BC - 1))
                    mm.then_inc(full, 1)
                if n == CONV_AT + 3:
                    dst, full = open_bank("cvar")
                    pe.wait_ge(csq_ok, BC)
                    for c in range(BC):
                        mm = nc.tensor.matmul(dst, mean_w, csq[:, c], start=(c == 0), stop=(c == BC - 1))
                    mm.then_inc(full, 1)
                if 1 <= n <= len(units):
                    q, hd = units[n - 1]
                    dst, full = open_bank("PT", (q, hd))
                    pe.wait_ge(p_ok, n)
                    for j in range(q + 1):
                        mm = nc.tensor.transpose(dst[:, j * P:(j + 1) * P], prob[:, (n - 1) % 2, j * P:(j + 1) * P], ident)
                    mm.then_inc(full, 1)
                if n >= 2:
                    q, hd = units[n - 2]
                    if hd == 0:
                        o_dst, _ = open_bank("O", q)
                        copied(pe, "v", TILES - 1)
                    copied(pe, "PT", (q, hd))
                    for j in range(q + 1):
                        mm = nc.tensor.matmul(o_dst[:, hd * A_DIM:(hd + 1) * A_DIM], probT[:, n % 2, j * P:(j + 1) * P],
                                              v0[:, j, hd * A_DIM:(hd + 1) * A_DIM], start=(j == 0), stop=(j == q))
                    mm.then_inc(pv_done, 1)
                    if hd == 2 and q > 0:
                        a_transpose(q - 1)
            a_transpose(TILES - 1)
            copied(pe, "aT", TILES - 1)
            pe.wait_ge(b_ok, BC)
            for half in range(2):
                n = block_no[("even", "w_out", half)]
                for k in range(2):
                    dense_half(n, k, [("out0", half, q) for q in range(TILES)], cat_hi, cat_lo, False)
            moe(0)

            norm(2)
            normed(pe, 2)

            def odd(kind, hd, job):
                n = block_no[("odd", kind, hd)]
                for half in range(2):
                    dense_half(n, half, [(job, hd, i) for i in range(4)], uT_hi, uT_lo, kind == "qk")

            def tail(hd):
                for q in range(TILES):
                    dst, full = open_bank("yT", hd, q)
                    pe.wait_ge(y_ok, hd * TILES + q + 1)
                    for c in range(4):
                        mm = nc.tensor.transpose(dst[:, c * P:(c + 1) * P], sg[:, q, c * P:(c + 1) * P], ident)
                    mm.then_inc(full, 1)
                n = block_no[("odd", "wo", hd)]
                for half in range(2):
                    pe.wait_ge(lo_ok[half], dense[n] + 1)
                    hi, lo = parts(half)
                    for q in range(TILES):
                        dst, full = open_bank("out1", hd, half, q)
                        copied(pe, "yT", hd, q)
                        for j in range(4):
                            c = slice(q * P, (q + 1) * P)
                            mm = product(dst, (yT_hi[:, j, c], yT_lo[:, j, c]), (hi[:, j], lo[:, j]), j == 0, j == 3)
                        mm.then_inc(full, 1)

            for hd in range(R_HEADS):
                odd("qk", hd, "qk")
                if hd:
                    tail(hd - 1)
                odd("v", hd, "rv")
                pe.wait_ge(radd, 4 * (hd + 1))
                for j in range(TILES):
                    dst, full = open_bank("ST", hd, j)
                    w = (TILES - j) * P
                    for c in range(2):
                        mm = nc.tensor.matmul(dst[:, 0:w], qkT[:, 2 + c, j * P:(j + 1) * P], qkT[:, c, j * P:SEQ],
                                              start=(c == 0), stop=(c == 1))
                    mm.then_inc(full, 1)
                odd("g", hd, "rg")
                copied(pe, "rv", hd, TILES - 1)
                copied(pe, "ST", hd, TILES - 1)
                for q in range(TILES):
                    dst, full = open_bank("inner", hd, q)
                    for j in range(q + 1):
                        mm = nc.tensor.matmul(dst, smT[:, ST_AT[j] + (q - j) * P:ST_AT[j] + (q - j + 1) * P], v1[:, j],
                                              start=(j == 0), stop=(j == q))
                    mm.then_inc(full, 1)
            tail(R_HEADS - 1)
            moe(1)

        @block.scalar
        def _(act):
            def bank(*name):
                b, _, full = banks.at(*name)
                act.wait_ge(bank_full[b], full)
                return psum[:, b], bank_free[b]

            def norm(n):
                for q in range(TILES):
                    if n == 0:
                        act.wait_ge(x_in[q], 16)
                    elif n == 1:
                        copied(act, "out0", 1, q)
                    elif n == 3:
                        copied(act, "out1", R_HEADS - 1, 1, q)
                    else:
                        act.wait_ge(h_ready, TILES * (n // 2 - 1) + q + 1)
                    if n or q:
                        act.wait_ge(squares, TILES * n + q)
                    nc.scalar.activation(junk, h[:, q], ACT.Square, accum_out=stat[:, q:q + 1]).then_inc(squares, 1)
                act.wait_ge(mean_sq, n + 1)
                nc.scalar.activation(stat[:, 8:12], stat[:, 4:8], ACT.Sqrt).then_inc(root, 1)

            def load_gain(n):
                act.dma_start(gain_row[:], gains_dram[n]).then_inc(gain_in, 16)

            def norm_copies(n):
                if n:
                    act.wait_ge(xs_ready, TILES * (n + 1))
                    load_gain(n + 1)
                if n % 2 == 0:
                    for j in range(KC):
                        src, _ = bank("norm", n, j)
                        nc.scalar.activation(uT_hi[:, j], src, ACT.Copy).then_inc(norm_hi, 1)
                else:
                    for j in range(1, KC, 2):
                        src, free = bank("norm", n, j)
                        nc.scalar.activation(uT[:, j], src, ACT.Copy).then_inc(free, 1)

            act.dma_start(square[:], c_square).then_inc(const_in, 16)
            load_gain(0)
            act.wait_ge(const_in, 16)
            for dst, src in ((tab_a[:], c_tab_a), (small[:], c_small), (slot_no[:], c_slot), (convw[:], conv_w),
                             (convp[:], conv_p), (wr[:], router_w), (br[:], router_b)):
                act.dma_start(dst, src).then_inc(const_in, 16)

            norm(0)
            split_hi(act, 0)
            norm_copies(0)
            split_hi(act, 1)
            for c in range(BC):
                src, free = bank("gate", c)
                nc.scalar.activation(sigT[:, c], src, ACT.Sigmoid).then_inc(free, 1)
            split_hi(act, 2)
            split_hi(act, 3)
            for c in range(4):
                src, free = bank("proj", "q", c)
                nc.scalar.activation(rawT[:, c], src, ACT.Copy).then_inc(free, 1)
            split_hi(act, 4)
            for c in range(4):
                src, free = bank("proj", "k", c)
                act.wait_ge(rot_cos, c + 1)
                bank("rot", "q", c)
                nc.scalar.activation(rawT[:, c], src, ACT.Copy).then_inc(free, 1)
            split_hi(act, 5)
            for q in range(TILES):
                src, free = bank("v", q)
                nc.scalar.activation(v0[:, q], src, ACT.Copy).then_inc(free, 1)

            def turned(q):
                src, _ = bank("aT", q)
                nc.scalar.activation(cat_hi[:, 0:4, q * P:(q + 1) * P], src.rearrange("p (c t) -> p c t", c=4),
                                     ACT.Copy).then_inc(aT_hi, 1)

            units = attention_units()
            for n in range(len(units) + 2):
                if n < len(units):
                    q, hd = units[n]
                    w = (q + 1) * P
                    act.wait_ge(mx_ok, n + 1)
                    if n >= 2:
                        b, _, full = banks.at("PT", units[n - 2])
                        act.wait_ge(bank_full[b], full)
                    if hd == 0 and q:
                        act.wait_ge(den_r, q)
                    nc.scalar.activation(prob[:, n % 2, 0:w], sm[:, n % 2, 0:w], ACT.Exp, bias=stat[:, 16 + n % 2:17 + n % 2],
                                         accum_out=stat[:, 24 + hd:25 + hd]).then_inc(p_ok, 1)
                if n >= 1 and n <= len(units):
                    q, hd = units[n - 1]
                    w = (q + 1) * P
                    src, free = bank("PT", (q, hd))
                    if n >= 3:
                        act.wait_ge(pv_done, n - 2)
                    nc.scalar.activation(probT[:, (n - 1) % 2, 0:w], src[:, 0:w], ACT.Copy).then_inc(free, 1)
                if n == CONV_AT + 2:
                    copied(act, "cmean")
                    for c in range(BC):
                        nc.scalar.activation(csq[:, c], conv[:, 4 + c], ACT.Square).then_inc(csq_ok, 1)
                if n == CONV_AT + 4:
                    src, free = bank("cvar")
                    act.wait_ge(eps_ok, 1)
                    nc.scalar.activation(crt, src, ACT.Sqrt, bias=stat[:, 40:41]).then_inc(free, 1)
                if n == CONV_AT + 6:
                    for c in range(BC):
                        act.wait_ge(cnorm, c + 1)
                        nc.scalar.activation(conv[:, 4 + c], conv[:, 4 + c], ACT.Silu, bias=convp[:, 2, c:c + 1],
                                             scale=convp[:, 1, c:c + 1]).then_inc(b_silu, 1)
                        act.wait_ge(b_silu, c + 1)
                        nc.scalar.activation(cat_hi[:, 4 + c], conv[:, 4 + c], ACT.Copy).then_inc(b_hi, 1)
                    load_gain(1)
                if n >= 4 and units[n - 2][1] == 2 and units[n - 2][0]:
                    turned(units[n - 2][0] - 1)
            turned(TILES - 1)
            split_hi(act, 6)

            def store_rows(layer):
                act.wait_ge(xs_ready, TILES * (2 * layer + 2))
                act.dma_start(xs_rows, xs[:, :].rearrange("p (q d) -> p q d", q=TILES)).then_inc(xs_stored, 16)

            def copy_tokens(m, n, b):
                act.wait_ge(m.xT_psum, n)
                for half in range(2):
                    ins = nc.scalar.activation(xeT_hi[:, 8 * b + 4 * half:8 * b + 4 * half + 4],
                                               psum[:, half].rearrange("p (c t) -> p c t", c=4), ACT.Copy)
                ins.then_inc(m.xT_hi, 1)

            def silu(m, n):
                act.wait_ge(m.gate_psum, n)
                nc.scalar.activation(silu_g, psum[:, 2], ACT.Silu).then_inc(m.silu_ok, 1)

            def copy_hidden(m, n):
                act.wait_ge(m.hidT_psum, n)
                nc.scalar.activation(hidT_hi, psum[:, 4].rearrange("p (c t) -> p c t", c=HC), ACT.Copy).then_inc(m.hidT_hi, 1)

            def copy_y(m, n, b):
                act.wait_ge(m.down_psum, n)
                act.wait_ge(m.y_free, n)
                nc.scalar.activation(y_e[:, b, 0:512], psum[:, 5], ACT.Copy).then_inc(m.y_act, 1)

            def moe(layer):
                m, past = main, EXPERTS * layer
                moe_split(act, layer, "gate", 0, 0, False)
                act.wait_ge(reduced, layer + 1)
                nc.scalar.activation(exps1, diff1, ACT.Exp).then_inc(exp_done, 1)
                act.wait_ge(second, layer + 1)
                nc.scalar.activation(exps2, diff2, ACT.Exp).then_inc(exp_done, 1)
                if not layer:
                    act.sem_inc(m.y_act, 1)
                copy_tokens(m, past + 1, 0)

                def body(e, s, turn):
                    last = type(e) is int and e == EXPERTS - 1
                    moe_split(act, layer, "up", s, turn, False)
                    if s:
                        copy_hidden(m, e + past)
                        act.wait_ge(m.hid_ok, e + past)
                    silu(m, e + (past + 1))
                    if s:
                        moe_split(act, layer, "down", s - 1, turn, False)
                    if last:
                        moe_split(act, layer, "down", EXPERTS - 1, 0, False)
                    else:
                        copy_tokens(m, e + (past + 2), (s + 1) % 2)
                        moe_split(act, layer, "gate", s + 1, turn, False)
                    if s:
                        copy_y(m, e + past, (s - 1) % 2)

                expert_steps(act, body)
                copy_hidden(m, past + EXPERTS)
                copy_y(m, past + EXPERTS, (EXPERTS - 1) % 2)
                act.wait_ge(index_ok, layer + 1)
                most = act.value_load(load[0:1, layer:layer + 1], min_val=0, max_val=SEQ)
                with act.If(most > P):
                    m = over[layer]
                    for c in range(1, SLOT_TILES):
                        with act.Fori(0, EXPERTS) as e:
                            n = e + (EXPERTS * (c - 1) + 1)
                            copy_tokens(m, n, 0)
                            act.wait_ge(over_landed[layer], 48 * n)
                            for b in range(4):
                                nc.scalar.activation(part(w_hi[b]), half_of(b // 2, b % 2, False), ACT.Copy).then_inc(m.hi, 1)
                            silu(m, n)
                            for b in range(2):
                                act.wait_ge(m.lo, 6 * n - 5 + b)
                                nc.scalar.activation(part(w_hi[b]), half_of(2, b, True), ACT.Copy).then_inc(m.hi, 1)
                            copy_hidden(m, n)
                            copy_y(m, n, 0)
                act.wait_ge(moe_done, layer + 1)
                for q in range(TILES):
                    for k in range(TOPK):
                        act.dma_start(y_back[k][:, q], y_rows[:, k, q]).then_inc(y_in[q], 16)

            norm(1)
            store_rows(0)
            norm_copies(1)
            moe(0)

            norm(2)
            split_hi(act, block_no[("odd", "qk", 0)])
            bank("norm", 2, KC - 1)
            act.dma_start(tab_r, c_tab_r).then_inc(tab_r_in, 16)
            norm_copies(2)

            def turned_y(hd):
                for q in range(TILES):
                    src, _ = bank("yT", hd, q)
                    nc.scalar.activation(yT_hi[:, :, q * P:(q + 1) * P], src.rearrange("p (c t) -> p c t", c=4),
                                         ACT.Copy).then_inc(yT_hi_ok, 1)

            for hd in range(R_HEADS):
                if hd:
                    split_hi(act, block_no[("odd", "wo", hd - 1)])
                    turned_y(hd - 1)
                split_hi(act, block_no[("odd", "v", hd)])
                split_hi(act, block_no[("odd", "g", hd)])
                for q in range(TILES):
                    src, free = bank("rv", hd, q)
                    nc.scalar.activation(v1[:, q], src, ACT.Copy).then_inc(free, 1)
                split_hi(act, block_no[("odd", "qk", hd + 1) if hd < R_HEADS - 1 else ("odd", "wo", hd)])
                for q in range(TILES):
                    src, free = bank("rg", hd, q)
                    nc.scalar.activation(sg[:, q], src, ACT.Silu).then_inc(free, 1)
                act.wait_ge(gaggr, TILES * (hd + 1))
                nc.scalar.activation(stat[:, 44:48], stat[:, 49:56:2], ACT.Sqrt, bias=stat[:, 40:41]).then_inc(groot, 1)
            turned_y(R_HEADS - 1)
            norm(3)
            store_rows(1)
            norm_copies(3)
            moe(1)
            norm(4)

        @block.vector
        def _(dve):
            V = nc.vector
            steps = [0]

            def link(ins):
                steps[0] += 1
                ins.then_inc(step, 1)
                dve.wait_ge(step, steps[0])

            def bank(*name):
                b, _, full = banks.at(*name)
                dve.wait_ge(bank_full[b], full)
                return psum[:, b], bank_free[b]

            def root_mean(n):
                dve.wait_ge(squares, TILES * (n + 1))
                V.tensor_scalar(stat[:, 4:8], stat[:, 0:4], 1.0 / DM, EPS, ALU.mult, ALU.add).then_inc(mean_sq, 1)
                dve.wait_ge(root, n + 1)
                V.reciprocal(stat[:, 12:16], stat[:, 8:12]).then_inc(rstd_ok, 1)
                dve.wait_ge(rstd_ok, n + 1)

            def norm(n):
                root_mean(n)
                dve.wait_ge(gain_in, 16 * (n + 1))
                for q in range(TILES):
                    V.scalar_tensor_tensor(out=xs[:, q * DM:(q + 1) * DM], in0=h[:, q], scalar=stat[:, 12 + q:13 + q],
                                           in1=gain_row[:], op0=ALU.mult, op1=ALU.mult).then_inc(xs_ready, 1)

            def norm_copies(n):
                if n % 2 == 0:
                    for j in range(KC):
                        src, free = bank("norm", n, j)
                        dve.wait_ge(norm_hi, KC * (n // 2) + j + 1)
                        V.tensor_tensor(uT_lo[:, j], src, uT_hi[:, j].bitcast(F32), ALU.subtract).then_inc(free, 1)
                else:
                    for j in range(0, KC, 2):
                        src, free = bank("norm", n, j)
                        V.tensor_copy(uT[:, j], src).then_inc(free, 1)

            V.memset(stat[:, 40:41], EPS).then_inc(eps_ok, 1)
            norm(0)
            split_lo(dve, 0, 0)
            split_lo(dve, 0, 1)
            norm_copies(0)
            V.memset(conv_in[:, :, 0:PAD], 0.0).then_inc(eps_ok, 1)
            dve.wait_ge(eps_ok, 2)
            split_lo(dve, 1, 0)
            split_lo(dve, 1, 1)
            split_lo(dve, 2, 0)
            split_lo(dve, 2, 1)
            dve.wait_ge(const_in, 16 * N_CONST)
            for c in range(BC):
                copied(dve, "gate", c)
                src, free = bank("val", c)
                V.tensor_tensor(conv_in[:, c, PAD:], src, sigT[:, c], ALU.mult).then_inc(free, 1)
            copied(dve, "val", BC - 1)

            def taps(first, last):
                for i in range(first, last):
                    k, c = i // 3, i % 3
                    if k:
                        dve.wait_ge(tap, i - 2)
                        V.scalar_tensor_tensor(out=conv[:, 4 + c], in0=conv_in[:, c, k:k + SEQ], scalar=convw[:, c, k:k + 1],
                                               in1=conv[:, 4 + c], op0=ALU.mult, op1=ALU.add).then_inc(tap, 1)
                    else:
                        V.tensor_scalar(conv[:, 4 + c], conv_in[:, c, k:k + SEQ], convw[:, c, k:k + 1], convp[:, 0, c:c + 1],
                                        ALU.mult, ALU.add).then_inc(tap, 1)

            def rotate(which):
                for c in range(4):
                    n = ROPE_CHUNKS.index((which, c))
                    src, free = bank("rot", which, c)
                    if n >= 2:
                        dve.wait_ge(rot_done, n - 1)
                    V.tensor_tensor(sm[:, n % 2], src, sin_a, ALU.mult).then_inc(free, 1)
                    copied(dve, "rot", which, c)
                    dve.wait_ge(rot_cos, n + 1)
                    t = (qT if which == "q" else kT)[:, c]
                    V.tensor_tensor(t, t, sm[:, n % 2], ALU.add).then_inc(rot_done, 1)

            taps(0, 12)
            split_lo(dve, 3, 0)
            taps(12, 24)
            split_lo(dve, 3, 1)
            taps(24, 33)
            split_lo(dve, 4, 0)
            taps(33, 45)
            split_lo(dve, 4, 1)
            rotate("q")
            split_lo(dve, 5, 0)
            taps(45, 66)
            rotate("k")
            taps(66, 3 * TAPS)
            split_lo(dve, 5, 1)
            dve.wait_ge(rot_done, 8)

            units = attention_units()
            def turned(q):
                src, free = bank("aT", q)
                dve.wait_ge(aT_hi, q + 1)
                t = slice(q * P, (q + 1) * P)
                V.tensor_tensor(cat_lo[:, 0:4, t], src.rearrange("p (c t) -> p c t", c=4), cat_hi[:, 0:4, t].bitcast(F32),
                                ALU.subtract).then_inc(free, 1)

            for n in range(len(units) + 3):
                if n < len(units):
                    q, hd = units[n]
                    w = (q + 1) * P
                    src, free = bank("S", (q, hd))
                    if n >= 2:
                        dve.wait_ge(p_ok, n - 1)
                    V.scalar_tensor_tensor(out=sm[:, n % 2, 0:w], in0=src[:, 0:w], scalar=A_DIM ** -0.5,
                                           in1=bias_a[:, SEQ - w:SEQ], op0=ALU.mult, op1=ALU.add).then_inc(free, 1)
                    copied(dve, "S", (q, hd))
                    V.tensor_reduce(stat[:, 16 + n % 2:17 + n % 2], sm[:, n % 2, 0:w], AX.X, ALU.max, negate=True) \
                        .then_inc(mx_ok, 1)
                if n % A_HEADS == 0 and n:
                    dve.wait_ge(p_ok, n)
                    if n > A_HEADS:
                        copied(dve, "O", n // A_HEADS - 2)
                    V.reciprocal(stat[:, 32:40], stat[:, 24:32]).then_inc(den_r, 1)
                    dve.wait_ge(den_r, n // A_HEADS)
                if n >= 3 and (n - 3) % A_HEADS == A_HEADS - 1:
                    q = (n - 3) // A_HEADS
                    b, _, _ = banks.at("O", q)
                    dve.wait_ge(pv_done, n - 2)
                    V.tensor_tensor(a_out[:, q].rearrange("p (h d) -> p h d", h=A_HEADS),
                                    psum[:, b].rearrange("p (h d) -> p h d", h=A_HEADS),
                                    stat[:, 32:40].unsqueeze(2).broadcast_to([P, A_HEADS, A_DIM]), ALU.mult) \
                        .then_inc(bank_free[b], 1)
                if n == CONV_AT + 1:
                    src, free = bank("cmean")
                    for c in range(BC):
                        ins = V.tensor_tensor(conv[:, 4 + c], conv[:, 4 + c], src, ALU.subtract)
                    ins.then_inc(free, 1)
                if n == CONV_AT + 5:
                    copied(dve, "cvar")
                    V.reciprocal(crs, crt).then_inc(crs_ok, 1)
                    dve.wait_ge(crs_ok, 1)
                    for c in range(BC):
                        V.tensor_tensor(conv[:, 4 + c], conv[:, 4 + c], crs, ALU.mult).then_inc(cnorm, 1)
                if n == CONV_AT + 8:
                    for c in range(BC):
                        dve.wait_ge(b_hi, c + 1)
                        V.tensor_tensor(cat_lo[:, 4 + c], conv[:, 4 + c], cat_hi[:, 4 + c].bitcast(F32), ALU.subtract) \
                            .then_inc(b_ok, 1)
                if n >= 5 and n - 3 < len(units) and units[n - 3][1] == 2 and units[n - 3][0]:
                    turned(units[n - 3][0] - 1)
            turned(TILES - 1)
            split_lo(dve, 6, 0)
            split_lo(dve, 6, 1)
            for half in range(2):
                for q in range(TILES):
                    src, free = bank("out0", half, q)
                    dst = h[:, q, half * 512:(half + 1) * 512]
                    V.tensor_tensor(dst, dst, src, ALU.add).then_inc(free, 1)

            def first_best(values, width, top, rank, out):
                c = cand[:, 0:TILES * width].rearrange("p (q n) -> p q n", q=TILES)
                wide = [P, TILES, width]
                link(V.tensor_reduce(top, values, AX.X, ALU.max))
                link(V.tensor_tensor(c, values, top.unsqueeze(2).broadcast_to(wide), ALU.is_equal))
                link(V.tensor_tensor(c, c, rank.unsqueeze(1).broadcast_to(wide), ALU.mult))
                link(V.tensor_reduce(pick, c, AX.X, ALU.max))
                link(V.tensor_tensor(out, c, pick.unsqueeze(2).broadcast_to(wide), ALU.is_equal))

            def route(layer):
                src, free = bank("logits", layer)
                V.tensor_tensor(logit, src[:, 0:TILES * NROUT].rearrange("p (q n) -> p q n", q=TILES),
                                br[:, layer].unsqueeze(1).broadcast_to([P, TILES, NROUT]), ALU.add).then_inc(free, 1)
                copied(dve, "logits", layer)
                group = logit[:, :, 0:GROUPS]
                first_best(group, GROUPS, best, small[:, 0:4], of_group)
                V.tensor_tensor(diff1.rearrange("p (q g) -> p q g", q=TILES), group,
                                best.unsqueeze(2).broadcast_to([P, TILES, GROUPS]), ALU.subtract).then_inc(reduced, 1)
                for q in range(TILES):
                    link(V.tensor_tensor(prod[:, 0:EXPERTS].rearrange("p (g e) -> p g e", g=GROUPS),
                                         logit[:, q, GROUPS:].rearrange("p (g e) -> p g e", g=GROUPS),
                                         of_group[:, q].unsqueeze(2).broadcast_to([P, GROUPS, PER_GROUP]), ALU.mult))
                    link(V.tensor_reduce(sel[:, q], prod[:, 0:EXPERTS].rearrange("p (g e) -> p e g", g=GROUPS), AX.X, ALU.add))
                first_best(sel, PER_GROUP, best, small[:, 4:12], fine[0])
                link(V.scalar_tensor_tensor(out=sel2, in0=fine[0], scalar=NEG, in1=sel, op0=ALU.mult, op1=ALU.add))
                first_best(sel2, PER_GROUP, best2, small[:, 4:12], fine[1])
                V.tensor_tensor(diff2, best2, best, ALU.subtract).then_inc(second, 1)
                for k in range(TOPK):
                    for q in range(TILES):
                        ins = V.tensor_tensor(chosen_k[k][:, q].rearrange("p (g e) -> p g e", g=GROUPS),
                                              of_group[:, q].unsqueeze(2).broadcast_to([P, GROUPS, PER_GROUP]),
                                              fine[k][:, q].unsqueeze(1).broadcast_to([P, GROUPS, PER_GROUP]), ALU.mult)
                link(ins)
                V.tensor_tensor(both, chosen_k[0], chosen_k[1], ALU.add).then_inc(chosen, 1)
                dve.wait_ge(exp_done, 2 * layer + 2)
                link(V.tensor_reduce(gp, exps1.rearrange("p (q g) -> p q g", q=TILES), AX.X, ALU.add))
                link(V.tensor_scalar(pick, exps2, 1.0, None, ALU.add))
                link(V.tensor_tensor(pick, pick, gp, ALU.mult))
                link(V.reciprocal(gate[:, 0], pick))
                link(V.tensor_tensor(gate[:, 1], gate[:, 0], exps2, ALU.mult))
                for k in range(TOPK):
                    ins = V.tensor_tensor(rows[:, k * TILES:(k + 1) * TILES], chosen_k[k],
                                          small[:, 12 + k * TILES:12 + (k + 1) * TILES].unsqueeze(2)
                                          .broadcast_to([P, TILES, EXPERTS]), ALU.mult)
                src, free = bank("pos", layer)
                V.tensor_reduce(most_f, src[:, TILES * EXPERTS:(TILES + 1) * EXPERTS], AX.X, ALU.max)
                V.tensor_copy(pos, src[:, 0:TILES * EXPERTS].rearrange("p (q n) -> p q n", q=TILES)).then_inc(free, 1)
                copied(dve, "pos", layer)
                V.tensor_copy(load[:, layer:layer + 1], most_f)
                for k in range(TOPK):
                    link(V.tensor_tensor(prod.rearrange("p (q n) -> p q n", q=TILES), pos, chosen_k[k], ALU.mult))
                    link(V.tensor_reduce(rank[:, k * TILES:(k + 1) * TILES], prod.rearrange("p (q n) -> p q n", q=TILES),
                                         AX.X, ALU.add))
                for k in range(TOPK * TILES):
                    ins = V.tensor_scalar(oh[:, k], slot_no[:], rank[:, k:k + 1], None, ALU.is_equal)
                ins.then_inc(placed, 1)
                src, free = bank("table", layer)
                V.tensor_copy(pos.rearrange("p q n -> p (q n)"), src[:, 0:SLOT_TILES * EXPERTS]).then_inc(free, 1)
                copied(dve, "table", layer)
                table = pos.rearrange("p q n -> p (q n)")
                link(V.tensor_scalar(prod, table, 0.0, EMPTY, ALU.is_equal, ALU.mult))
                link(V.scalar_tensor_tensor(out=table, in0=table, scalar=-1.0, in1=prod, op0=ALU.add, op1=ALU.add))
                link(V.tensor_scalar(prod, table, float(SEQ), -float(SEQ), ALU.is_ge, ALU.mult))
                both_at = index[:, :, :, :].rearrange("p c e k -> p (c e) k")
                link(V.tensor_copy(both_at[:, :, 1], table))
                V.tensor_tensor(both_at[:, :, 0], table, prod, ALU.add).then_inc(index_ok, 1)

            def copy_tokens(m, n, b):
                dve.wait_ge(m.xT_hi, n)
                for half in range(2):
                    c = slice(8 * b + 4 * half, 8 * b + 4 * half + 4)
                    ins = V.tensor_tensor(xeT_lo[:, c], psum[:, half].rearrange("p (c t) -> p c t", c=4),
                                          xeT_hi[:, c].bitcast(F32), ALU.subtract)
                ins.then_inc(m.xT_ok, 1)

            def copy_hidden(m, n):
                dve.wait_ge(m.hidT_hi, n)
                V.tensor_tensor(hidT_lo, psum[:, 4].rearrange("p (c t) -> p c t", c=HC), hidT_hi.bitcast(F32),
                                ALU.subtract).then_inc(m.hidT_ok, 1)

            def hidden(m, n):
                dve.wait_ge(m.up_psum, n)
                dve.wait_ge(m.silu_ok, n)
                V.tensor_tensor(hid, silu_g, psum[:, 3], ALU.mult).then_inc(m.hid_ok, 1)

            def copy_y(m, n, b):
                dve.wait_ge(m.down_psum, n)
                dve.wait_ge(m.y_free, n)
                V.tensor_copy(y_e[:, b, 512:1024], psum[:, 6]).then_inc(m.y_dve, 1)

            def moe(layer):
                m, past = main, EXPERTS * layer
                norm(2 * layer + 1)
                norm_copies(2 * layer + 1)
                moe_split(dve, layer, "gate", 0, 0, True)
                route(layer)
                if not layer:
                    dve.sem_inc(m.y_dve, 1)
                copy_tokens(m, past + 1, 0)

                def body(e, s, turn):
                    last = type(e) is int and e == EXPERTS - 1
                    moe_split(dve, layer, "up", s, turn, True)
                    if s:
                        copy_hidden(m, e + past)
                        moe_split(dve, layer, "down", s - 1, turn, True)
                    hidden(m, e + (past + 1))
                    if last:
                        moe_split(dve, layer, "down", EXPERTS - 1, 0, True)
                    else:
                        copy_tokens(m, e + (past + 2), (s + 1) % 2)
                        moe_split(dve, layer, "gate", s + 1, turn, True)
                    if s:
                        copy_y(m, e + past, (s - 1) % 2)

                expert_steps(dve, body)
                copy_hidden(m, past + EXPERTS)
                copy_y(m, past + EXPERTS, (EXPERTS - 1) % 2)
                most = dve.value_load(load[0:1, layer:layer + 1], min_val=0, max_val=SEQ)
                with dve.If(most > P):
                    m = over[layer]
                    for c in range(1, SLOT_TILES):
                        with dve.Fori(0, EXPERTS) as e:
                            n = e + (EXPERTS * (c - 1) + 1)
                            copy_tokens(m, n, 0)
                            for b in range(4):
                                dve.wait_ge(m.hi, 6 * n - 5 + b)
                                V.tensor_tensor(part(w_lo[b]), half_of(b // 2, b % 2, False), part(w_hi[b]).bitcast(F32),
                                                ALU.subtract).then_inc(m.lo, 1)
                            hidden(m, n)
                            for b in range(2):
                                dve.wait_ge(m.hi, 6 * n - 1 + b)
                                V.tensor_tensor(part(w_lo[b]), half_of(2, b, True), part(w_hi[b]).bitcast(F32),
                                                ALU.subtract).then_inc(m.lo, 1)
                            copy_hidden(m, n)
                            copy_y(m, n, 0)
                for q in range(TILES):
                    dve.wait_ge(y_in[q], 32 * (layer + 1))
                    link(V.scalar_tensor_tensor(out=h[:, q], in0=y_back[0][:, q], scalar=gate[:, 0, q:q + 1],
                                                in1=h[:, q], op0=ALU.mult, op1=ALU.add))
                    V.scalar_tensor_tensor(out=h[:, q], in0=y_back[1][:, q], scalar=gate[:, 1, q:q + 1],
                                           in1=h[:, q], op0=ALU.mult, op1=ALU.add).then_inc(h_ready, 1)

            moe(0)

            norm(2)
            for half in range(2):
                split_lo(dve, block_no[("odd", "qk", 0)], half)
            norm_copies(2)
            dve.wait_ge(tab_r_in, 16)
            cos_r, sin_r = tab_r[:, 0], tab_r[:, 1]

            def lo(kind, hd, half):
                split_lo(dve, block_no[("odd", kind, hd)], half)

            def turned_y(hd):
                for q in range(TILES):
                    src, free = bank("yT", hd, q)
                    dve.wait_ge(yT_hi_ok, hd * TILES + q + 1)
                    t = slice(q * P, (q + 1) * P)
                    V.tensor_tensor(yT_lo[:, :, t], src.rearrange("p (c t) -> p c t", c=4), yT_hi[:, :, t].bitcast(F32),
                                    ALU.subtract).then_inc(free, 1)

            def residual(hd, half):
                for q in range(TILES):
                    src, free = bank("out1", hd, half, q)
                    dst = h[:, q, half * 512:(half + 1) * 512]
                    V.tensor_tensor(dst, dst, src, ALU.add).then_inc(free, 1)

            for hd in range(R_HEADS):
                if hd:
                    lo("wo", hd - 1, 0)
                    lo("wo", hd - 1, 1)
                for a in (0, 2):
                    x1, free1 = bank("qk", hd, a)
                    x2, free2 = bank("qk", hd, a + 1)
                    if hd and not a:
                        dve.wait_ge(y_ok, TILES * hd)
                    if hd or a:
                        dve.wait_ge(radd, 4 * hd + a)
                    V.tensor_tensor(rot_tmp[:, 0], x1, cos_r, ALU.mult)
                    V.tensor_tensor(rot_tmp[:, 1], x2, sin_r, ALU.mult)
                    V.tensor_tensor(qkT[:, a + 1], x2, cos_r, ALU.mult).then_inc(free2, 1)
                    V.tensor_tensor(gn, x1, sin_r, ALU.mult).then_inc(free1, 1)
                    copied(dve, "qk", hd, a)
                    copied(dve, "qk", hd, a + 1)
                    V.tensor_tensor(qkT[:, a], rot_tmp[:, 0], rot_tmp[:, 1], ALU.subtract).then_inc(radd, 1)
                    V.tensor_tensor(qkT[:, a + 1], qkT[:, a + 1], gn, ALU.add).then_inc(radd, 1)
                if hd:
                    turned_y(hd - 1)
                    lo("v", hd, 0)
                    residual(hd - 1, 0)
                    lo("v", hd, 1)
                    residual(hd - 1, 1)
                else:
                    lo("v", hd, 0)
                    lo("v", hd, 1)
                lo("g", hd, 0)
                lo("g", hd, 1)
                for j in range(TILES):
                    src, free = bank("ST", hd, j)
                    w = (TILES - j) * P
                    V.tensor_tensor(smT[:, ST_AT[j]:ST_AT[j] + w], src[:, 0:w], tab_r[:, 2 + hd, 0:w], ALU.mult).then_inc(free, 1)
                ahead = ("qk", hd + 1) if hd < R_HEADS - 1 else ("wo", hd)
                lo(*ahead, 0)
                lo(*ahead, 1)
                dve.wait_ge(radd, 4 * (hd + 1))
                if hd:
                    dve.wait_ge(y_ok, TILES * hd)
                for q in range(TILES):
                    src, _ = bank("inner", hd, q)
                    V.bn_stats(stat[:, 64 + 6 * q:70 + 6 * q], src).then_inc(gstat, 1)
                    dve.wait_ge(gstat, hd * TILES + q + 1)
                    V.bn_aggr(stat[:, 48 + 2 * q:50 + 2 * q], stat[:, 64 + 6 * q:70 + 6 * q]).then_inc(gaggr, 1)
                dve.wait_ge(groot, hd + 1)
                V.reciprocal(stat[:, 56:60], stat[:, 44:48]).then_inc(grec, 1)
                dve.wait_ge(grec, hd + 1)
                for q in range(TILES):
                    src, free = bank("inner", hd, q)
                    if q >= 2:
                        dve.wait_ge(y_ok, hd * TILES + q - 1)
                    V.tensor_scalar(rot_tmp[:, q % 2], src, stat[:, 48 + 2 * q:49 + 2 * q], stat[:, 56 + q:57 + q],
                                    ALU.subtract, ALU.mult).then_inc(free, 1)
                    copied(dve, "inner", hd, q)
                    copied(dve, "rg", hd, q)
                    V.tensor_tensor(sg[:, q], sg[:, q], rot_tmp[:, q % 2], ALU.mult).then_inc(y_ok, 1)
            turned_y(R_HEADS - 1)
            residual(R_HEADS - 1, 0)
            residual(R_HEADS - 1, 1)
            moe(1)
            norm(4)

        @block.gpsimd
        def _(pool):
            G = nc.gpsimd
            pool.wait_ge(const_in, 16 * N_CONST)

            def taps(first, last):
                c = BC - 1
                for k in range(first, last):
                    if not k:
                        G.tensor_scalar(conv[:, 4 + c], conv_in[:, c, 0:SEQ], convw[:, c, 0:1], convp[:, 0, c:c + 1],
                                        ALU.mult, ALU.add).then_inc(tap_pool, 1)
                        continue
                    if k >= 3:
                        pool.wait_ge(tap_pool, k - 1)
                    G.tensor_scalar(tap_in[:, k % 2], conv_in[:, c, k:k + SEQ], convw[:, c, k:k + 1], None, ALU.mult) \
                        .then_inc(tap_mul, 1)
                    pool.wait_ge(tap_mul, k)
                    pool.wait_ge(tap_pool, k)
                    G.tensor_tensor(conv[:, 4 + c], conv[:, 4 + c], tap_in[:, k % 2], ALU.add).then_inc(tap_pool, 1)

            def cosines(which):
                for c in range(4):
                    copied(pool, "proj", which, c)
                    if which == "q":
                        copied(pool, "val", c)
                    G.tensor_tensor((qT if which == "q" else kT)[:, c], rawT[:, c], cos_a, ALU.mult).then_inc(rot_cos, 1)

            copied(pool, "val", BC - 1)
            taps(0, 9)
            cosines("q")
            taps(9, 16)
            cosines("k")
            taps(16, TAPS)

            def gather(m, c, e, b, n):
                src = index[:, c, e, 0:1] if type(e) is int else index[:, c, bass.ds(e, 1), 0]
                G.tensor_copy(gather_at[:, b:b + 1], src).then_inc(m.indexed[b], 1)
                pool.wait_ge(m.indexed[b], n)
                pool.sem_inc(lists_read, 1)
                G.indirect_dma_start(x_e[:, b], None, xs_dram, bass.IndirectOffsetOnAxis(ap=gather_at[:, b:b + 1], axis=0),
                                     bounds_check=SEQ - 1, oob_is_err=False).then_inc(m.gathered[b], 16)

            def scatter(m, c, e, b, n, count):
                src = index[:, c, e, 1:2] if type(e) is int else index[:, c, bass.ds(e, 1), 1]
                G.tensor_copy(scatter_at[:, 0:1], src).then_inc(m.sc_indexed, 1)
                pool.wait_ge(m.sc_indexed, n)
                pool.sem_inc(lists_read, 1)
                G.indirect_dma_start(y_dram, bass.IndirectOffsetOnAxis(ap=scatter_at[:, 0:1], axis=0), y_e[:, b], None,
                                     bounds_check=TOPK * SEQ - 1, oob_is_err=False).then_inc(m.scattered[b], 16)
                pool.wait_ge(m.scattered[b], 16 * count)
                pool.sem_inc(m.y_free, 1)

            def number(v):
                return v if type(v) is int else pool.snap(v)

            for layer in range(DEPTH):
                m, past = main, EXPERTS * layer
                if not layer:
                    pool.sem_inc(m.y_free, 2)
                pool.wait_ge(index_ok, layer + 1)
                pool.wait_ge(xs_stored, 16 * (layer + 1))
                gather(m, 0, 0, 0, past // 2 + 1)
                gather(m, 0, 1, 1, past // 2 + 1)

                def body(e, s, turn):
                    if type(e) is not int or e < EXPERTS - 2:
                        ahead, count = number(e + 2), number(turn + (past // 2 + s // 2 + 2))
                        pool.wait_ge(m.xT_psum, e + (past + 1))
                        gather(m, 0, ahead, s % 2, count)
                    if s:
                        store(e - 1, s - 1, turn)

                def store(e, s, turn):
                    e, count = number(e), number(turn + (past // 2 + s // 2 + 1))
                    pool.wait_ge(m.y_act, e + (past + 2))
                    pool.wait_ge(m.y_dve, e + (past + 2))
                    scatter(m, 0, e, s % 2, e + (past + 1), count)

                expert_steps(pool, body)
                store(EXPERTS - 1, 3, TURNS)

                most = pool.value_load(load[0:1, layer:layer + 1], min_val=0, max_val=SEQ)
                with pool.If(most > P):
                    m = over[layer]
                    pool.sem_inc(m.y_free, 1)
                    for c in range(1, SLOT_TILES):
                        with pool.Fori(0, EXPERTS) as e:
                            n = e + (EXPERTS * (c - 1) + 1)
                            pool.sem_inc(m.go, 1)
                            gather(m, c, e, 0, n)
                            pool.wait_ge(m.y_act, n)
                            pool.wait_ge(m.y_dve, n)
                            scatter(m, c, e, 0, n, n)
                pool.sem_inc(moe_done, 1)


def kernel(**inputs):
    import concourse.bacc as bacc
    from concourse.bass_utils import run_bass_kernel_spmd

    a = {k: np.asarray(v) for k, v in inputs.items()}
    arrays = {k: np.ascontiguousarray(a[k]) for k in
              ("x", "even_w_in", "even_w_out", "odd_w_in", "odd_w_out", "expert_w_gate", "expert_w_up", "expert_w_down")}
    rows = [a["mix_norm"][0], a["ffn_norm"][0], a["mix_norm"][1], a["ffn_norm"][1], a["final_norm"]]
    arrays["gains"] = np.ascontiguousarray(np.broadcast_to(np.stack(rows)[:, None], (5, P, DM)))
    arrays["conv_w"] = np.ascontiguousarray(a["conv_w"][0].reshape(TAPS, BC, P).transpose(2, 1, 0))
    arrays["conv_p"] = np.ascontiguousarray(
        np.stack([a[k][0].reshape(BC, P) for k in ("conv_b", "conv_norm_g", "conv_norm_b")]).transpose(2, 0, 1))
    router = np.concatenate([a["router_w1"], a["router_w2"]], 2)
    arrays["router_w"] = np.ascontiguousarray(router.reshape(DEPTH, P, KC, NROUT).transpose(1, 0, 2, 3))
    arrays["router_b"] = np.ascontiguousarray(
        np.broadcast_to(np.concatenate([a["router_b1"], a["router_b2"]], 1), (P, DEPTH, NROUT)))
    arrays.update(shape_constants())
    arrays = {f"in_{k}": v for k, v in arrays.items()}

    nc = bacc.Bacc("TRN2", target_bir_lowering=False, num_devices=1, dynamic_dma_scratch_size=4096)
    aps = {k[3:]: nc.dram_tensor(k, v.shape, mybir.dt.from_np(v.dtype), kind="ExternalInput").ap() for k, v in arrays.items()}
    out = nc.dram_tensor("out", (1, SEQ, DM), F32, kind="ExternalOutput").ap()
    trunk_kernel(nc, out=out, **aps)
    r = run_bass_kernel_spmd(nc, [arrays], core_ids=[0])
    return r.results[0]["out"]
```

```python
from contextlib import ExitStack

import numpy as np

import concourse.bass as bass
from concourse import mybir

F32 = mybir.dt.float32
F32R = mybir.dt.float32r
U32 = mybir.dt.uint32
ALU = mybir.AluOpType
ACT = mybir.ActivationFunctionType
AX = mybir.AxisListType

P = 128
SEQ, DM, DEPTH = 512, 1024, 2
TILES = SEQ // P
KC = DM // P
EPS = 1e-6
NEG = -1e30
A_HEADS, A_DIM = 8, 64
A_WIDTH = A_HEADS * A_DIM
BRANCHES = ((128, 1), (512, 4), (2048, 16))
ROPE_THETA, ROPE_DIM = 500000.0, 16
B_WIDTH = DM - A_WIDTH
BC = B_WIDTH // P
TAPS = 31
PAD = TAPS - 1
R_HEADS, R_QK, R_V = 4, 256, 512
R_QKW, R_VW = R_HEADS * R_QK, R_HEADS * R_V
RET_THETA = 10000.0
GROUPS, PER_GROUP = 4, 8
EXPERTS = GROUPS * PER_GROUP
HID = 512
HC = HID // P
TOPK = 2
NROUT = GROUPS + EXPERTS
N_CONST = 8
CONV_AT = 21
ST_AT = [0, 4 * P, 7 * P, 9 * P]
SLOTS = 3
BLOCK = 4096
HALF = BLOCK // 2
FIRST = 96
SLOT_AT = [0] + list(range(FIRST, SEQ - P, P)) + [SEQ - P]
SLOT_TILES = len(SLOT_AT)
ARENA = 55168
EMPTY = 4096.0


def shape_constants():
    p = np.arange(P)
    ident = np.eye(P, dtype=np.float32)
    ones = np.ones((P, P), np.float32)
    before = (p[:, None] < p[None, :]).astype(np.float32)
    mean = np.full((P, P), 1.0 / B_WIDTH, np.float32)
    half = ROPE_DIM // 2
    swap = np.zeros((P, P), np.float32)
    for h in range(P // A_DIM):
        for i in range(half):
            swap[h * A_DIM + half + i, h * A_DIM + i] = -1.0
            swap[h * A_DIM + i, h * A_DIM + half + i] = 1.0
    square = np.stack([ident, ones, before, mean, swap], 1)

    inv = (np.float32(ROPE_THETA) ** (-np.arange(0, ROPE_DIM, 2, dtype=np.float32) / ROPE_DIM)).astype(np.float32)
    ang = (np.arange(SEQ, dtype=np.float32)[:, None] * inv[None]).astype(np.float32)
    cos_a, sin_a = np.ones((P, SEQ), np.float32), np.zeros((P, SEQ), np.float32)
    for h in range(P // A_DIM):
        for i in range(ROPE_DIM):
            cos_a[h * A_DIM + i] = np.cos(ang[:, i % half])
            sin_a[h * A_DIM + i] = np.sin(ang[:, i % half])
    bias = np.empty((P, SEQ), np.float32)
    for b in range(TILES):
        dist = P * (TILES - 1 - b) + p[:, None] - p[None, :]
        count = sum(((dist >= 0) & (dist % dil == 0) & (dist <= win)).astype(np.int64) for win, dil in BRANCHES)
        bias[:, b * P:(b + 1) * P] = np.where(count > 0, np.log(np.maximum(count, 1)), NEG)
    tab_a = np.stack([cos_a, sin_a, bias], 1)

    inv = (np.float32(RET_THETA) ** (-np.linspace(0.0, 1.0, R_QK // 2, dtype=np.float32))).astype(np.float32)
    ang = (inv[:, None] * np.arange(SEQ, dtype=np.float32)[None]).astype(np.float32)
    decay = np.empty((P, R_HEADS, SEQ), np.float32)
    for h in range(R_HEADS):
        log_decay = np.log(1.0 - 2.0 ** (-5.0 - h))
        for d in range(TILES):
            diff = P * d + p[None, :] - p[:, None]
            decay[:, h, d * P:(d + 1) * P] = np.where(diff >= 0, np.exp(log_decay * np.maximum(diff, 0)), 0.0) * R_QK ** -0.5
    tab_r = np.concatenate([np.cos(ang)[:, None], np.sin(ang)[:, None], decay], 1).astype(np.float32)

    slot = np.broadcast_to(np.arange(SEQ, dtype=np.float32), (P, SEQ)).copy()
    small = np.zeros((P, 32), np.float32)
    small[:, 0:4] = np.arange(GROUPS, 0, -1)
    small[:, 4:12] = np.arange(PER_GROUP, 0, -1)
    for k in range(TOPK):
        for q in range(TILES):
            small[:, 12 + k * TILES + q] = k * SEQ + q * P + p + 1
    return {"c_square": square, "c_tab_a": tab_a, "c_tab_r": tab_r, "c_slot": slot, "c_small": small}


class Banks:

    def __init__(self):
        self.uses = [0] * 8
        self.fulls = [0] * 8
        self.jobs = {}
        self.turn = 0

    def plan(self, name, bank=None):
        if bank is None:
            bank, self.turn = self.turn, (self.turn + 1) % 8
        self.fulls[bank] += name[0] != "O"
        self.jobs[name] = (bank, self.uses[bank], self.fulls[bank])
        self.uses[bank] += 1

    def at(self, *name):
        return self.jobs[name]


def plan_banks():
    b = Banks()

    def norm(n):
        for j in range(KC):
            b.plan(("norm", n, j))

    norm(0)
    for c in range(BC):
        b.plan(("gate", c))
    for c in range(BC):
        b.plan(("val", c))
    for which, c in ROPE_CHUNKS[:4]:
        b.plan(("proj", which, c))
    for which, c in ROPE_CHUNKS[4:]:
        b.plan(("proj", which, c))
    for which, c in ROPE_CHUNKS[:4]:
        b.plan(("rot", which, c))
    for q in range(TILES):
        b.plan(("v", q))
    for which, c in ROPE_CHUNKS[4:]:
        b.plan(("rot", which, c))
    units = attention_units()
    for n in range(len(units) + 2):
        if n < len(units):
            b.plan(("S", units[n]), n % 3)
        if n == CONV_AT:
            b.plan(("cmean",), 7)
        if n == CONV_AT + 3:
            b.plan(("cvar",), 7)
        if 1 <= n <= len(units):
            b.plan(("PT", units[n - 1]), 3 + (n - 1) % 2)
        if n >= 2:
            q, h = units[n - 2]
            if h == 0:
                b.plan(("O", q), 5 + q % 2)
        if n >= 4:
            q, h = units[min(n - 2, len(units) - 1)]
            if h == 2 and q > 0:
                b.plan(("aT", q - 1), 7)
    b.plan(("aT", TILES - 1), 7)
    b.turn = 0
    for half in range(2):
        for q in range(TILES):
            b.plan(("out0", half, q))
    norm(1)
    b.plan(("logitsT", 0))
    b.plan(("logits", 0))
    b.plan(("pos", 0))
    b.plan(("table", 0))
    b.before_experts = [list(b.uses)]
    norm(2)
    for kind, h, i in retention_order():
        b.plan((kind, h) + (i if type(i) is tuple else (i,)))
    norm(3)
    b.plan(("logitsT", 1))
    b.plan(("logits", 1))
    b.plan(("pos", 1))
    b.plan(("table", 1))
    b.before_experts.append(list(b.uses))
    return b


ROPE_CHUNKS = [(which, c) for which in "qk" for c in range(A_WIDTH // P)]


def attention_units():
    return [(q, h) for q in range(TILES) for h in range(A_HEADS)]


def retention_order():
    order = []

    def tail(h):
        for q in range(TILES):
            order.append(("yT", h, q))
        for half in range(2):
            for q in range(TILES):
                order.append(("out1", h, (half, q)))

    for h in range(R_HEADS):
        order += [("qk", h, i) for i in range(4)]
        order += [("rv", h, q) for q in range(TILES)]
        if h:
            tail(h - 1)
        order += [("ST", h, j) for j in range(TILES)]
        order += [("rg", h, q) for q in range(TILES)]
        order += [("inner", h, q) for q in range(TILES)]
    tail(R_HEADS - 1)
    return order


def plan_blocks():
    even = [("w_in", c) for c in (4, 3, 0, 1, 2)] + [("w_out", c) for c in range(2)]
    odd = []
    for h in range(R_HEADS):
        odd += [("qk", h), ("v", h)]
        if h:
            odd.append(("wo", h - 1))
        odd.append(("g", h))
    odd.append(("wo", R_HEADS - 1))
    return even, odd


def trunk_kernel(nc, x, even_w_in, even_w_out, odd_w_in, odd_w_out, expert_w_gate, expert_w_up, expert_w_down,
                 gains, conv_w, conv_p, router_w, router_b, c_square, c_tab_a, c_tab_r, c_slot, c_small, out):
    banks = plan_banks()
    even_blocks, odd_blocks = plan_blocks()
    n_moe = 3 * EXPERTS
    block_no = {("even",) + b: n for n, b in enumerate(even_blocks)}
    moe_start = [len(even_blocks)]
    first_odd = moe_start[0] + n_moe
    block_no.update({("odd",) + b: first_odd + n for n, b in enumerate(odd_blocks)})
    moe_start.append(first_odd + len(odd_blocks))
    landed_at = {}
    fills = [0] * SLOTS
    for n in range(moe_start[1] + n_moe):
        two = first_odd <= n < moe_start[1] and odd_blocks[n - first_odd][0] == "qk"
        fills[n % SLOTS] += 32 if two else 16
        landed_at[n] = fills[n % SLOTS]
    dense = {}
    for n in list(range(moe_start[0])) + list(range(first_odd, moe_start[1])):
        dense[n] = len(dense)

    xs_dram = nc.dram_tensor("xs_dram", (SEQ, DM), F32, kind="Internal").ap()
    y_dram = nc.dram_tensor("y_dram", (TOPK * SEQ, DM), F32, kind="Internal").ap()

    with ExitStack() as ctx:
        def sem(name):
            return ctx.enter_context(nc.semaphore(name))

        psum = ctx.enter_context(nc.psum_tensor("psum", [P, 8, 512], F32))

        base = (nc.sbuf_base + 31) // 32 * 32
        ctx.enter_context(nc.sbuf_tensor("arena", [P, ARENA + 8], F32))
        top = [0]

        def place(name, shape, dt=F32, at=None):
            size = int(np.prod(shape[1:]))
            if at is None:
                at, top[0] = top[0], top[0] + (size + 7) // 8 * 8
            assert at + size <= ARENA, name
            return nc.alloc_sbuf_tensor_at(name, shape, dt, offset=base + 4 * at)[tuple([slice(None)] * len(shape))]

        raw = place("raw", [P, SLOTS, BLOCK])
        w_hi = [place(f"w_hi{b}", [P, HALF], F32R) for b in range(2)]
        w_lo = [place(f"w_lo{b}", [P, HALF], F32R) for b in range(2)]
        h = place("h", [P, TILES, DM])
        xs_at = top[0]
        xs = place("xs", [P, TILES * DM])
        uT_hi = place("uT_hi", [P, KC, SEQ], F32R)
        uT_lo = place("uT_lo", [P, KC, SEQ], F32R)
        square = place("square", [P, 5, P])
        slot_no = place("slot_no", [P, SEQ])
        small = place("small", [P, 32])
        gain_row = place("gain_row", [P, DM])
        convw = place("convw", [P, BC, TAPS])
        convp = place("convp", [P, 3, BC])
        wr = place("wr", [P, DEPTH, KC, NROUT])
        br = place("br", [P, DEPTH, NROUT])
        stat = place("stat", [P, 96])
        index = place("index", [P, SLOT_TILES, EXPERTS, 2], U32)
        load = place("load", [P, DEPTH], U32)
        gather_at = place("gather_at", [P, 2], U32)
        scatter_at = place("scatter_at", [P, 2], U32)
        shared = top[0]

        qT = place("qT", [P, 4, SEQ])
        kT = place("kT", [P, 4, SEQ])
        v0 = place("v0", [P, TILES, 512])
        conv_in = place("conv_in", [P, BC, SEQ + PAD])
        sm = place("sm", [P, 2, 512])
        prob = place("prob", [P, 2, 512])
        probT = place("probT", [P, 2, 512])
        tab_a = place("tab_a", [P, 3, SEQ])
        tap_in = place("tap_in", [P, 2, SEQ])
        sigT = qT
        mixT = xs[:, :].rearrange("p (c t) -> p c t", c=KC)
        rawT = mixT
        conv = mixT
        a_out = xs[:, 0:2048].rearrange("p (q n) -> p q n", q=TILES)
        cat_hi, cat_lo = uT_hi, uT_lo
        csq = conv_in[:, :, 0:SEQ]
        crt, crs = gain_row[:, 0:SEQ], gain_row[:, SEQ:]

        top[0] = shared
        qkT = place("qkT", [P, 4, SEQ])
        v1 = place("v1", [P, TILES, 512])
        sg = place("sg", [P, TILES, 512])
        smT = place("smT", [P, 10 * P])
        rot_tmp = place("rot_tmp", [P, 2, SEQ])
        gn = place("gn", [P, SEQ])
        yT_hi = place("yT_hi", [P, 4, SEQ], F32R)
        yT_lo = place("yT_lo", [P, 4, SEQ], F32R)
        tab_r = xs[:, 0:6 * SEQ].rearrange("p (c t) -> p c t", c=6)

        top[0] = shared
        uT = place("uT", [P, KC, SEQ])
        x_e = place("x_e", [P, 2, DM], at=shared)
        y_e = place("y_e", [P, 2, DM], at=shared + 2 * DM)
        oh = place("oh", [P, KC, SEQ], F32R, at=xs_at)
        silu_g = place("silu_g", [P, HID])
        hid = place("hid", [P, HID])
        rows = place("rows", [P, TOPK * TILES, EXPERTS], F32R)
        rt = place("rt", [P, 1216])
        w_hi += [place(f"w_hi{b}", [P, HALF], F32R) for b in (2, 3)]
        w_lo += [place(f"w_lo{b}", [P, HALF], F32R) for b in (2, 3)]
        xeT_hi, xeT_lo = [u[:, 4 * 0:4].rearrange("p a (b t) -> p (a b) t", t=P) for u in (uT_hi, uT_lo)]
        hidT_hi, hidT_lo = [u[:, 4].rearrange("p (c t) -> p c t", c=HC) for u in (uT_hi, uT_lo)]
        junk = place("junk", [P, DM], at=shared + 4096)
        y_back = [xs[:, :].rearrange("p (q n) -> p q n", q=TILES), uT[:, :, :].rearrange("p (q c) t -> p q (c t)", q=TILES)]

        used = [0]

        def take(n):
            used[0] += n
            assert used[0] <= 1216
            return rt[:, used[0] - n:used[0]]

        logit = take(TILES * NROUT).rearrange("p (q n) -> p q n", q=TILES)
        diff1 = take(16)
        exps1 = take(16)
        diff2 = take(TILES)
        exps2 = take(TILES)
        gp = take(TILES)
        best = take(TILES)
        best2 = take(TILES)
        pick = take(TILES)
        gate = take(TOPK * TILES).rearrange("p (k q) -> p k q", k=TOPK)
        of_group = take(16).rearrange("p (q g) -> p q g", q=TILES)
        cand = take(32)
        sel = take(32).rearrange("p (q n) -> p q n", q=TILES)
        sel2 = take(32).rearrange("p (q n) -> p q n", q=TILES)
        fine = [take(32).rearrange("p (q n) -> p q n", q=TILES) for _ in range(TOPK)]
        prod_all = take(SLOT_TILES * EXPERTS)
        prod = prod_all[:, 0:TILES * EXPERTS]
        chosen_k = [take(TILES * EXPERTS).rearrange("p (q n) -> p q n", q=TILES) for _ in range(TOPK)]
        both = take(TILES * EXPERTS).rearrange("p (q n) -> p q n", q=TILES)
        table = take(SLOT_TILES * EXPERTS)
        pos = table[:, 0:TILES * EXPERTS].rearrange("p (q n) -> p q n", q=TILES)
        rank = take(TOPK * TILES)
        most_f = take(1)
        ident, ones, before = square[:, 0], square[:, 1], square[:, 2]
        mean_w, swap = square[:, 3], square[:, 4]
        cos_a, sin_a, bias_a = tab_a[:, 0], tab_a[:, 1], tab_a[:, 2]

        bank_full = [sem(f"bank_full{b}") for b in range(8)]
        bank_free = [sem(f"bank_free{b}") for b in range(8)]
        landed = [sem(f"landed{s}") for s in range(SLOTS)]
        x_in = [sem(f"x_in{q}") for q in range(TILES)]
        const_in = sem("const_in")
        tab_r_in = sem("tab_r_in")
        h_ready = sem("h_ready")
        squares = sem("squares")
        mean_sq = sem("mean_sq")
        root = sem("root")
        rstd_ok = sem("rstd_ok")
        gain_in = sem("gain_in")
        norm_hi = sem("norm_hi")
        aT_hi = sem("aT_hi")
        b_silu = sem("b_silu")
        b_hi = sem("b_hi")
        yT_hi_ok = sem("yT_hi_ok")
        hi_ok = [sem(f"hi_ok{b}") for b in range(2)]
        lo_ok = [sem(f"lo_ok{b}") for b in range(2)]
        first_half = sem("first_half")
        xs_ready = sem("xs_ready")
        rot_cos = sem("rot_cos")
        rot_done = sem("rot_done")
        tap = sem("tap")
        tap_pool = sem("tap_pool")
        tap_mul = sem("tap_mul")
        csq_ok = sem("csq_ok")
        crs_ok = sem("crs_ok")
        cnorm = sem("cnorm")
        b_ok = sem("b_ok")
        mx_ok = sem("mx_ok")
        p_ok = sem("p_ok")
        pv_done = sem("pv_done")
        den_r = sem("den_r")
        radd = sem("radd")
        gstat = sem("gstat")
        gaggr = sem("gaggr")
        groot = sem("groot")
        grec = sem("grec")
        y_ok = sem("y_ok")
        out_sent = sem("out_sent")

        class MoePass:

            def __init__(self, tag, over_pass=False):
                buffers = 1 if over_pass else 2
                self.indexed = [sem(f"{tag}_gather_at{b}") for b in range(buffers)]
                self.gathered = [sem(f"{tag}_gathered{b}") for b in range(buffers)]
                self.xT_psum = sem(f"{tag}_xT_psum")
                self.xT_ok = sem(f"{tag}_xT_ok")
                self.xT_hi = sem(f"{tag}_xT_hi")
                self.hidT_hi = sem(f"{tag}_hidT_hi")
                if over_pass:
                    self.hi, self.lo = sem(f"{tag}_hi"), sem(f"{tag}_lo")
                else:
                    self.hi = [sem(f"{tag}_hi{b}") for b in range(4)]
                    self.lo = [sem(f"{tag}_lo{b}") for b in range(4)]
                if not over_pass:
                    self.gate_half = sem(f"{tag}_gate_half")
                    self.up_half = sem(f"{tag}_up_half")
                    self.down_half = sem(f"{tag}_down_half")
                self.gate_psum = sem(f"{tag}_gate_psum")
                self.up_psum = sem(f"{tag}_up_psum")
                self.silu_ok = sem(f"{tag}_silu_ok")
                self.hid_ok = sem(f"{tag}_hid_ok")
                self.hidT_psum = sem(f"{tag}_hidT_psum")
                self.hidT_ok = sem(f"{tag}_hidT_ok")
                self.down_psum = sem(f"{tag}_down_psum")
                self.y_act = sem(f"{tag}_y_act")
                self.y_dve = sem(f"{tag}_y_dve")
                self.sc_indexed = sem(f"{tag}_sc_indexed")
                self.scattered = [sem(f"{tag}_scattered{b}") for b in range(buffers)]
                self.y_free = sem(f"{tag}_y_free")
                if over_pass:
                    self.lists = sem(f"{tag}_lists")
                    self.table = sem(f"{tag}_table")
                    self.go = sem(f"{tag}_go")

        main = MoePass("m")
        over = [MoePass(f"o{l}", True) for l in range(DEPTH)]
        over_landed = [sem(f"over_landed{l}") for l in range(DEPTH)]
        xs_stored = sem("xs_stored")
        step = sem("step")
        exp_done = sem("exp_done")
        index_ok = sem("index_ok")
        lists_read = sem("lists_read")
        reduced = sem("reduced")
        second = sem("second")
        chosen = sem("chosen")
        placed = sem("placed")
        eps_ok = sem("eps_ok")
        y_in = [sem(f"y_in{q}") for q in range(TILES)]
        moe_done = sem("moe_done")

        w_in = even_w_in[0].rearrange("(p j) n -> p j n", j=KC)
        w_out = even_w_out[0].rearrange("(j p) n -> p j n", p=P)
        o_in = odd_w_in[0].rearrange("(p j) n -> p j n", j=KC)
        o_out = odd_w_out[0].rearrange("(h j p) n -> p h j n", h=R_HEADS, p=P)
        wg_dram = expert_w_gate.rearrange("l e (p j) n -> l e p (j n)", j=KC)
        wu_dram = expert_w_up.rearrange("l e (p j) n -> l e p (j n)", j=KC)
        wd_dram = expert_w_down.rearrange("l e (p j) n -> l e p (j n)", j=HC)
        x_dram = x[0].rearrange("(q p) d -> p q d", p=P)
        out_dram = out[0].rearrange("(q p) d -> p q d", p=P)
        xs_rows = xs_dram.rearrange("(q p) d -> p q d", p=P)
        y_rows = y_dram.rearrange("(k q p) d -> p k q d", k=TOPK, p=P)

        def half_of(n, half, by_columns):
            if by_columns:
                return raw[:, n % SLOTS].rearrange("p (j c n) -> p c j n", j=HC, c=2)[:, half]
            return raw[:, n % SLOTS].rearrange("p (c j n) -> p c j n", c=2, j=4)[:, half]

        def part(w):
            return w[:, :].rearrange("p (j n) -> p j n", j=4)

        def down_no(e):
            return gate_no(e + 1) + 2 if e < EXPERTS - 1 else n_moe - 1

        def gate_no(e):
            return 2 + 3 * (e - 1) if e else 0

        def up_no(e):
            return gate_no(e) + 1

        FILLS = n_moe // 2
        TURNS = (EXPERTS - 4) // 2

        def one(src, layer, e):
            return src[layer, e] if type(e) is int else src[layer, bass.ds(e, 1)].rearrange("a p n -> p (a n)")

        def expert_steps(eng, body):
            body(0, 0, 0)
            body(1, 1, 0)
            with eng.Fori(0, TURNS) as i:
                body(2 * i + 2, 2, i)
                body(2 * i + 3, 3, i)
            body(EXPERTS - 2, 2, TURNS)
            body(EXPERTS - 1, 3, TURNS)

        def copied(eng, *name):
            b, u, _ = banks.at(*name)
            eng.wait_ge(bank_free[b], u + 1)

        def last_product(n):
            if n < moe_start[0]:
                kind, c = even_blocks[n]
                name = ("out0", c, 3) if kind == "w_out" else \
                    {4: ("gate", 3), 3: ("val", 3), 0: ("proj", "q", 3), 1: ("proj", "k", 3), 2: ("v", 3)}[c]
            else:
                kind, hd = odd_blocks[n - first_odd]
                name = {"qk": ("qk", hd, 3), "wo": ("out1", hd, 1, 3), "v": ("rv", hd, 3), "g": ("rg", hd, 3)}[kind]
            bank, _, full = banks.at(*name)
            return bank_full[bank], full

        half_count, count = {}, 0
        for n in dense:
            if not (n >= first_odd and odd_blocks[n - first_odd][0] == "wo"):
                count += 1
                half_count[n] = count

        def half_used(n, half):
            if half:
                return last_product(n)
            if n in half_count:
                return first_half, half_count[n]
            bank, _, full = banks.at("out1", odd_blocks[n - first_odd][1], 0, 3)
            return bank_full[bank], full

        def moe_half_used(layer, k, half):
            m = main
            if k < 2:
                e, kind = 0, k
            elif k == n_moe - 1:
                e, kind = EXPERTS - 1, 2
            else:
                kind = (k - 2) % 3
                e = (k - 2) // 3 + (kind < 2)
            return ((m.gate_half, m.gate_psum), (m.up_half, m.up_psum), (m.down_half, m.down_psum))[kind][half], \
                EXPERTS * layer + e + 1

        def split_hi(act, n, halves=(0, 1)):
            by_columns = n >= first_odd and odd_blocks[n - first_odd][0] == "wo"
            act.wait_ge(landed[n % SLOTS], landed_at[n])
            for half in halves:
                if n - 1 in dense:
                    act.wait_ge(*half_used(n - 1, half))
                elif n:
                    act.wait_ge(main.down_psum, EXPERTS)
                nc.scalar.activation(part(w_hi[half]), half_of(n, half, by_columns), ACT.Copy).then_inc(hi_ok[half], 1)

        def split_lo(dve, n, half):
            by_columns = n >= first_odd and odd_blocks[n - first_odd][0] == "wo"
            dve.wait_ge(hi_ok[half], dense[n] + 1)
            nc.vector.tensor_tensor(part(w_lo[half]), half_of(n, half, by_columns), part(w_hi[half]).bitcast(F32),
                                    ALU.subtract).then_inc(lo_ok[half], 1)

        def moe_split(eng, layer, kind, s, turn, lo):
            m = main
            k = {"gate": gate_no, "up": up_no, "down": down_no}[kind](s)
            n = moe_start[layer] + k
            for half in range(2):
                b = 2 * (k % 2) + half
                src = half_of(n, half, kind == "down")
                if lo:
                    eng.wait_ge(m.hi[b], layer * FILLS + k // 2 + 1 + 3 * turn)
                    nc.vector.tensor_tensor(part(w_lo[b]), src, part(w_hi[b]).bitcast(F32), ALU.subtract).then_inc(m.lo[b], 1)
                    continue
                eng.wait_ge(landed[n % SLOTS], landed_at[n] + 32 * turn)
                if k >= 2:
                    done, value = moe_half_used(layer, k - 2, half)
                    eng.wait_ge(done, value + 2 * turn)
                elif k == 0:
                    eng.wait_ge(*half_used(n - 1, half))
                nc.scalar.activation(part(w_hi[b]), src, ACT.Copy).then_inc(m.hi[b], 1)

        block = ctx.enter_context(nc.Block())

        @block.sync
        def _(sp):
            def split(n):
                if n in dense:
                    return lo_ok[1], dense[n] + 1
                layer = int(n >= moe_start[1])
                k = n - moe_start[layer]
                return main.lo[2 * (k % 2) + 1], layer * FILLS + k // 2 + 1

            def fill(n, parts):
                if n >= SLOTS:
                    sp.wait_ge(*split(n - SLOTS))
                for dst, src in parts:
                    sp.dma_start(dst, src).then_inc(landed[n % SLOTS], 16)

            def blocked(n):
                return raw[:, n % SLOTS].rearrange("p (j n) -> p j n", j=KC)

            for q in range(TILES):
                sp.dma_start(h[:, q], x_dram[:, q]).then_inc(x_in[q], 16)
            sp.wait_ge(const_in, 16)
            sp.wait_ge(gain_in, 16)
            for b in even_blocks:
                n = block_no[("even",) + b]
                if n == 1:
                    sp.wait_ge(const_in, 16 * N_CONST)
                src, c = (w_in, b[1]) if b[0] == "w_in" else (w_out, b[1])
                fill(n, [(blocked(n), src[:, :, c * 512:(c + 1) * 512])])

            def experts(layer):
                first = moe_start[layer]

                def load_step(e, s, turn):
                    for kind, src, x in (("gate", wg_dram, e), ("up", wu_dram, e), ("down", wd_dram, e - 1)):
                        if s == 0 and kind == "down":
                            continue
                        n = first + (down_no(s - 1) if kind == "down" else gate_no(s) + (kind == "up"))
                        done, value = split(n - SLOTS)
                        if n - SLOTS in dense:
                            sp.wait_ge(done, value)
                        else:
                            sp.wait_ge(done, value + 3 * turn)
                        sp.dma_start(raw[:, n % SLOTS], one(src, layer, x)).then_inc(landed[n % SLOTS], 16)

                expert_steps(sp, load_step)
                fill(first + n_moe - 1, [(raw[:, (first + n_moe - 1) % SLOTS], wd_dram[layer, EXPERTS - 1])])

                sp.wait_ge(index_ok, layer + 1)
                most = sp.value_load(load[0:1, layer:layer + 1], min_val=0, max_val=SEQ)
                with sp.If(most > FIRST):
                    m = over[layer]
                    for c in range(1, SLOT_TILES):
                        with sp.Fori(0, EXPERTS) as e:
                            sp.wait_ge(m.go, e + (EXPERTS * (c - 1) + 1))
                            for k, src in enumerate((wg_dram, wu_dram, wd_dram)):
                                sp.dma_start(raw[:, k], one(src, layer, e)).then_inc(over_landed[layer], 16)
                    sp.wait_ge(moe_done, layer + 1)

            experts(0)
            for b in odd_blocks:
                n = block_no[("odd",) + b]
                kind, hd = b
                if n == first_odd + 1:
                    for q in range(TILES):
                        sp.wait_ge(y_in[q], 32)
                if kind == "qk":
                    fill(n, [(blocked(n)[:, :, 0:R_QK], o_in[:, :, hd * R_QK:(hd + 1) * R_QK]),
                             (blocked(n)[:, :, R_QK:], o_in[:, :, R_QKW + hd * R_QK:R_QKW + (hd + 1) * R_QK])])
                elif kind == "wo":
                    fill(n, [(raw[:, n % SLOTS].rearrange("p (j n) -> p j n", j=HC), o_out[:, hd])])
                else:
                    c = 2 * R_QKW + (R_VW if kind == "g" else 0) + hd * R_V
                    fill(n, [(blocked(n), o_in[:, :, c:c + R_V])])
            experts(1)
            for q in range(TILES):
                sp.wait_ge(xs_ready, 4 * TILES + q + 1)
                sp.dma_start(out_dram[:, q], xs[:, q * DM:(q + 1) * DM]).then_inc(out_sent, 16)
            sp.wait_ge(out_sent, 16 * TILES)

        @block.tensor
        def _(pe):
            def open_bank(*name):
                b, u, _ = banks.at(*name)
                if u:
                    pe.wait_ge(bank_free[b], u)
                return psum[:, b], bank_full[b]

            def product(dst, still, moving, start, stop):
                nc.tensor.matmul(dst, still[0], moving[0], start=start, stop=False)
                nc.tensor.matmul(dst, still[1], moving[0], start=False, stop=False)
                return nc.tensor.matmul(dst, still[0], moving[1], start=False, stop=stop)

            def norm(n):
                for q in range(TILES):
                    pe.wait_ge(xs_ready, TILES * n + q + 1)
                    for j in range(KC):
                        b, _, _ = banks.at("norm", n, j)
                        if q == 0:
                            open_bank("norm", n, j)
                        mm = nc.tensor.transpose(psum[:, b, q * P:(q + 1) * P], xs[:, q * DM + j:(q + 1) * DM:KC], ident)
                        if q == TILES - 1:
                            mm.then_inc(bank_full[b], 1)

            def parts(half):
                return part(w_hi[half]), part(w_lo[half])

            def dense_half(n, half, names, x_hi, x_lo, channels_out, norm=None):
                pe.wait_ge(lo_ok[half], dense[n] + 1)
                hi, lo = parts(half)
                for i, name in enumerate(names):
                    if half == 0:
                        dst, full = open_bank(*name)
                    else:
                        b, _, _ = banks.at(*name)
                        dst, full = psum[:, b], bank_full[b]
                    c = slice(i * P, (i + 1) * P)
                    for j in range(4):
                        if i == 0 and norm is not None:
                            copied(pe, "norm", norm, 4 * half + j)
                        w = (hi[:, j], lo[:, j])
                        x = (x_hi[:, 4 * half + j], x_lo[:, 4 * half + j])
                        if channels_out:
                            mm = product(dst, [a[:, c] for a in w], x, half + j == 0, half * j == 3)
                        else:
                            mm = product(dst, [a[:, c] for a in x], w, half + j == 0, half * j == 3)
                    if half:
                        mm.then_inc(full, 1)
                if not half:
                    mm.then_inc(first_half, 1)

            def transpose_tokens(m, b, r=FIRST):
                for j in range(KC):
                    mm = nc.tensor.transpose(psum[:, j // 4, (j % 4) * P:(j % 4) * P + r], x_e[0:r, b, j:DM:KC],
                                             ident[0:r, 0:r])
                mm.then_inc(m.xT_psum, 1)

            def up_product(pairs, bank, b, half_done, done, ready, r=FIRST):
                for half, pair in enumerate(pairs):
                    hi, lo = part(w_hi[pair]), part(w_lo[pair])
                    ready(pair, False)
                    for j in range(4):
                        c = 8 * b + 4 * half + j
                        nc.tensor.matmul(psum[0:r, bank], xeT_hi[:, c, 0:r], hi[:, j], start=(half + j == 0), stop=False)
                        nc.tensor.matmul(psum[0:r, bank], xeT_lo[:, c, 0:r], hi[:, j], start=False, stop=False)
                    ready(pair, True)
                    for j in range(4):
                        c = 8 * b + 4 * half + j
                        mm = nc.tensor.matmul(psum[0:r, bank], xeT_hi[:, c, 0:r], lo[:, j], start=False,
                                              stop=(half * j == 3))
                    if half:
                        mm.then_inc(done, 1)
                    elif half_done:
                        mm.then_inc(half_done, 1)

            def transpose_hidden(m, r=FIRST):
                for j in range(HC):
                    mm = nc.tensor.transpose(psum[:, 4, j * P:j * P + r], hid[0:r, j:HID:HC], ident[0:r, 0:r])
                mm.then_inc(m.hidT_psum, 1)

            def down_product(m, pairs, half_done, ready, r=FIRST):
                for half, pair in enumerate(pairs):
                    hi, lo = part(w_hi[pair]), part(w_lo[pair])
                    ready(pair, False)
                    for j in range(HC):
                        nc.tensor.matmul(psum[0:r, 5 + half], hidT_hi[:, j, 0:r], hi[:, j], start=(j == 0), stop=False)
                        nc.tensor.matmul(psum[0:r, 5 + half], hidT_lo[:, j, 0:r], hi[:, j], start=False, stop=False)
                    ready(pair, True)
                    for j in range(HC):
                        mm = nc.tensor.matmul(psum[0:r, 5 + half], hidT_hi[:, j, 0:r], lo[:, j], start=False,
                                              stop=(j == HC - 1))
                    if half:
                        mm.then_inc(m.down_psum, 1)
                    elif half_done:
                        mm.then_inc(half_done, 1)

            def moe(layer):
                m, past = main, EXPERTS * layer
                norm(2 * layer + 1)
                dst, full = open_bank("logitsT", layer)
                for j in range(KC):
                    copied(pe, "norm", 2 * layer + 1, j)
                    mm = nc.tensor.matmul(dst[0:NROUT], wr[:, layer, j], uT[:, j], start=(j == 0), stop=(j == KC - 1))
                mm.then_inc(full, 1)
                dst, full = open_bank("logits", layer)
                copied(pe, "logitsT", layer)
                for q in range(TILES):
                    mm = nc.tensor.transpose(dst[:, q * NROUT:(q + 1) * NROUT], silu_g[0:NROUT, q * P:(q + 1) * P],
                                             ident[0:NROUT, 0:NROUT])
                mm.then_inc(full, 1)
                dst, full = open_bank("pos", layer)
                pe.wait_ge(chosen, layer + 1)
                for q in range(TILES):
                    for t in range(q + 1):
                        nc.tensor.matmul(dst[:, q * EXPERTS:(q + 1) * EXPERTS], before if t == q else ones, both[:, t],
                                         start=(t == 0), stop=(t == q))
                for t in range(TILES):
                    mm = nc.tensor.matmul(dst[:, TILES * EXPERTS:(TILES + 1) * EXPERTS], ones, both[:, t],
                                          start=(t == 0), stop=(t == TILES - 1))
                mm.then_inc(full, 1)
                dst, full = open_bank("table", layer)
                pe.wait_ge(placed, layer + 1)
                for k in range(TOPK * TILES):
                    mm = nc.tensor.matmul(dst[:, 0:EXPERTS], oh[:, k, 0:P], rows[:, k], start=(k == 0),
                                          stop=(k == TOPK * TILES - 1))
                mm.then_inc(full, 1)

                for b in range(8):
                    pe.wait_ge(bank_free[b], banks.before_experts[layer][b])
                pe.wait_ge(m.gathered[0], 16 * (past // 2 + 1))
                transpose_tokens(m, 0)

                def split_of(k, turn):
                    def ready(pair, lo):
                        pe.wait_ge((m.lo if lo else m.hi)[pair], layer * FILLS + k // 2 + 1 + 3 * turn)
                    return (2 * (k % 2), 2 * (k % 2) + 1), ready

                def body(e, s, turn):
                    pe.wait_ge(m.xT_ok, e + (past + 1))
                    if past or s:
                        pe.wait_ge(m.silu_ok, e + past)
                    pairs, ready = split_of(gate_no(s), turn)
                    up_product(pairs, 2, s % 2, m.gate_half, m.gate_psum, ready)
                    if past or s:
                        pe.wait_ge(m.hid_ok, e + past)
                    if s:
                        transpose_hidden(m)
                    pairs, ready = split_of(up_no(s), turn)
                    up_product(pairs, 3, s % 2, m.up_half, m.up_psum, ready)
                    if type(e) is not int or e < EXPERTS - 1:
                        pe.wait_ge(m.gathered[(s + 1) % 2], 16 * (turn + (past // 2 + (s + 1) // 2 + 1)))
                        transpose_tokens(m, (s + 1) % 2)
                    if s:
                        down(e - 1, down_no(s - 1), turn)

                def down(e, k, turn):
                    pe.wait_ge(m.hidT_ok, e + (past + 1))
                    pe.wait_ge(m.y_act, e + (past + 1))
                    pe.wait_ge(m.y_dve, e + (past + 1))
                    pairs, ready = split_of(k, turn)
                    down_product(m, pairs, m.down_half, ready)

                expert_steps(pe, body)
                pe.wait_ge(m.hid_ok, past + EXPERTS)
                transpose_hidden(m)
                down(EXPERTS - 1, n_moe - 1, 0)

                pe.wait_ge(index_ok, layer + 1)
                most = pe.value_load(load[0:1, layer:layer + 1], min_val=0, max_val=SEQ)
                with pe.If(most > FIRST):
                    m = over[layer]
                    pe.wait_ge(m.lists, 1)
                    for c in range(1, SLOT_TILES):
                        for k in range(TOPK * TILES):
                            mm = nc.tensor.matmul(psum[:, 7, c * EXPERTS:(c + 1) * EXPERTS],
                                                  oh[:, k, SLOT_AT[c]:SLOT_AT[c] + P], rows[:, k],
                                                  start=(k == 0), stop=(k == TOPK * TILES - 1))
                    mm.then_inc(m.table, 1)
                    for c in range(1, SLOT_TILES):
                        with pe.Fori(0, EXPERTS) as e:
                            n = e + (EXPERTS * (c - 1) + 1)

                            def ready_at(first):
                                def ready(pair, lo):
                                    pe.wait_ge(m.lo if lo else m.hi, 6 * n - 5 + first + pair % 2)
                                return ready

                            pe.wait_ge(m.gathered[0], 16 * n)
                            transpose_tokens(m, 0, P)
                            pe.wait_ge(m.xT_ok, n)
                            up_product((0, 1), 2, 0, None, m.gate_psum, ready_at(0), P)
                            up_product((2, 3), 3, 0, None, m.up_psum, ready_at(2), P)
                            pe.wait_ge(m.hid_ok, n)
                            transpose_hidden(m, P)
                            pe.wait_ge(m.hidT_ok, n)
                            down_product(m, (0, 1), None, ready_at(4), P)

            def a_transpose(q):
                dst, full = open_bank("aT", q)
                copied(pe, "O", q)
                for c in range(4):
                    mm = nc.tensor.transpose(dst[:, c * P:(c + 1) * P], a_out[:, q, c * P:(c + 1) * P], ident)
                mm.then_inc(full, 1)

            pe.wait_ge(const_in, 16)
            norm(0)
            pe.wait_ge(const_in, 16 * N_CONST)

            def even(c, half, norm=None):
                n = block_no[("even", "w_in", c)]
                names = {4: [("gate", i) for i in range(4)], 3: [("val", i) for i in range(4)],
                         0: [("proj", "q", i) for i in range(4)], 1: [("proj", "k", i) for i in range(4)],
                         2: [("v", i) for i in range(4)]}[c]
                dense_half(n, half, names, uT_hi, uT_lo, c != 2, norm)

            def rotate(which):
                for c in range(4):
                    dst, full = open_bank("rot", which, c)
                    copied(pe, "proj", which, c)
                    nc.tensor.matmul(dst, swap, rawT[:, c], start=True, stop=True).then_inc(full, 1)

            even(4, 0, 0)
            even(4, 1, 0)
            for c, half in ((3, 0), (3, 1), (0, 0), (0, 1), (1, 0)):
                even(c, half)
            even(1, 1)
            rotate("q")
            even(2, 0)
            rotate("k")
            even(2, 1)

            units = attention_units()
            pe.wait_ge(rot_done, 8)
            for n in range(len(units) + 2):
                if n < len(units):
                    q, hd = units[n]
                    dst, full = open_bank("S", (q, hd))
                    r = slice((hd % 2) * A_DIM, (hd % 2 + 1) * A_DIM)
                    w = (q + 1) * P
                    nc.tensor.matmul(dst[:, 0:w], qT[r, hd // 2, q * P:(q + 1) * P], kT[r, hd // 2, 0:w],
                                     start=True, stop=True).then_inc(full, 1)
                if n == CONV_AT:
                    dst, full = open_bank("cmean")
                    pe.wait_ge(tap, 3 * TAPS)
                    pe.wait_ge(tap_pool, TAPS)
                    for c in range(BC):
                        mm = nc.tensor.matmul(dst, mean_w, conv[:, 4 + c], start=(c == 0), stop=(c == BC - 1))
                    mm.then_inc(full, 1)
                if n == CONV_AT + 3:
                    dst, full = open_bank("cvar")
                    pe.wait_ge(csq_ok, BC)
                    for c in range(BC):
                        mm = nc.tensor.matmul(dst, mean_w, csq[:, c], start=(c == 0), stop=(c == BC - 1))
                    mm.then_inc(full, 1)
                if 1 <= n <= len(units):
                    q, hd = units[n - 1]
                    dst, full = open_bank("PT", (q, hd))
                    pe.wait_ge(p_ok, n)
                    for j in range(q + 1):
                        mm = nc.tensor.transpose(dst[:, j * P:(j + 1) * P], prob[:, (n - 1) % 2, j * P:(j + 1) * P], ident)
                    mm.then_inc(full, 1)
                if n >= 2:
                    q, hd = units[n - 2]
                    if hd == 0:
                        o_dst, _ = open_bank("O", q)
                        copied(pe, "v", TILES - 1)
                    copied(pe, "PT", (q, hd))
                    for j in range(q + 1):
                        mm = nc.tensor.matmul(o_dst[:, hd * A_DIM:(hd + 1) * A_DIM], probT[:, n % 2, j * P:(j + 1) * P],
                                              v0[:, j, hd * A_DIM:(hd + 1) * A_DIM], start=(j == 0), stop=(j == q))
                    mm.then_inc(pv_done, 1)
                    if hd == 2 and q > 0:
                        a_transpose(q - 1)
            a_transpose(TILES - 1)
            copied(pe, "aT", TILES - 1)
            pe.wait_ge(b_ok, BC)
            for half in range(2):
                n = block_no[("even", "w_out", half)]
                for k in range(2):
                    dense_half(n, k, [("out0", half, q) for q in range(TILES)], cat_hi, cat_lo, False)
            moe(0)

            norm(2)

            def odd(kind, hd, job):
                n = block_no[("odd", kind, hd)]
                for half in range(2):
                    dense_half(n, half, [(job, hd, i) for i in range(4)], uT_hi, uT_lo, kind == "qk",
                               2 if (kind, hd) == ("qk", 0) else None)

            def tail(hd):
                for q in range(TILES):
                    dst, full = open_bank("yT", hd, q)
                    pe.wait_ge(y_ok, hd * TILES + q + 1)
                    for c in range(4):
                        mm = nc.tensor.transpose(dst[:, c * P:(c + 1) * P], sg[:, q, c * P:(c + 1) * P], ident)
                    mm.then_inc(full, 1)
                n = block_no[("odd", "wo", hd)]
                for half in range(2):
                    pe.wait_ge(lo_ok[half], dense[n] + 1)
                    hi, lo = parts(half)
                    for q in range(TILES):
                        dst, full = open_bank("out1", hd, half, q)
                        copied(pe, "yT", hd, q)
                        for j in range(4):
                            c = slice(q * P, (q + 1) * P)
                            mm = product(dst, (yT_hi[:, j, c], yT_lo[:, j, c]), (hi[:, j], lo[:, j]), j == 0, j == 3)
                        mm.then_inc(full, 1)

            for hd in range(R_HEADS):
                odd("qk", hd, "qk")
                odd("v", hd, "rv")
                if hd:
                    tail(hd - 1)
                pe.wait_ge(radd, 4 * (hd + 1))
                for j in range(TILES):
                    dst, full = open_bank("ST", hd, j)
                    w = (TILES - j) * P
                    for c in range(2):
                        mm = nc.tensor.matmul(dst[:, 0:w], qkT[:, 2 + c, j * P:(j + 1) * P], qkT[:, c, j * P:SEQ],
                                              start=(c == 0), stop=(c == 1))
                    mm.then_inc(full, 1)
                odd("g", hd, "rg")
                copied(pe, "rv", hd, TILES - 1)
                copied(pe, "ST", hd, TILES - 1)
                for q in range(TILES):
                    dst, full = open_bank("inner", hd, q)
                    for j in range(q + 1):
                        mm = nc.tensor.matmul(dst, smT[:, ST_AT[j] + (q - j) * P:ST_AT[j] + (q - j + 1) * P], v1[:, j],
                                              start=(j == 0), stop=(j == q))
                    mm.then_inc(full, 1)
            tail(R_HEADS - 1)
            moe(1)

        @block.scalar
        def _(act):
            def bank(*name):
                b, _, full = banks.at(*name)
                act.wait_ge(bank_full[b], full)
                return psum[:, b], bank_free[b]

            def norm(n):
                for q in range(TILES):
                    if n == 0:
                        act.wait_ge(x_in[q], 16)
                    elif n == 1:
                        copied(act, "out0", 1, q)
                    elif n == 3:
                        copied(act, "out1", R_HEADS - 1, 1, q)
                    else:
                        act.wait_ge(h_ready, TILES * (n // 2 - 1) + q + 1)
                    if n or q:
                        act.wait_ge(squares, TILES * n + q)
                    nc.scalar.activation(junk, h[:, q], ACT.Square, accum_out=stat[:, q:q + 1]).then_inc(squares, 1)
                    act.wait_ge(mean_sq, TILES * n + q + 1)
                    nc.scalar.activation(stat[:, 8 + q:9 + q], stat[:, 4 + q:5 + q], ACT.Sqrt).then_inc(root, 1)

            def load_gain(n):
                act.dma_start(gain_row[:], gains[n]).then_inc(gain_in, 16)

            def norm_copies(n, half=None):
                if n and half != 1:
                    act.wait_ge(xs_ready, TILES * (n + 1))
                    load_gain(n + 1)
                if n % 2 == 0:
                    for j in range(4 * half, 4 * half + 4):
                        src, _ = bank("norm", n, j)
                        nc.scalar.activation(uT_hi[:, j], src, ACT.Copy).then_inc(norm_hi, 1)
                else:
                    for j in range(1, KC, 2):
                        src, free = bank("norm", n, j)
                        nc.scalar.activation(uT[:, j], src, ACT.Copy).then_inc(free, 1)

            act.dma_start(square[:], c_square).then_inc(const_in, 16)
            load_gain(0)
            act.wait_ge(const_in, 16)
            for dst, src in ((tab_a[:], c_tab_a), (small[:], c_small), (slot_no[:], c_slot), (convw[:], conv_w),
                             (convp[:], conv_p), (wr[:], router_w), (br[:], router_b)):
                act.dma_start(dst, src).then_inc(const_in, 16)

            norm(0)
            for half in range(2):
                split_hi(act, 0, (half,))
                norm_copies(0, half)
            split_hi(act, 1)
            for c in range(BC):
                src, free = bank("gate", c)
                nc.scalar.activation(sigT[:, c], src, ACT.Sigmoid).then_inc(free, 1)
            split_hi(act, 2)
            split_hi(act, 3)
            for c in range(4):
                src, free = bank("proj", "q", c)
                nc.scalar.activation(rawT[:, c], src, ACT.Copy).then_inc(free, 1)
            split_hi(act, 4)
            for c in range(4):
                src, free = bank("proj", "k", c)
                act.wait_ge(rot_cos, c + 1)
                bank("rot", "q", c)
                nc.scalar.activation(rawT[:, c], src, ACT.Copy).then_inc(free, 1)
            split_hi(act, 5)
            for q in range(TILES):
                src, free = bank("v", q)
                nc.scalar.activation(v0[:, q], src, ACT.Copy).then_inc(free, 1)

            def turned(q):
                src, _ = bank("aT", q)
                nc.scalar.activation(cat_hi[:, 0:4, q * P:(q + 1) * P], src.rearrange("p (c t) -> p c t", c=4),
                                     ACT.Copy).then_inc(aT_hi, 1)

            units = attention_units()
            for n in range(len(units) + 2):
                if n < len(units):
                    q, hd = units[n]
                    w = (q + 1) * P
                    act.wait_ge(mx_ok, n + 1)
                    if n >= 2:
                        b, _, full = banks.at("PT", units[n - 2])
                        act.wait_ge(bank_full[b], full)
                    if hd == 0 and q:
                        act.wait_ge(den_r, q)
                    nc.scalar.activation(prob[:, n % 2, 0:w], sm[:, n % 2, 0:w], ACT.Exp, bias=stat[:, 16 + n % 2:17 + n % 2],
                                         accum_out=stat[:, 24 + hd:25 + hd]).then_inc(p_ok, 1)
                if n >= 1 and n <= len(units):
                    q, hd = units[n - 1]
                    w = (q + 1) * P
                    src, free = bank("PT", (q, hd))
                    if n >= 3:
                        act.wait_ge(pv_done, n - 2)
                    nc.scalar.activation(probT[:, (n - 1) % 2, 0:w], src[:, 0:w], ACT.Copy).then_inc(free, 1)
                if n == CONV_AT + 2:
                    copied(act, "cmean")
                    for c in range(BC):
                        nc.scalar.activation(csq[:, c], conv[:, 4 + c], ACT.Square).then_inc(csq_ok, 1)
                if n == CONV_AT + 4:
                    src, free = bank("cvar")
                    act.wait_ge(eps_ok, 1)
                    nc.scalar.activation(crt, src, ACT.Sqrt, bias=stat[:, 40:41]).then_inc(free, 1)
                if n == CONV_AT + 6:
                    for c in range(BC):
                        act.wait_ge(cnorm, c + 1)
                        nc.scalar.activation(conv[:, 4 + c], conv[:, 4 + c], ACT.Silu, bias=convp[:, 2, c:c + 1],
                                             scale=convp[:, 1, c:c + 1]).then_inc(b_silu, 1)
                        act.wait_ge(b_silu, c + 1)
                        nc.scalar.activation(cat_hi[:, 4 + c], conv[:, 4 + c], ACT.Copy).then_inc(b_hi, 1)
                    load_gain(1)
                if n >= 4 and units[n - 2][1] == 2 and units[n - 2][0]:
                    turned(units[n - 2][0] - 1)
            turned(TILES - 1)
            split_hi(act, 6)

            def store_rows(layer):
                act.wait_ge(xs_ready, TILES * (2 * layer + 2))
                act.dma_start(xs_rows, xs[:, :].rearrange("p (q d) -> p q d", q=TILES)).then_inc(xs_stored, 16)

            def copy_tokens(m, n, b, r=FIRST):
                act.wait_ge(m.xT_psum, n)
                for half in range(2):
                    ins = nc.scalar.activation(xeT_hi[:, 8 * b + 4 * half:8 * b + 4 * half + 4, 0:r],
                                               psum[:, half].rearrange("p (c t) -> p c t", c=4)[:, :, 0:r], ACT.Copy)
                ins.then_inc(m.xT_hi, 1)

            def silu(m, n, r=FIRST):
                act.wait_ge(m.gate_psum, n)
                nc.scalar.activation(silu_g[0:r], psum[0:r, 2], ACT.Silu).then_inc(m.silu_ok, 1)

            def copy_hidden(m, n, r=FIRST):
                act.wait_ge(m.hidT_psum, n)
                nc.scalar.activation(hidT_hi[:, :, 0:r], psum[:, 4].rearrange("p (c t) -> p c t", c=HC)[:, :, 0:r], ACT.Copy) \
                    .then_inc(m.hidT_hi, 1)

            def copy_y(m, n, b, r=FIRST):
                act.wait_ge(m.down_psum, n)
                act.wait_ge(m.y_free, n)
                nc.scalar.activation(y_e[0:r, b, 0:512], psum[0:r, 5], ACT.Copy).then_inc(m.y_act, 1)

            def moe(layer):
                m, past = main, EXPERTS * layer
                moe_split(act, layer, "gate", 0, 0, False)
                src, free = bank("logitsT", layer)
                nc.scalar.activation(silu_g[0:NROUT], src[0:NROUT], ACT.Copy).then_inc(free, 1)
                moe_split(act, layer, "up", 0, 0, False)
                act.wait_ge(reduced, layer + 1)
                nc.scalar.activation(exps1, diff1, ACT.Exp).then_inc(exp_done, 1)
                act.wait_ge(second, layer + 1)
                nc.scalar.activation(exps2, diff2, ACT.Exp).then_inc(exp_done, 1)
                if not layer:
                    act.sem_inc(m.y_act, 1)
                copy_tokens(m, past + 1, 0)

                def body(e, s, turn):
                    last = type(e) is int and e == EXPERTS - 1
                    if s:
                        moe_split(act, layer, "up", s, turn, False)
                    if s:
                        copy_hidden(m, e + past)
                        act.wait_ge(m.hid_ok, e + past)
                    silu(m, e + (past + 1))
                    if s:
                        moe_split(act, layer, "down", s - 1, turn, False)
                    if last:
                        moe_split(act, layer, "down", EXPERTS - 1, 0, False)
                    else:
                        copy_tokens(m, e + (past + 2), (s + 1) % 2)
                        moe_split(act, layer, "gate", s + 1, turn, False)
                    if s:
                        copy_y(m, e + past, (s - 1) % 2)

                expert_steps(act, body)
                copy_hidden(m, past + EXPERTS)
                copy_y(m, past + EXPERTS, (EXPERTS - 1) % 2)
                act.wait_ge(index_ok, layer + 1)
                most = act.value_load(load[0:1, layer:layer + 1], min_val=0, max_val=SEQ)
                with act.If(most > FIRST):
                    m = over[layer]
                    for c in range(1, SLOT_TILES):
                        with act.Fori(0, EXPERTS) as e:
                            n = e + (EXPERTS * (c - 1) + 1)
                            copy_tokens(m, n, 0, P)
                            act.wait_ge(over_landed[layer], 48 * n)
                            for b in range(4):
                                nc.scalar.activation(part(w_hi[b]), half_of(b // 2, b % 2, False), ACT.Copy).then_inc(m.hi, 1)
                            silu(m, n, P)
                            for b in range(2):
                                act.wait_ge(m.lo, 6 * n - 5 + b)
                                nc.scalar.activation(part(w_hi[b]), half_of(2, b, True), ACT.Copy).then_inc(m.hi, 1)
                            copy_hidden(m, n, P)
                            copy_y(m, n, 0, P)
                act.wait_ge(moe_done, layer + 1)
                for q in range(TILES):
                    for k in range(TOPK):
                        act.dma_start(y_back[k][:, q], y_rows[:, k, q]).then_inc(y_in[q], 16)

            norm(1)
            store_rows(0)
            norm_copies(1)
            moe(0)

            norm(2)
            split_hi(act, block_no[("odd", "qk", 0)])
            bank("norm", 2, KC - 1)
            act.dma_start(tab_r, c_tab_r).then_inc(tab_r_in, 16)
            norm_copies(2, 0)
            norm_copies(2, 1)

            def turned_y(hd):
                for q in range(TILES):
                    src, _ = bank("yT", hd, q)
                    nc.scalar.activation(yT_hi[:, :, q * P:(q + 1) * P], src.rearrange("p (c t) -> p c t", c=4),
                                         ACT.Copy).then_inc(yT_hi_ok, 1)

            for hd in range(R_HEADS):
                split_hi(act, block_no[("odd", "v", hd)])
                if hd:
                    split_hi(act, block_no[("odd", "wo", hd - 1)])
                for q in range(TILES):
                    src, free = bank("rv", hd, q)
                    nc.scalar.activation(v1[:, q], src, ACT.Copy).then_inc(free, 1)
                if hd:
                    turned_y(hd - 1)
                split_hi(act, block_no[("odd", "g", hd)])
                split_hi(act, block_no[("odd", "qk", hd + 1) if hd < R_HEADS - 1 else ("odd", "wo", hd)])
                for q in range(TILES):
                    src, free = bank("rg", hd, q)
                    nc.scalar.activation(sg[:, q], src, ACT.Silu).then_inc(free, 1)
                act.wait_ge(gaggr, TILES * (hd + 1))
                nc.scalar.activation(stat[:, 44:48], stat[:, 49:56:2], ACT.Sqrt, bias=stat[:, 40:41]).then_inc(groot, 1)
            turned_y(R_HEADS - 1)
            norm(3)
            store_rows(1)
            norm_copies(3)
            moe(1)
            norm(4)

        @block.vector
        def _(dve):
            V = nc.vector
            steps = [0]

            def link(ins):
                steps[0] += 1
                ins.then_inc(step, 1)
                dve.wait_ge(step, steps[0])

            def bank(*name):
                b, _, full = banks.at(*name)
                dve.wait_ge(bank_full[b], full)
                return psum[:, b], bank_free[b]

            def norm(n, q):
                dve.wait_ge(squares, TILES * n + q + 1)
                V.tensor_scalar(stat[:, 4 + q:5 + q], stat[:, q:q + 1], 1.0 / DM, EPS, ALU.mult, ALU.add).then_inc(mean_sq, 1)
                dve.wait_ge(root, TILES * n + q + 1)
                V.reciprocal(stat[:, 12 + q:13 + q], stat[:, 8 + q:9 + q]).then_inc(rstd_ok, 1)
                dve.wait_ge(rstd_ok, TILES * n + q + 1)
                dve.wait_ge(gain_in, 16 * (n + 1))
                V.scalar_tensor_tensor(out=xs[:, q * DM:(q + 1) * DM], in0=h[:, q], scalar=stat[:, 12 + q:13 + q],
                                       in1=gain_row[:], op0=ALU.mult, op1=ALU.mult).then_inc(xs_ready, 1)

            def norm_copies(n, half=None):
                if n % 2 == 0:
                    for j in range(4 * half, 4 * half + 4):
                        src, free = bank("norm", n, j)
                        dve.wait_ge(norm_hi, KC * (n // 2) + j + 1)
                        V.tensor_tensor(uT_lo[:, j], src, uT_hi[:, j].bitcast(F32), ALU.subtract).then_inc(free, 1)
                else:
                    for j in range(0, KC, 2):
                        src, free = bank("norm", n, j)
                        V.tensor_copy(uT[:, j], src).then_inc(free, 1)

            V.memset(stat[:, 40:41], EPS).then_inc(eps_ok, 1)
            for q in range(TILES):
                norm(0, q)
            for half in range(2):
                split_lo(dve, 0, half)
                norm_copies(0, half)
            V.memset(conv_in[:, :, 0:PAD], 0.0).then_inc(eps_ok, 1)
            dve.wait_ge(eps_ok, 2)
            split_lo(dve, 1, 0)
            split_lo(dve, 1, 1)
            split_lo(dve, 2, 0)
            split_lo(dve, 2, 1)
            dve.wait_ge(const_in, 16 * N_CONST)
            for c in range(BC):
                copied(dve, "gate", c)
                src, free = bank("val", c)
                V.tensor_tensor(conv_in[:, c, PAD:], src, sigT[:, c], ALU.mult).then_inc(free, 1)
            copied(dve, "val", BC - 1)

            def taps(first, last):
                for i in range(first, last):
                    k, c = i // 3, i % 3
                    if k:
                        dve.wait_ge(tap, i - 2)
                        V.scalar_tensor_tensor(out=conv[:, 4 + c], in0=conv_in[:, c, k:k + SEQ], scalar=convw[:, c, k:k + 1],
                                               in1=conv[:, 4 + c], op0=ALU.mult, op1=ALU.add).then_inc(tap, 1)
                    else:
                        V.tensor_scalar(conv[:, 4 + c], conv_in[:, c, k:k + SEQ], convw[:, c, k:k + 1], convp[:, 0, c:c + 1],
                                        ALU.mult, ALU.add).then_inc(tap, 1)

            def rotate(which):
                for c in range(4):
                    n = ROPE_CHUNKS.index((which, c))
                    src, free = bank("rot", which, c)
                    if n >= 2:
                        dve.wait_ge(rot_done, n - 1)
                    V.tensor_tensor(sm[:, n % 2], src, sin_a, ALU.mult).then_inc(free, 1)
                    copied(dve, "rot", which, c)
                    dve.wait_ge(rot_cos, n + 1)
                    t = (qT if which == "q" else kT)[:, c]
                    V.tensor_tensor(t, t, sm[:, n % 2], ALU.add).then_inc(rot_done, 1)

            taps(0, 12)
            split_lo(dve, 3, 0)
            taps(12, 24)
            split_lo(dve, 3, 1)
            taps(24, 42)
            split_lo(dve, 4, 0)
            taps(42, 51)
            split_lo(dve, 4, 1)
            rotate("q")
            split_lo(dve, 5, 0)
            rotate("k")
            split_lo(dve, 5, 1)
            dve.wait_ge(rot_done, 8)

            units = attention_units()
            def turned(q):
                src, free = bank("aT", q)
                dve.wait_ge(aT_hi, q + 1)
                t = slice(q * P, (q + 1) * P)
                V.tensor_tensor(cat_lo[:, 0:4, t], src.rearrange("p (c t) -> p c t", c=4), cat_hi[:, 0:4, t].bitcast(F32),
                                ALU.subtract).then_inc(free, 1)

            for n in range(len(units) + 3):
                if n < len(units):
                    q, hd = units[n]
                    w = (q + 1) * P
                    src, free = bank("S", (q, hd))
                    if n >= 2:
                        dve.wait_ge(p_ok, n - 1)
                    V.scalar_tensor_tensor(out=sm[:, n % 2, 0:w], in0=src[:, 0:w], scalar=A_DIM ** -0.5,
                                           in1=bias_a[:, SEQ - w:SEQ], op0=ALU.mult, op1=ALU.add).then_inc(free, 1)
                    copied(dve, "S", (q, hd))
                    V.tensor_reduce(stat[:, 16 + n % 2:17 + n % 2], sm[:, n % 2, 0:w], AX.X, ALU.max, negate=True) \
                        .then_inc(mx_ok, 1)
                if n < CONV_AT - 1:
                    taps(min(51 + 3 * n, 3 * TAPS), min(51 + 3 * n + 3, 3 * TAPS))
                if n % A_HEADS == 0 and n:
                    dve.wait_ge(p_ok, n)
                    if n > A_HEADS:
                        copied(dve, "O", n // A_HEADS - 2)
                    V.reciprocal(stat[:, 32:40], stat[:, 24:32]).then_inc(den_r, 1)
                    dve.wait_ge(den_r, n // A_HEADS)
                if n >= 3 and (n - 3) % A_HEADS == A_HEADS - 1:
                    q = (n - 3) // A_HEADS
                    b, _, _ = banks.at("O", q)
                    dve.wait_ge(pv_done, n - 2)
                    V.tensor_tensor(a_out[:, q].rearrange("p (h d) -> p h d", h=A_HEADS),
                                    psum[:, b].rearrange("p (h d) -> p h d", h=A_HEADS),
                                    stat[:, 32:40].unsqueeze(2).broadcast_to([P, A_HEADS, A_DIM]), ALU.mult) \
                        .then_inc(bank_free[b], 1)
                if n == CONV_AT + 1:
                    src, free = bank("cmean")
                    for c in range(BC):
                        ins = V.tensor_tensor(conv[:, 4 + c], conv[:, 4 + c], src, ALU.subtract)
                    ins.then_inc(free, 1)
                if n == CONV_AT + 5:
                    copied(dve, "cvar")
                    V.reciprocal(crs, crt).then_inc(crs_ok, 1)
                    dve.wait_ge(crs_ok, 1)
                    for c in range(BC):
                        V.tensor_tensor(conv[:, 4 + c], conv[:, 4 + c], crs, ALU.mult).then_inc(cnorm, 1)
                if n == CONV_AT + 8:
                    for c in range(BC):
                        dve.wait_ge(b_hi, c + 1)
                        V.tensor_tensor(cat_lo[:, 4 + c], conv[:, 4 + c], cat_hi[:, 4 + c].bitcast(F32), ALU.subtract) \
                            .then_inc(b_ok, 1)
                if n >= 5 and n - 3 < len(units) and units[n - 3][1] == 2 and units[n - 3][0]:
                    turned(units[n - 3][0] - 1)
            turned(TILES - 1)
            split_lo(dve, 6, 0)
            split_lo(dve, 6, 1)
            for half in range(2):
                for q in range(TILES):
                    src, free = bank("out0", half, q)
                    dst = h[:, q, half * 512:(half + 1) * 512]
                    V.tensor_tensor(dst, dst, src, ALU.add).then_inc(free, 1)
                    if half and q:
                        norm(1, q - 1)
            norm(1, TILES - 1)

            def first_best(values, width, top, rank, out):
                c = cand[:, 0:TILES * width].rearrange("p (q n) -> p q n", q=TILES)
                wide = [P, TILES, width]
                link(V.tensor_reduce(top, values, AX.X, ALU.max))
                link(V.tensor_tensor(c, values, top.unsqueeze(2).broadcast_to(wide), ALU.is_equal))
                link(V.tensor_tensor(c, c, rank.unsqueeze(1).broadcast_to(wide), ALU.mult))
                link(V.tensor_reduce(pick, c, AX.X, ALU.max))
                link(V.tensor_tensor(out, c, pick.unsqueeze(2).broadcast_to(wide), ALU.is_equal))

            def route(layer):
                src, free = bank("logits", layer)
                V.tensor_tensor(logit, src[:, 0:TILES * NROUT].rearrange("p (q n) -> p q n", q=TILES),
                                br[:, layer].unsqueeze(1).broadcast_to([P, TILES, NROUT]), ALU.add).then_inc(free, 1)
                copied(dve, "logits", layer)
                group = logit[:, :, 0:GROUPS]
                first_best(group, GROUPS, best, small[:, 0:4], of_group)
                V.tensor_tensor(diff1.rearrange("p (q g) -> p q g", q=TILES), group,
                                best.unsqueeze(2).broadcast_to([P, TILES, GROUPS]), ALU.subtract).then_inc(reduced, 1)
                for q in range(TILES):
                    link(V.tensor_tensor(prod[:, 0:EXPERTS].rearrange("p (g e) -> p g e", g=GROUPS),
                                         logit[:, q, GROUPS:].rearrange("p (g e) -> p g e", g=GROUPS),
                                         of_group[:, q].unsqueeze(2).broadcast_to([P, GROUPS, PER_GROUP]), ALU.mult))
                    link(V.tensor_reduce(sel[:, q], prod[:, 0:EXPERTS].rearrange("p (g e) -> p e g", g=GROUPS), AX.X, ALU.add))
                first_best(sel, PER_GROUP, best, small[:, 4:12], fine[0])
                link(V.scalar_tensor_tensor(out=sel2, in0=fine[0], scalar=NEG, in1=sel, op0=ALU.mult, op1=ALU.add))
                first_best(sel2, PER_GROUP, best2, small[:, 4:12], fine[1])
                V.tensor_tensor(diff2, best2, best, ALU.subtract).then_inc(second, 1)
                for k in range(TOPK):
                    for q in range(TILES):
                        ins = V.tensor_tensor(chosen_k[k][:, q].rearrange("p (g e) -> p g e", g=GROUPS),
                                              of_group[:, q].unsqueeze(2).broadcast_to([P, GROUPS, PER_GROUP]),
                                              fine[k][:, q].unsqueeze(1).broadcast_to([P, GROUPS, PER_GROUP]), ALU.mult)
                link(ins)
                V.tensor_tensor(both, chosen_k[0], chosen_k[1], ALU.add).then_inc(chosen, 1)
                moe_split(dve, layer, "up", 0, 0, True)
                for k in range(TOPK):
                    ins = V.tensor_tensor(rows[:, k * TILES:(k + 1) * TILES], chosen_k[k],
                                          small[:, 12 + k * TILES:12 + (k + 1) * TILES].unsqueeze(2)
                                          .broadcast_to([P, TILES, EXPERTS]), ALU.mult)
                src, free = bank("pos", layer)
                V.tensor_reduce(most_f, src[:, TILES * EXPERTS:(TILES + 1) * EXPERTS], AX.X, ALU.max)
                V.tensor_copy(pos, src[:, 0:TILES * EXPERTS].rearrange("p (q n) -> p q n", q=TILES)).then_inc(free, 1)
                copied(dve, "pos", layer)
                V.tensor_copy(load[:, layer:layer + 1], most_f)
                for k in range(TOPK):
                    link(V.tensor_tensor(prod.rearrange("p (q n) -> p q n", q=TILES), pos, chosen_k[k], ALU.mult))
                    link(V.tensor_reduce(rank[:, k * TILES:(k + 1) * TILES], prod.rearrange("p (q n) -> p q n", q=TILES),
                                         AX.X, ALU.add))
                dve.wait_ge(xs_stored, 16 * (layer + 1))
                for k in range(TOPK * TILES):
                    ins = V.tensor_scalar(oh[:, k, 0:P], slot_no[:, 0:P], rank[:, k:k + 1], None, ALU.is_equal)
                ins.then_inc(placed, 1)
                dve.wait_ge(exp_done, 2 * layer + 2)
                link(V.tensor_reduce(gp, exps1.rearrange("p (q g) -> p q g", q=TILES), AX.X, ALU.add))
                link(V.tensor_scalar(pick, exps2, 1.0, None, ALU.add))
                link(V.tensor_tensor(pick, pick, gp, ALU.mult))
                link(V.reciprocal(gate[:, 0], pick))
                link(V.tensor_tensor(gate[:, 1], gate[:, 0], exps2, ALU.mult))
                src, free = bank("table", layer)
                V.tensor_copy(table[:, 0:EXPERTS], src[:, 0:EXPERTS]).then_inc(free, 1)
                copied(dve, "table", layer)
                make_lists(0, 1, link, index_ok)

            def make_lists(first, last, link, done):
                t, p = (a[:, first * EXPERTS:last * EXPERTS] for a in (table, prod_all))
                link(V.tensor_scalar(p, t, 0.0, EMPTY, ALU.is_equal, ALU.mult))
                link(V.scalar_tensor_tensor(out=t, in0=t, scalar=-1.0, in1=p, op0=ALU.add, op1=ALU.add))
                link(V.tensor_scalar(p, t, float(SEQ), -float(SEQ), ALU.is_ge, ALU.mult))
                both_at = index[:, first:last].rearrange("p c e k -> p (c e) k")
                link(V.tensor_copy(both_at[:, :, 1], t))
                V.tensor_tensor(both_at[:, :, 0], t, p, ALU.add).then_inc(done, 1)

            def copy_tokens(m, n, b, r=FIRST):
                dve.wait_ge(m.xT_hi, n)
                for half in range(2):
                    c = slice(8 * b + 4 * half, 8 * b + 4 * half + 4)
                    ins = V.tensor_tensor(xeT_lo[:, c, 0:r], psum[:, half].rearrange("p (c t) -> p c t", c=4)[:, :, 0:r],
                                          xeT_hi[:, c, 0:r].bitcast(F32), ALU.subtract)
                ins.then_inc(m.xT_ok, 1)

            def copy_hidden(m, n, r=FIRST):
                dve.wait_ge(m.hidT_hi, n)
                V.tensor_tensor(hidT_lo[:, :, 0:r], psum[:, 4].rearrange("p (c t) -> p c t", c=HC)[:, :, 0:r],
                                hidT_hi[:, :, 0:r].bitcast(F32), ALU.subtract).then_inc(m.hidT_ok, 1)

            def hidden(m, n, r=FIRST):
                dve.wait_ge(m.up_psum, n)
                dve.wait_ge(m.silu_ok, n)
                V.tensor_tensor(hid[0:r], silu_g[0:r], psum[0:r, 3], ALU.mult).then_inc(m.hid_ok, 1)

            def copy_y(m, n, b, r=FIRST):
                dve.wait_ge(m.down_psum, n)
                dve.wait_ge(m.y_free, n)
                V.tensor_copy(y_e[0:r, b, 512:1024], psum[0:r, 6]).then_inc(m.y_dve, 1)

            def moe(layer):
                m, past = main, EXPERTS * layer
                norm_copies(2 * layer + 1)
                moe_split(dve, layer, "gate", 0, 0, True)
                route(layer)
                if not layer:
                    dve.sem_inc(m.y_dve, 1)
                copy_tokens(m, past + 1, 0)

                def body(e, s, turn):
                    last = type(e) is int and e == EXPERTS - 1
                    if s:
                        moe_split(dve, layer, "up", s, turn, True)
                    if s:
                        copy_hidden(m, e + past)
                        moe_split(dve, layer, "down", s - 1, turn, True)
                    hidden(m, e + (past + 1))
                    if last:
                        moe_split(dve, layer, "down", EXPERTS - 1, 0, True)
                    else:
                        copy_tokens(m, e + (past + 2), (s + 1) % 2)
                        moe_split(dve, layer, "gate", s + 1, turn, True)
                    if s:
                        copy_y(m, e + past, (s - 1) % 2)

                expert_steps(dve, body)
                copy_hidden(m, past + EXPERTS)
                copy_y(m, past + EXPERTS, (EXPERTS - 1) % 2)
                most = dve.value_load(load[0:1, layer:layer + 1], min_val=0, max_val=SEQ)
                with dve.If(most > FIRST):
                    m = over[layer]
                    for k in range(TOPK * TILES):
                        ins = V.tensor_scalar(oh[:, k, P:], slot_no[:, P:], rank[:, k:k + 1], None, ALU.is_equal)
                    ins.then_inc(m.lists, 1)
                    dve.wait_ge(m.table, 1)
                    steps_here = [1]

                    def link_here(ins):
                        steps_here[0] += 1
                        ins.then_inc(m.table, 1)
                        dve.wait_ge(m.table, steps_here[0])

                    further = slice(EXPERTS, SLOT_TILES * EXPERTS)
                    link_here(V.tensor_copy(table[:, further], psum[:, 7, further]))
                    make_lists(1, SLOT_TILES, link_here, m.lists)
                    for c in range(1, SLOT_TILES):
                        with dve.Fori(0, EXPERTS) as e:
                            n = e + (EXPERTS * (c - 1) + 1)
                            copy_tokens(m, n, 0, P)
                            for b in range(4):
                                dve.wait_ge(m.hi, 6 * n - 5 + b)
                                V.tensor_tensor(part(w_lo[b]), half_of(b // 2, b % 2, False), part(w_hi[b]).bitcast(F32),
                                                ALU.subtract).then_inc(m.lo, 1)
                            hidden(m, n, P)
                            for b in range(2):
                                dve.wait_ge(m.hi, 6 * n - 1 + b)
                                V.tensor_tensor(part(w_lo[b]), half_of(2, b, True), part(w_hi[b]).bitcast(F32),
                                                ALU.subtract).then_inc(m.lo, 1)
                            copy_hidden(m, n, P)
                            copy_y(m, n, 0, P)
                for q in range(TILES):
                    dve.wait_ge(y_in[q], 32 * (layer + 1))
                    link(V.scalar_tensor_tensor(out=h[:, q], in0=y_back[0][:, q], scalar=gate[:, 0, q:q + 1],
                                                in1=h[:, q], op0=ALU.mult, op1=ALU.add))
                    V.scalar_tensor_tensor(out=h[:, q], in0=y_back[1][:, q], scalar=gate[:, 1, q:q + 1],
                                           in1=h[:, q], op0=ALU.mult, op1=ALU.add).then_inc(h_ready, 1)
                    if q:
                        norm(2 * layer + 2, q - 1)
                norm(2 * layer + 2, TILES - 1)

            moe(0)

            for half in range(2):
                split_lo(dve, block_no[("odd", "qk", 0)], half)
                norm_copies(2, half)
            dve.wait_ge(tab_r_in, 16)
            cos_r, sin_r = tab_r[:, 0], tab_r[:, 1]

            def lo(kind, hd, half):
                split_lo(dve, block_no[("odd", kind, hd)], half)

            def turned_y(hd):
                for q in range(TILES):
                    src, free = bank("yT", hd, q)
                    dve.wait_ge(yT_hi_ok, hd * TILES + q + 1)
                    t = slice(q * P, (q + 1) * P)
                    V.tensor_tensor(yT_lo[:, :, t], src.rearrange("p (c t) -> p c t", c=4), yT_hi[:, :, t].bitcast(F32),
                                    ALU.subtract).then_inc(free, 1)

            def residual(hd, half):
                for q in range(TILES):
                    src, free = bank("out1", hd, half, q)
                    dst = h[:, q, half * 512:(half + 1) * 512]
                    V.tensor_tensor(dst, dst, src, ALU.add).then_inc(free, 1)
                    if hd == R_HEADS - 1 and half and q:
                        norm(3, q - 1)

            for hd in range(R_HEADS):
                lo("v", hd, 0)
                lo("v", hd, 1)
                for a in (0, 2):
                    x1, free1 = bank("qk", hd, a)
                    x2, free2 = bank("qk", hd, a + 1)
                    if hd and not a:
                        dve.wait_ge(y_ok, TILES * hd)
                    if hd or a:
                        dve.wait_ge(radd, 4 * hd + a)
                    V.tensor_tensor(rot_tmp[:, 0], x1, cos_r, ALU.mult)
                    V.tensor_tensor(rot_tmp[:, 1], x2, sin_r, ALU.mult)
                    V.tensor_tensor(qkT[:, a + 1], x2, cos_r, ALU.mult).then_inc(free2, 1)
                    V.tensor_tensor(gn, x1, sin_r, ALU.mult).then_inc(free1, 1)
                    copied(dve, "qk", hd, a)
                    copied(dve, "qk", hd, a + 1)
                    V.tensor_tensor(qkT[:, a], rot_tmp[:, 0], rot_tmp[:, 1], ALU.subtract).then_inc(radd, 1)
                    V.tensor_tensor(qkT[:, a + 1], qkT[:, a + 1], gn, ALU.add).then_inc(radd, 1)
                if hd:
                    lo("wo", hd - 1, 0)
                    lo("wo", hd - 1, 1)
                    turned_y(hd - 1)
                    lo("g", hd, 0)
                    residual(hd - 1, 0)
                    lo("g", hd, 1)
                    residual(hd - 1, 1)
                else:
                    lo("g", hd, 0)
                    lo("g", hd, 1)
                for j in range(TILES):
                    src, free = bank("ST", hd, j)
                    w = (TILES - j) * P
                    V.tensor_tensor(smT[:, ST_AT[j]:ST_AT[j] + w], src[:, 0:w], tab_r[:, 2 + hd, 0:w], ALU.mult).then_inc(free, 1)
                ahead = ("qk", hd + 1) if hd < R_HEADS - 1 else ("wo", hd)
                lo(*ahead, 0)
                lo(*ahead, 1)
                dve.wait_ge(radd, 4 * (hd + 1))
                if hd:
                    dve.wait_ge(y_ok, TILES * hd)
                for q in range(TILES):
                    src, _ = bank("inner", hd, q)
                    V.bn_stats(stat[:, 64 + 6 * q:70 + 6 * q], src).then_inc(gstat, 1)
                    dve.wait_ge(gstat, hd * TILES + q + 1)
                    V.bn_aggr(stat[:, 48 + 2 * q:50 + 2 * q], stat[:, 64 + 6 * q:70 + 6 * q]).then_inc(gaggr, 1)
                dve.wait_ge(groot, hd + 1)
                V.reciprocal(stat[:, 56:60], stat[:, 44:48]).then_inc(grec, 1)
                dve.wait_ge(grec, hd + 1)
                for q in range(TILES):
                    src, free = bank("inner", hd, q)
                    if q >= 2:
                        dve.wait_ge(y_ok, hd * TILES + q - 1)
                    V.tensor_scalar(rot_tmp[:, q % 2], src, stat[:, 48 + 2 * q:49 + 2 * q], stat[:, 56 + q:57 + q],
                                    ALU.subtract, ALU.mult).then_inc(free, 1)
                    copied(dve, "inner", hd, q)
                    copied(dve, "rg", hd, q)
                    V.tensor_tensor(sg[:, q], sg[:, q], rot_tmp[:, q % 2], ALU.mult).then_inc(y_ok, 1)
            turned_y(R_HEADS - 1)
            residual(R_HEADS - 1, 0)
            residual(R_HEADS - 1, 1)
            norm(3, TILES - 1)
            moe(1)

        @block.gpsimd
        def _(pool):
            G = nc.gpsimd
            pool.wait_ge(const_in, 16 * N_CONST)

            def taps(first, last):
                c = BC - 1
                for k in range(first, last):
                    if not k:
                        G.tensor_scalar(conv[:, 4 + c], conv_in[:, c, 0:SEQ], convw[:, c, 0:1], convp[:, 0, c:c + 1],
                                        ALU.mult, ALU.add).then_inc(tap_pool, 1)
                        continue
                    if k >= 3:
                        pool.wait_ge(tap_pool, k - 1)
                    G.tensor_scalar(tap_in[:, k % 2], conv_in[:, c, k:k + SEQ], convw[:, c, k:k + 1], None, ALU.mult) \
                        .then_inc(tap_mul, 1)
                    pool.wait_ge(tap_mul, k)
                    pool.wait_ge(tap_pool, k)
                    G.tensor_tensor(conv[:, 4 + c], conv[:, 4 + c], tap_in[:, k % 2], ALU.add).then_inc(tap_pool, 1)

            def cosines(which):
                for c in range(4):
                    copied(pool, "proj", which, c)
                    if which == "q":
                        copied(pool, "val", c)
                    G.tensor_tensor((qT if which == "q" else kT)[:, c], rawT[:, c], cos_a, ALU.mult).then_inc(rot_cos, 1)

            copied(pool, "val", BC - 1)
            taps(0, 9)
            cosines("q")
            cosines("k")
            taps(9, TAPS)

            def gather(m, c, e, b, n):
                r = P if c else FIRST
                src = index[0:r, c, e, 0:1] if type(e) is int else index[0:r, c, bass.ds(e, 1), 0]
                G.tensor_copy(gather_at[0:r, b:b + 1], src).then_inc(m.indexed[b], 1)
                pool.wait_ge(m.indexed[b], n)
                pool.sem_inc(lists_read, 1)
                G.indirect_dma_start(x_e[0:r, b], None, xs_dram, bass.IndirectOffsetOnAxis(ap=gather_at[0:r, b:b + 1], axis=0),
                                     bounds_check=SEQ - 1, oob_is_err=False).then_inc(m.gathered[b], 16)

            def scatter(m, c, e, b, n, count):
                r = P if c else FIRST
                src = index[0:r, c, e, 1:2] if type(e) is int else index[0:r, c, bass.ds(e, 1), 1]
                G.tensor_copy(scatter_at[0:r, 0:1], src).then_inc(m.sc_indexed, 1)
                pool.wait_ge(m.sc_indexed, n)
                pool.sem_inc(lists_read, 1)
                G.indirect_dma_start(y_dram, bass.IndirectOffsetOnAxis(ap=scatter_at[0:r, 0:1], axis=0), y_e[0:r, b], None,
                                     bounds_check=TOPK * SEQ - 1, oob_is_err=False).then_inc(m.scattered[b], 16)
                pool.wait_ge(m.scattered[b], 16 * count)
                pool.sem_inc(m.y_free, 1)

            def number(v):
                return v if type(v) is int else pool.snap(v)

            for layer in range(DEPTH):
                m, past = main, EXPERTS * layer
                if not layer:
                    pool.sem_inc(m.y_free, 2)
                pool.wait_ge(index_ok, layer + 1)
                pool.wait_ge(xs_stored, 16 * (layer + 1))
                gather(m, 0, 0, 0, past // 2 + 1)
                gather(m, 0, 1, 1, past // 2 + 1)

                def body(e, s, turn):
                    if type(e) is not int or e < EXPERTS - 2:
                        ahead, count = number(e + 2), number(turn + (past // 2 + s // 2 + 2))
                        pool.wait_ge(m.xT_psum, e + (past + 1))
                        gather(m, 0, ahead, s % 2, count)
                    if s:
                        store(e - 1, s - 1, turn)

                def store(e, s, turn):
                    e, count = number(e), number(turn + (past // 2 + s // 2 + 1))
                    pool.wait_ge(m.y_act, e + (past + 2))
                    pool.wait_ge(m.y_dve, e + (past + 2))
                    scatter(m, 0, e, s % 2, e + (past + 1), count)

                expert_steps(pool, body)
                store(EXPERTS - 1, 3, TURNS)

                most = pool.value_load(load[0:1, layer:layer + 1], min_val=0, max_val=SEQ)
                with pool.If(most > FIRST):
                    m = over[layer]
                    pool.wait_ge(m.lists, 2)
                    pool.sem_inc(m.y_free, 1)
                    for c in range(1, SLOT_TILES):
                        with pool.Fori(0, EXPERTS) as e:
                            n = e + (EXPERTS * (c - 1) + 1)
                            pool.sem_inc(m.go, 1)
                            gather(m, c, e, 0, n)
                            pool.wait_ge(m.y_act, n)
                            pool.wait_ge(m.y_dve, n)
                            scatter(m, c, e, 0, n, n)
                pool.sem_inc(moe_done, 1)


def kernel(**inputs):
    import concourse.bacc as bacc
    from concourse.bass_utils import run_bass_kernel_spmd

    a = {k: np.asarray(v) for k, v in inputs.items()}
    arrays = {k: np.ascontiguousarray(a[k]) for k in
              ("x", "even_w_in", "even_w_out", "odd_w_in", "odd_w_out", "expert_w_gate", "expert_w_up", "expert_w_down")}
    rows = [a["mix_norm"][0], a["ffn_norm"][0], a["mix_norm"][1], a["ffn_norm"][1], a["final_norm"]]
    arrays["gains"] = np.ascontiguousarray(np.broadcast_to(np.stack(rows)[:, None], (5, P, DM)))
    arrays["conv_w"] = np.ascontiguousarray(a["conv_w"][0].reshape(TAPS, BC, P).transpose(2, 1, 0))
    arrays["conv_p"] = np.ascontiguousarray(
        np.stack([a[k][0].reshape(BC, P) for k in ("conv_b", "conv_norm_g", "conv_norm_b")]).transpose(2, 0, 1))
    router = np.concatenate([a["router_w1"], a["router_w2"]], 2)
    arrays["router_w"] = np.ascontiguousarray(router.reshape(DEPTH, P, KC, NROUT).transpose(1, 0, 2, 3))
    arrays["router_b"] = np.ascontiguousarray(
        np.broadcast_to(np.concatenate([a["router_b1"], a["router_b2"]], 1), (P, DEPTH, NROUT)))
    arrays.update(shape_constants())
    arrays = {f"in_{k}": v for k, v in arrays.items()}

    nc = bacc.Bacc("TRN2", target_bir_lowering=False, num_devices=1, dynamic_dma_scratch_size=4096)
    aps = {k[3:]: nc.dram_tensor(k, v.shape, mybir.dt.from_np(v.dtype), kind="ExternalInput").ap() for k, v in arrays.items()}
    out = nc.dram_tensor("out", (1, SEQ, DM), F32, kind="ExternalOutput").ap()
    trunk_kernel(nc, out=out, **aps)
    r = run_bass_kernel_spmd(nc, [arrays], core_ids=[0])
    return r.results[0]["out"]
```
